# Optimizing a Trainium2 kernel written in Bass

```python
import math
import jax, jax.numpy as jnp
from jax import lax
import numpy as np

D_MODEL = 1024
BATCH = 1
SEQ = 2048
DEPTH = 1
DEC_BATCH = 8
DEC_SEQ = 16
PAST_LEN = 512

CHUNK = 64
QBLOCK = 128
N_HEADS = 8
QK_NOPE = 64
QK_ROPE = 32
V_DIM = 64
Q_LORA = 256
KV_LORA = 256
ROPE_THETA = 10000.0
MLA_WIDTH = N_HEADS * V_DIM
ATTN_SCALE = 1.0 / math.sqrt(QK_NOPE + QK_ROPE)
POOL_WINDOWS = (2, 4, 8, 16)
N_POOL_GROUPS = 4
POOL_WIDTH = D_MODEL - MLA_WIDTH
POOL_GROUP_W = POOL_WIDTH // N_POOL_GROUPS
POOL_HIST = max(POOL_WINDOWS) - 1
IN_WIDTH = Q_LORA + KV_LORA + QK_ROPE + POOL_WIDTH
D_FF = 2816
CONV_W = 3
PLE_DIM = 256
ALPHA = (2 * DEPTH) ** 0.25
BETA = (8 * DEPTH) ** -0.25
LN_EPS = 1e-5
RMS_EPS = 1e-6
NEG = -1e30

kernel_name = "mla_pool_convffn_deepnorm_stream_step"

def rms_norm(x, g):
    xf = x.astype(jnp.float32)
    y = xf * lax.rsqrt(jnp.mean(xf * xf, axis=-1, keepdims=True) + RMS_EPS)
    return (y * g.astype(jnp.float32)).astype(x.dtype)

def layer_norm(x, g, b):
    xf = x.astype(jnp.float32)
    mu = jnp.mean(xf, axis=-1, keepdims=True)
    var = jnp.mean(jnp.square(xf - mu), axis=-1, keepdims=True)
    y = (xf - mu) * lax.rsqrt(var + LN_EPS)
    return (y * g.astype(jnp.float32) + b.astype(jnp.float32)).astype(x.dtype)

def rope_tables(pos):
    inv = 1.0 / (ROPE_THETA ** (jnp.arange(0, QK_ROPE, 2, dtype=jnp.float32) / QK_ROPE))
    ang = pos.astype(jnp.float32)[:, None] * inv[None, :]
    return jnp.cos(ang), jnp.sin(ang)

def apply_rope(x, cos, sin):
    half = x.shape[-1] // 2
    x1, x2 = x[..., :half], x[..., half:]
    c, s = cos.astype(x.dtype), sin.astype(x.dtype)
    return jnp.concatenate([x1 * c - x2 * s, x2 * c + x1 * s], axis=-1)

def prompt_attention(q, k, v, pos):
    B, S, H, Dk = q.shape
    nb = S // QBLOCK
    qb = q.reshape(B, nb, QBLOCK, H, Dk).transpose(1, 0, 2, 3, 4)
    k_chunk = pos // CHUNK
    q_chunk = (pos // CHUNK).reshape(nb, QBLOCK)

    def one_block(args):
        qi, qc = args
        s = jnp.einsum('bqhd,bkhd->bhqk', qi, k).astype(jnp.float32) * ATTN_SCALE
        mask = k_chunk[None, :] <= qc[:, None]
        s = jnp.where(mask[None, None], s, NEG)
        p = jax.nn.softmax(s, axis=-1).astype(v.dtype)
        return jnp.einsum('bhqk,bkhd->bqhd', p, v)

    o = lax.map(one_block, (qb, q_chunk))
    return o.transpose(1, 0, 2, 3, 4).reshape(B, S, H, V_DIM)

def sample_attention(q_nope, q_rope, c_all, kr_all, w_kv_b, q_pos):
    L = c_all.shape[1]
    w = w_kv_b.reshape(KV_LORA, N_HEADS, QK_NOPE + V_DIM)
    w_uk, w_uv = w[..., :QK_NOPE], w[..., QK_NOPE:]
    q_lat = jnp.einsum('bqhn,lhn->bqhl', q_nope, w_uk)
    s = (jnp.einsum('bqhl,bkl->bhqk', q_lat, c_all)
         + jnp.einsum('bqhr,bkr->bhqk', q_rope, kr_all)).astype(jnp.float32) * ATTN_SCALE
    mask = (jnp.arange(L) // CHUNK)[None, :] <= (q_pos // CHUNK)[:, None]
    s = jnp.where(mask[None, None], s, NEG)
    p = jax.nn.softmax(s, axis=-1).astype(c_all.dtype)
    o_lat = jnp.einsum('bhqk,bkl->bqhl', p, c_all)
    return jnp.einsum('bqhl,lhv->bqhv', o_lat, w_uv)

def pool_mix(u_ext, n_hist, pos0, w_pool, s_pool):
    B, L, _ = u_ext.shape
    T = L - n_hist
    G, C = N_POOL_GROUPS, POOL_GROUP_W
    ug = u_ext.astype(jnp.float32).reshape(B, L, G, C)
    cs = jnp.concatenate([jnp.zeros((B, 1, G, C), jnp.float32), jnp.cumsum(ug, axis=1)], axis=1)
    win = np.array(POOL_WINDOWS, dtype=np.int32)
    j = np.arange(T, dtype=np.int32)[:, None]
    hi = np.broadcast_to(n_hist + j + 1, (T, G))
    lo = np.maximum(hi - win[None, :], 0)
    cnt = np.minimum(win[None, :], pos0 + j + 1).astype(np.float32)
    gi = np.arange(G)[None, :]
    win_sum = cs[:, hi, gi] - cs[:, lo, gi]
    d = win_sum / jnp.asarray(cnt)[None, :, :, None] - ug[:, n_hist:]
    y = jnp.einsum('btgc,gcd->btgd', d.astype(u_ext.dtype), w_pool)
    return y.reshape(B, T, POOL_WIDTH) * s_pool

def conv_ffn(h, conv_hist, w_up, w_dw, b_dw, w_down):
    up = h @ w_up
    T = up.shape[1]
    ext = jnp.concatenate([conv_hist.astype(up.dtype), up], axis=1)
    c = ext[:, 0:T] * w_dw[0] + ext[:, 1:T + 1] * w_dw[1] + ext[:, 2:T + 2] * w_dw[2] + b_dw
    a, b = jnp.split(c, 2, axis=-1)
    return (jax.nn.silu(a) * b) @ w_down, ext[:, -(CONV_W - 1):]

def layer(x, pe, pos0, ckv_hist, kr_hist, pool_hist, conv_hist, lp):
    (w_in, g_q, w_q_b, g_kv, w_kv_b, w_pool, s_pool, w_o, ln1_g, ln1_b,
     w_up, w_dw, b_dw, w_down, w_pg, w_pe, ln2_g, ln2_b) = lp
    B, T, _ = x.shape
    pos = pos0 + jnp.arange(T, dtype=jnp.int32)
    cos, sin = rope_tables(pos)
    z = x @ w_in
    q_a, c_raw, kr_raw, u = jnp.split(z, [Q_LORA, Q_LORA + KV_LORA, Q_LORA + KV_LORA + QK_ROPE], axis=-1)
    q = (rms_norm(q_a, g_q) @ w_q_b).reshape(B, T, N_HEADS, QK_NOPE + QK_ROPE)
    q_nope = q[..., :QK_NOPE]
    q_rope = apply_rope(q[..., QK_NOPE:], cos[:, None, :], sin[:, None, :])
    c = rms_norm(c_raw, g_kv)
    kr = apply_rope(kr_raw, cos, sin)
    if ckv_hist is None:
        kv = (c @ w_kv_b).reshape(B, T, N_HEADS, QK_NOPE + V_DIM)
        k = jnp.concatenate([kv[..., :QK_NOPE],
                             jnp.broadcast_to(kr[:, :, None, :], (B, T, N_HEADS, QK_ROPE))], axis=-1)
        qf = jnp.concatenate([q_nope, q_rope], axis=-1)
        o = prompt_attention(qf, k, kv[..., QK_NOPE:], pos)
        u_ext, n_hist = u, 0
    else:
        c_all = jnp.concatenate([ckv_hist.astype(c.dtype), c], axis=1)
        kr_all = jnp.concatenate([kr_hist.astype(kr.dtype), kr], axis=1)
        o = sample_attention(q_nope, q_rope, c_all, kr_all, w_kv_b, pos)
        u_ext, n_hist = jnp.concatenate([pool_hist.astype(u.dtype), u], axis=1), POOL_HIST
    pool_out = pool_mix(u_ext, n_hist, pos0, w_pool, s_pool)
    new_pool = u_ext[:, -POOL_HIST:]
    mix = jnp.concatenate([o.reshape(B, T, MLA_WIDTH), pool_out], axis=-1) @ w_o
    x1 = layer_norm(ALPHA * x + mix, ln1_g, ln1_b)
    ffn, new_conv = conv_ffn(x1, conv_hist, w_up, w_dw, b_dw, w_down)
    ple = jax.nn.sigmoid(x1 @ w_pg) * (pe @ w_pe)
    x2 = layer_norm(ALPHA * x1 + ffn + ple, ln2_g, ln2_b)
    return x2, c, kr, new_pool, new_conv

def setup_inputs(seed: int = 0) -> dict:
    key = jax.random.key(seed)
    ks = jax.random.split(key, 32)
    f32 = jnp.float32
    nrm = lambda k, shape, std: jax.random.normal(k, shape, f32) * std
    return {
        "x_prompt": nrm(ks[0], (BATCH, SEQ, D_MODEL), 1.0),
        "x_sample": nrm(ks[1], (DEC_BATCH, DEC_SEQ, D_MODEL), 1.0),
        "cache_ckv": nrm(ks[2], (DEPTH, DEC_BATCH, PAST_LEN, KV_LORA), 1.0),
        "cache_krope": nrm(ks[3], (DEPTH, DEC_BATCH, PAST_LEN, QK_ROPE), 1.0),
        "state_pool": nrm(ks[4], (DEPTH, DEC_BATCH, POOL_HIST, POOL_WIDTH), 1.0),
        "state_ffn_conv": nrm(ks[5], (DEPTH, DEC_BATCH, CONV_W - 1, 2 * D_FF), 1.0),
        "p_prompt": nrm(ks[6], (DEPTH, BATCH, SEQ, PLE_DIM), 1.0),
        "p_sample": nrm(ks[7], (DEPTH, DEC_BATCH, DEC_SEQ, PLE_DIM), 1.0),
        "w_in": nrm(ks[8], (DEPTH, D_MODEL, IN_WIDTH), D_MODEL ** -0.5),
        "g_q": 1.0 + nrm(ks[9], (DEPTH, Q_LORA), 0.02),
        "w_q_b": nrm(ks[10], (DEPTH, Q_LORA, N_HEADS * (QK_NOPE + QK_ROPE)), Q_LORA ** -0.5),
        "g_kv": 1.0 + nrm(ks[11], (DEPTH, KV_LORA), 0.02),
        "w_kv_b": nrm(ks[12], (DEPTH, KV_LORA, N_HEADS * (QK_NOPE + V_DIM)), KV_LORA ** -0.5),
        "w_pool": nrm(ks[13], (DEPTH, N_POOL_GROUPS, POOL_GROUP_W, POOL_GROUP_W), POOL_GROUP_W ** -0.5),
        "s_pool": 1.0 + nrm(ks[14], (DEPTH, POOL_WIDTH), 0.02),
        "w_o": nrm(ks[15], (DEPTH, D_MODEL, D_MODEL), BETA * D_MODEL ** -0.5),
        "ln1_g": 1.0 + nrm(ks[16], (DEPTH, D_MODEL), 0.02),
        "ln1_b": nrm(ks[17], (DEPTH, D_MODEL), 0.02),
        "w_up": nrm(ks[18], (DEPTH, D_MODEL, 2 * D_FF), D_MODEL ** -0.5),
        "w_dw": nrm(ks[19], (DEPTH, CONV_W, 2 * D_FF), CONV_W ** -0.5),
        "b_dw": nrm(ks[20], (DEPTH, 2 * D_FF), 0.02),
        "w_down": nrm(ks[21], (DEPTH, D_FF, D_MODEL), BETA * D_FF ** -0.5),
        "w_pg": nrm(ks[22], (DEPTH, D_MODEL, D_MODEL), D_MODEL ** -0.5),
        "w_pe": nrm(ks[23], (DEPTH, PLE_DIM, D_MODEL), BETA * PLE_DIM ** -0.5),
        "ln2_g": 1.0 + nrm(ks[24], (DEPTH, D_MODEL), 0.02),
        "ln2_b": nrm(ks[25], (DEPTH, D_MODEL), 0.02),
    }

def reference(x_prompt, x_sample, cache_ckv, cache_krope, state_pool, state_ffn_conv, p_prompt, p_sample,
              w_in, g_q, w_q_b, g_kv, w_kv_b, w_pool, s_pool, w_o, ln1_g, ln1_b,
              w_up, w_dw, b_dw, w_down, w_pg, w_pe, ln2_g, ln2_b):
    n_past = cache_ckv.shape[2]
    hp, hs = x_prompt, x_sample
    ckv_p, kr_p, pool_p, conv_p = [], [], [], []
    ckv_s, kr_s, pool_s, conv_s = [], [], [], []
    for i in range(DEPTH):
        lp = (w_in[i], g_q[i], w_q_b[i], g_kv[i], w_kv_b[i], w_pool[i], s_pool[i], w_o[i],
              ln1_g[i], ln1_b[i], w_up[i], w_dw[i], b_dw[i], w_down[i], w_pg[i], w_pe[i],
              ln2_g[i], ln2_b[i])
        zero_conv = jnp.zeros((hp.shape[0], CONV_W - 1, 2 * D_FF), hp.dtype)
        hp, c1, k1, pl1, cv1 = layer(hp, p_prompt[i], 0, None, None, None, zero_conv, lp)
        hs, c2, k2, pl2, cv2 = layer(hs, p_sample[i], n_past, cache_ckv[i], cache_krope[i],
                                     state_pool[i], state_ffn_conv[i], lp)
        ckv_p.append(c1); kr_p.append(k1); pool_p.append(pl1); conv_p.append(cv1)
        ckv_s.append(c2); kr_s.append(k2); pool_s.append(pl2); conv_s.append(cv2)
    return (hp, hs,
            jnp.stack(ckv_p), jnp.stack(kr_p), jnp.stack(pool_p), jnp.stack(conv_p),
            jnp.stack(ckv_s), jnp.stack(kr_s), jnp.stack(pool_s), jnp.stack(conv_s))


_drawn_inputs = setup_inputs


def setup_inputs(seed=0):
    import zlib

    import numpy as np

    out = dict(_drawn_inputs(seed))
    spreads = {}
    factors = {'cache_krope': 4.322,
     'g_q': 8.0,
     'g_kv': 2.817,
     's_pool': 8.0,
     'ln1_g': 2.822,
     'ln1_b': 2.811,
     'b_dw': 7.138,
     'ln2_g': 2.847,
     'ln2_b': 2.806}
    for name, (base, spread) in spreads.items():
        noise = np.random.default_rng([zlib.crc32(name.encode()), seed]).standard_normal(out[name].shape)
        drawn = base * np.exp(spread * noise) if base else spread * noise
        out[name] = __import__('jax').numpy.asarray(drawn.astype(out[name].dtype))
    for name, factor in factors.items():
        out[name] = (out[name] * factor).astype(out[name].dtype)
    return out
```

```python
from contextlib import ExitStack

import concourse.bass as bass
from concourse import mybir

F32 = mybir.dt.float32
F32R = mybir.dt.float32r
ACT = mybir.ActivationFunctionType
ALU = mybir.AluOpType
AX = mybir.AxisListType

P = 128
D = 1024
KD = D // P
SEQ = 2048
ROWS, NEW, PAST = 8, 16, 512
SAMPLE = ROWS * NEW
TOK = SEQ + SAMPLE
LORA = 256
ROPE = 32
NOPE = 64
VD = 64
HEADS = 8
MLA = HEADS * VD
POOLS = (2, 4, 8, 16)
HIST = 15
FF = 2816
FT = FF // P
PLE = 256
CW = 512
CHUNKS = SEQ // CW
ALPHA = 2.0 ** 0.25
SCALE = (NOPE + ROPE) ** -0.5
NEG = -1e30
ds = bass.ds


class Arena:

    def __init__(self, nc, ctx, tag):
        self.nc, self.ctx, self.tag = nc, ctx, tag

    def sb(self, name, shape, dt=F32):
        return self.ctx.enter_context(self.nc.sbuf_tensor(f"{self.tag}_{name}", shape, dt))

    def bank(self, name):
        return self.ctx.enter_context(self.nc.psum_tensor(f"{self.tag}_{name}", [P, 512], F32))

    def sem(self, name):
        return self.nc.alloc_semaphore(name=f"{self.tag}_{name}")


def take(eng, met):
    eng.sem_inc(met, 1)


def f32(ap):
    return ap.bitcast(F32)


def product(pe, out, pairs, rhs_pairs, first, last, **kw):
    (lh, ll), (rh, rl) = pairs, rhs_pairs
    pe.matmul(out, lh, rh, start=first, stop=False, **kw)
    pe.matmul(out, ll, rh, start=False, stop=False, **kw)
    return pe.matmul(out, lh, rl, start=False, stop=last, **kw)

def at(c, per, k):
    return (c + 2) * per + k + 1


UNITS = ("c0", "c1", "q0", "q1", "kr", "u3", "u2", "u1", "u0")
UNIT_BANK = (0, 1, 2, 3, 0, 1, 2, 3, 0)
NU = len(UNITS)
RAW = 4
W_PIECES = 2 * 8 + 1 + 1


def nth(c, per, k):
    return (c + 1) * per + k + 1


def phase_project(nc, g):
    with ExitStack() as ctx:
        ar = Arena(nc, ctx, "pj")
        sb, bank, sem = ar.sb, ar.bank, ar.sem
        raw = sb("raw", [P, RAW, CW])
        w_hi = sb("w_hi", [P, 8, KD, P], F32R)
        w_lo = sb("w_lo", [P, 8, KD, P], F32R)
        wk_hi = sb("wk_hi", [P, KD, 64], F32R)
        wk_lo = sb("wk_lo", [P, KD, 64], F32R)
        wp_hi = sb("wp_hi", [P, 4, P], F32R)
        wp_lo = sb("wp_lo", [P, 4, P], F32R)
        x_hi = sb("x_hi", [P, 2, KD, CW], F32R)
        x_lo = sb("x_lo", [P, 2, KD, CW], F32R)
        u = sb("u", [P, 4, 16 + CW])
        win = sb("win", [P, 2, 16 + CW])
        dif = sb("dif", [P, 2, CW])
        t_hi = sb("t_hi", [P, 4, CW], F32R)
        t_lo = sb("t_lo", [P, 4, CW], F32R)
        lat = sb("lat", [P, 4, CW])
        sq = sb("sq", [P, CW])
        rstd = sb("rstd", [P, 2, CW])
        latn = sb("latn", [P, 2, CW])
        kr_t = sb("kr_t", [ROPE, 3, CW])
        trig = sb("trig", [64, CW])
        pool_o = sb("pool_o", [P, 2, CW])
        gains = sb("gains", [P, 8])
        inv_cnt = sb("inv_cnt", [P, 2, 4, 16])
        fix = sb("fix", [P, 16])
        ones = sb("ones", [P, P], F32R)
        ps = [bank(f"ps{i}") for i in range(4)]
        ps_stat = [bank("stat_c"), bank("stat_q")]
        ps_pool = [bank("pool0"), bank("pool1")]

        landed = [sem(f"landed{i}") for i in range(RAW)]
        const_in = sem("const_in")
        trig_in = sem("trig_in")
        hist_in = sem("hist_in")
        cleared = sem("cleared")
        split_hi = sem("split_hi")
        split_lo = sem("split_lo")
        unit_done = sem("unit_done")
        evac = sem("evac")
        squared = sem("squared")
        kr_mul = sem("kr_mul")
        kr_ready = sem("kr_ready")
        tmp_hi = sem("tmp_hi")
        tmp_lo = sem("tmp_lo")
        tmp_used = sem("tmp_used")
        var_eps = sem("var_eps")
        root = sem("root")
        rs = sem("rs")
        normed = sem("normed")
        step = sem("step")
        diff = sem("diff")
        fixed = sem("fixed")
        pool_ev = sem("pool_ev")
        st_lat = [sem("st_lat0"), sem("st_lat1")]
        st_kr = sem("st_kr")
        st_pool = [sem("st_pool0"), sem("st_pool1")]
        st_hist = sem("st_hist")
        SAMPLE_C = CHUNKS
        PJ_EPS = 1e-6

        w_dst = []
        for n, name in enumerate(UNITS):
            if name == "kr":
                w_dst.append((wk_hi[:, :, :], wk_lo[:, :, :]))
            else:
                m = n if n < 4 else n - 1
                w_dst += [(w_hi[:, m, 4 * h:4 * h + 4, :], w_lo[:, m, 4 * h:4 * h + 4, :]) for h in range(2)]
        w_dst.append((wp_hi[:, :, :], wp_lo[:, :, :]))
        assert len(w_dst) == W_PIECES

        def unit_w(n, k):
            if UNITS[n] == "kr":
                return wk_hi[:, k, :], wk_lo[:, k, :]
            m = n if n < 4 else n - 1
            return w_hi[:, m, k, :], w_lo[:, m, k, :]

        def x_slot(k):
            return (W_PIECES + k) % RAW

        def x_piece(c, k):
            return W_PIECES + c * KD + k

        def x_use(c, k):
            return (W_PIECES + k) // RAW + 1 + c * (KD // RAW)

        def rows16(ap):
            return ap.rearrange("p (r t) -> p r t", t=NEW)

        def rows32(ap):
            return ap.rearrange("p (r t) -> p r t", t=32)

        block = ctx.enter_context(nc.Block())

        @block.sync
        def _(sp):
            sp.dma_start(gains[:, :], g["gains"]).then_inc(const_in, 16)
            sp.dma_start(inv_cnt[:, :, :, :], g["inv_cnt"]).then_inc(const_in, 16)
            for m in range(W_PIECES):
                if m >= RAW:
                    sp.wait_ge(split_lo, m - RAW + 1)
                sp.dma_start(raw[:, m % RAW, :], g["w_in_p"][m]).then_inc(landed[m % RAW], 16)
            for s, n in ((st_lat[0], 2), (st_lat[1], 2), (st_kr, 1), (st_pool[0], 2), (st_pool[1], 2)):
                sp.sem_inc(s, 16 * n)

            def load_x(c):
                for k in range(KD):
                    sp.wait_ge(split_lo, x_piece(c, k) - RAW + 1)
                    sp.dma_start(raw[:, x_slot(k), :], g["x_t"][k * P:(k + 1) * P, ds(c * CW, CW)])\
                      .then_inc(landed[x_slot(k)], 16)

            def load_trig(c):
                sp.dma_start(trig[:, :], g["trig_k"][:, ds(c * CW, CW)]).then_inc(trig_in, 16)

            def store(c, width):
                for i in range(4):
                    dst = (g["c_t"], g["qn_t"])[i // 2]
                    sp.wait_ge(normed, nth(c, 4, i))
                    sp.dma_start(dst[(i % 2) * P:(i % 2 + 1) * P, ds(c * CW, width)], latn[:, i % 2, 0:width])\
                      .then_inc(st_lat[i % 2], 16)
                sp.wait_ge(kr_ready, nth(c, 1, 0))
                sp.dma_start(g["kr_t"][:, ds(c * CW, width)], kr_t[:, 2, 0:width]).then_inc(st_kr, 16)
                for i in range(4):
                    sp.wait_ge(pool_ev, nth(c, 4, i))
                    row = MLA + (3 - i) * P
                    sp.dma_start(g["mix_t"][row:row + P, ds(c * CW, width)], pool_o[:, i % 2, 0:width])\
                      .then_inc(st_pool[i % 2], 16)

            load_x(0)
            load_trig(0)
            with sp.Fori(0, CHUNKS) as c:
                load_x(c + 1)
                sp.wait_ge(kr_mul, nth(c, 2, 1))
                load_trig(c + 1)
                store(c, CW)
            sp.dma_start(g["pool_p"], u[:, :, CW + 1:CW + 16]).then_inc(st_hist, 16)
            sp.wait_ge(st_hist, 16)
            sp.wait_ge(diff, nth(CHUNKS - 1, 4, 3))
            for grp in range(4):
                sp.dma_start(rows32(u[:, grp, 0:ROWS * 32])[:, :, 1:16], g["pool_hist"][:, grp]).then_inc(hist_in, 16)
            sp.wait_ge(evac, nth(SAMPLE_C, 8, 7))
            for grp in range(4):
                sp.dma_start(g["pool_s"][:, grp], rows32(u[:, grp, 0:ROWS * 32])[:, :, 17:32]).then_inc(st_hist, 16)
            store(SAMPLE_C, SAMPLE)
            sp.wait_ge(st_hist, 80)
            for s, n in ((st_lat[0], 2), (st_lat[1], 2), (st_kr, 1), (st_pool[0], 2), (st_pool[1], 2)):
                sp.wait_ge(s, nth(SAMPLE_C, n, n - 1) * 16)

        @block.gpsimd
        def _(pool):
            pool.sem_inc(tmp_lo, 8)

            def split_x(c, par):
                for k in range(KD):
                    pool.wait_ge(split_hi, x_piece(c, k) + 1)
                    pool.tensor_tensor(x_lo[:, par, k, :], raw[:, x_slot(k), :], f32(x_hi[:, par, k, :]),
                                       ALU.subtract).then_inc(split_lo, 1)

            def tmp(c, i, src, width):
                pool.wait_ge(tmp_hi, nth(c, 8, i))
                pool.tensor_tensor(t_lo[:, i % 4, 0:width], src[:, 0:width], f32(t_hi[:, i % 4, 0:width]),
                                   ALU.subtract).then_inc(tmp_lo, 1)

            def chunk(c, par, width, more=True):
                for i in range(4):
                    tmp(c, i, sq[:, :], width)
                if more:
                    split_x(c + 1, 1 - par)
                for i in range(4):
                    tmp(c, 4 + i, dif[:, i % 2, :], width)

            for m in range(W_PIECES):
                hi, lo = w_dst[m]
                pool.wait_ge(split_hi, m + 1)
                pool.tensor_tensor(lo, raw[:, m % RAW, :].rearrange("p (a b) -> p a b", a=hi.shape[1]), f32(hi),
                                   ALU.subtract).then_inc(split_lo, 1)
            split_x(0, 0)
            with pool.Fori(0, CHUNKS // 2) as it:
                chunk(2 * it, 0, CW)
                chunk(2 * it + 1, 1, CW)
            chunk(SAMPLE_C, 0, SAMPLE, more=False)

        @block.scalar
        def _(act):
            for s, n in ((evac, 8), (squared, 4), (tmp_hi, 8), (root, 2), (pool_ev, 4)):
                act.sem_inc(s, n)

            def split_x(c, par):
                for k in range(KD):
                    act.wait_ge(landed[x_slot(k)], 16 * x_use(c, k))
                    if k == 0:
                        act.wait_ge(unit_done, nth(c - 2, NU, NU - 1))
                    act.activation(x_hi[:, par, k, :], raw[:, x_slot(k), :], ACT.Copy).then_inc(split_hi, 1)

            def chunk(c, par, width, sample=False):
                for i in range(4):
                    act.wait_ge(unit_done, nth(c, NU, i))
                    act.wait_ge(normed, nth(c - 1, 4, i))
                    act.activation(lat[:, i, 0:width], ps[i][:, 0:width], ACT.Copy).then_inc(evac, 1)
                    act.wait_ge(tmp_lo, nth(c, 8, i - 1))
                    act.activation(sq[:, 0:width], ps[i][:, 0:width], ACT.Square).then_inc(squared, 1)
                    act.wait_ge(squared, nth(c, 4, i))
                    act.wait_ge(tmp_used, nth(c, 8, i - 4))
                    act.activation(t_hi[:, i, 0:width], sq[:, 0:width], ACT.Copy).then_inc(tmp_hi, 1)
                if not sample:
                    split_x(c + 1, 1 - par)
                for i in range(4):
                    grp = 3 - i
                    if i < 2:
                        act.wait_ge(var_eps, nth(c, 2, i))
                        act.activation(rstd[:, i, 0:width], rstd[:, i, 0:width], ACT.Sqrt).then_inc(root, 1)
                    act.wait_ge(unit_done, nth(c, NU, 5 + i))
                    src = ps[UNIT_BANK[5 + i]][:, 0:width]
                    if sample:
                        act.wait_ge(hist_in, 64)
                        act.activation(rows32(u[:, grp, 0:ROWS * 32])[:, :, 16:32], rows16(src),
                                       ACT.Copy).then_inc(evac, 1)
                    else:
                        act.wait_ge(step, nth(c, 11, 0))
                        act.activation(u[:, grp, 16:16 + width], src, ACT.Copy).then_inc(evac, 1)
                for i in range(4):
                    act.wait_ge(diff, nth(c, 4, i))
                    act.wait_ge(tmp_used, nth(c, 8, i))
                    act.activation(t_hi[:, i, 0:width], dif[:, i % 2, 0:width], ACT.Copy).then_inc(tmp_hi, 1)
                for i in range(4):
                    act.wait_ge(tmp_used, nth(c, 8, 4 + i))
                    act.wait_ge(st_pool[i % 2], nth(c, 2, i // 2 - 1) * 16)
                    act.activation(pool_o[:, i % 2, 0:width], ps_pool[i % 2][:, 0:width], ACT.Copy,
                                   scale=gains[:, 4 + 3 - i:5 + 3 - i]).then_inc(pool_ev, 1)

            act.wait_ge(const_in, 32)
            for m in range(W_PIECES):
                hi, _ = w_dst[m]
                act.wait_ge(landed[m % RAW], 16 * (m // RAW + 1))
                act.activation(hi, raw[:, m % RAW, :].rearrange("p (a b) -> p a b", a=hi.shape[1]),
                               ACT.Copy).then_inc(split_hi, 1)
            for k in range(KD):
                act.wait_ge(landed[x_slot(k)], 16 * x_use(0, k))
                act.activation(x_hi[:, 0, k, :], raw[:, x_slot(k), :], ACT.Copy).then_inc(split_hi, 1)
            with act.Fori(0, CHUNKS // 2) as it:
                chunk(2 * it, 0, CW)
                chunk(2 * it + 1, 1, CW)
            chunk(SAMPLE_C, 0, SAMPLE, sample=True)

        @block.vector
        def _(dve):
            dve.memset(u[:, :, :], 0.0).then_inc(cleared, 1)
            dve.memset(f32(ones[:, :]), 1.0).then_inc(cleared, 1)
            for s, n in ((kr_mul, 2), (kr_ready, 1), (var_eps, 2), (rs, 2), (normed, 4), (step, 11), (diff, 4),
                         (fixed, 9)):
                dve.sem_inc(s, n)
            dve.wait_ge(cleared, 2)
            dve.wait_ge(const_in, 32)

            def normalise(c, j, width):
                dve.wait_ge(tmp_used, nth(c, 8, 2 * j + 1))
                dve.wait_ge(normed, nth(c - 1, 4, 2 * j + 1))
                dve.tensor_scalar(rstd[:, j, 0:width], ps_stat[j][:, 0:width], 1.0 / LORA, PJ_EPS,
                                  ALU.mult, ALU.add).then_inc(var_eps, 1)
                dve.wait_ge(root, nth(c, 2, j))
                dve.reciprocal(rstd[:, j, 0:width], rstd[:, j, 0:width]).then_inc(rs, 1)
                dve.wait_ge(rs, nth(c, 2, j))
                for i in (2 * j, 2 * j + 1):
                    dve.wait_ge(evac, nth(c, 8, i))
                    dve.wait_ge(st_lat[i % 2], nth(c, 2, j - 1) * 16)
                    dve.scalar_tensor_tensor(out=latn[:, i % 2, 0:width], in0=lat[:, i, 0:width],
                                             scalar=gains[:, i:i + 1], in1=rstd[:, j, 0:width],
                                             op0=ALU.mult, op1=ALU.mult).then_inc(normed, 1)

            def pool_group(c, i, width, sample, done):
                grp = 3 - i
                dve.wait_ge(evac, nth(c, 8, 4 + i))
                if sample:
                    dve.wait_ge(diff, nth(c, 4, i - 1))

                def span(buf, a, b):
                    if sample:
                        return rows32(buf[:, 0:ROWS * 32])[:, :, a:b]
                    return buf[:, a:b]
                end = 32 if sample else 16 + width
                src = u[:, grp, :]
                for level in range(1, grp + 2):
                    dst = win[:, level % 2, :]
                    lo, back = 2 ** level, 2 ** (level - 1)
                    dve.wait_ge(step, nth(c, 11, done - 1))
                    dve.tensor_tensor(span(dst, lo, end), span(src, lo, end), span(src, lo - back, end - back),
                                      ALU.add).then_inc(step, 1)
                    done += 1
                    src = dst
                dve.wait_ge(step, nth(c, 11, done - 1))
                dve.wait_ge(tmp_lo, nth(c, 8, 4 + i - 2))
                out = dif[:, i % 2, 0:width]
                main = dve.scalar_tensor_tensor(
                    out=rows16(out) if sample else out, in0=span(src, 16, end), scalar=1.0 / POOLS[grp],
                    in1=span(u[:, grp, :], 16, end), op0=ALU.mult, op1=ALU.subtract)
                if sample:
                    main.then_inc(diff, 1)
                else:
                    main.then_inc(fixed, 1)
                    dve.tensor_tensor(fix[:, :], src[:, 16:32], inv_cnt[:, 0, grp, :], ALU.mult).then_inc(fixed, 1)
                    dve.wait_ge(fixed, nth(c, 9, 2 * i + 1))
                    dve.tensor_tensor(dif[:, i % 2, 0:16], fix[:, :], u[:, grp, 16:32], ALU.subtract)\
                       .then_inc(diff, 1)
                return done

            def chunk(c, width, sample=False):
                done = 1
                if not sample:
                    dve.wait_ge(evac, nth(c - 1, 8, 7))
                    dve.tensor_copy(u[:, :, 1:16], u[:, :, CW + 1:CW + 16]).then_inc(step, 1)
                dve.wait_ge(unit_done, nth(c, NU, 4))
                dve.wait_ge(trig_in, nth(c - 1, 1, 0) * 16)
                dve.wait_ge(kr_ready, nth(c - 1, 1, 0))
                src = ps[UNIT_BANK[4]]
                dve.tensor_tensor(kr_t[:, 0, 0:width], src[0:32, 0:width], trig[0:32, 0:width], ALU.mult)\
                   .then_inc(kr_mul, 1)
                dve.tensor_tensor(kr_t[:, 1, 0:width], src[32:64, 0:width], trig[32:64, 0:width], ALU.mult)\
                   .then_inc(kr_mul, 1)
                dve.wait_ge(kr_mul, nth(c, 2, 1))
                dve.wait_ge(st_kr, nth(c - 1, 1, 0) * 16)
                dve.tensor_tensor(kr_t[:, 2, 0:width], kr_t[:, 0, 0:width], kr_t[:, 1, 0:width], ALU.add)\
                   .then_inc(kr_ready, 1)
                normalise(c, 0, width)
                done = pool_group(c, 0, width, sample, done)
                normalise(c, 1, width)
                for i in range(1, 4):
                    done = pool_group(c, i, width, sample, done)
                if not sample:
                    dve.wait_ge(diff, nth(c, 4, 3))
                    dve.tensor_copy(inv_cnt[:, 0, :, :], inv_cnt[:, 1, :, :]).then_inc(fixed, 1)
                    dve.wait_ge(fixed, nth(c, 9, 8))

            with dve.Fori(0, CHUNKS) as c:
                chunk(c, CW)
            dve.sem_inc(step, 1)
            chunk(SAMPLE_C, SAMPLE, sample=True)

        @block.tensor
        def _(pe):
            pe.sem_inc(unit_done, NU)
            pe.sem_inc(tmp_used, 8)
            pe.wait_ge(cleared, 2)

            def squares(c, i, width):
                pe.wait_ge(tmp_lo, nth(c, 8, i))
                if i % 2 == 0:
                    pe.wait_ge(var_eps, nth(c - 1, 2, i // 2))
                out = ps_stat[i // 2][:, 0:width]
                pe.matmul(out, ones[:, :], t_hi[:, i, 0:width], start=i % 2 == 0, stop=False)
                pe.matmul(out, ones[:, :], t_lo[:, i, 0:width], start=False, stop=i % 2 == 1).then_inc(tmp_used, 1)

            def chunk(c, par, width):
                for n in range(NU):
                    if n == 5:
                        squares(c, 0, width)
                        squares(c, 1, width)
                    if n == 6:
                        squares(c, 2, width)
                        squares(c, 3, width)
                    m = 64 if UNITS[n] == "kr" else P
                    b = UNIT_BANK[n]
                    if n == 8:
                        pe.wait_ge(kr_mul, nth(c, 2, 1))
                    elif n < 4:
                        pe.wait_ge(evac, nth(c - 1, 8, 4 + (n + 3) % 4))
                    else:
                        pe.wait_ge(evac, nth(c, 8, n - 4))
                        pe.wait_ge(squared, nth(c, 4, n - 4))
                    for k in range(KD):
                        if n == 0:
                            pe.wait_ge(split_lo, x_piece(c, k) + 1)
                        mm = product(pe, ps[b][0:m, 0:width], unit_w(n, k),
                                     (x_hi[:, par, k, 0:width], x_lo[:, par, k, 0:width]), k == 0, k == KD - 1)
                    mm.then_inc(unit_done, 1)
                for i in range(4):
                    pe.wait_ge(tmp_lo, nth(c, 8, 4 + i))
                    pe.wait_ge(pool_ev, nth(c, 4, i - 2))
                    product(pe, ps_pool[i % 2][:, 0:width], (wp_hi[:, 3 - i, :], wp_lo[:, 3 - i, :]),
                            (t_hi[:, i, 0:width], t_lo[:, i, 0:width]), True, True).then_inc(tmp_used, 1)

            with pe.Fori(0, CHUNKS // 2) as it:
                chunk(2 * it, 0, CW)
                chunk(2 * it + 1, 1, CW)
            chunk(SAMPLE_C, 0, SAMPLE)



HD_W = 8


def phase_heads(nc, g):
    with ExitStack() as ctx:
        ar = Arena(nc, ctx, "hd")
        sb, bank, sem = ar.sb, ar.bank, ar.sem
        raw = sb("raw", [P, 4, CW])
        wq_hi, wq_lo = sb("wq_hi", [P, HEADS, 2, P], F32R), sb("wq_lo", [P, HEADS, 2, P], F32R)
        wk_hi, wk_lo = sb("wk_hi", [P, HEADS // 2, 2, P], F32R), sb("wk_lo", [P, HEADS // 2, 2, P], F32R)
        wv_hi, wv_lo = sb("wv_hi", [P, 2, MLA], F32R), sb("wv_lo", [P, 2, MLA], F32R)
        x_hi, x_lo = sb("x_hi", [P, 2, 4, CW], F32R), sb("x_lo", [P, 2, 4, CW], F32R)
        trig = sb("trig", [P, CW])
        rot = sb("rot", [P, 2, CW])
        out = sb("out", [P, 4, CW])
        ps = [bank(f"ps{i}") for i in range(8)]

        landed = [sem(f"landed{i}") for i in range(4)]
        trig_in, met = sem("trig_in"), sem("met")
        split_hi, split_lo = sem("split_hi"), sem("split_lo")
        done = sem("done")
        copied = sem("copied")
        turned = sem("turned")
        rotated = sem("rotated")
        stored = [sem(f"stored{i}") for i in range(4)]

        w_dst = []
        for i in range(4):
            w_dst.append((wq_hi[:, 2 * i:2 * i + 2], wq_lo[:, 2 * i:2 * i + 2]))
        for i in range(2):
            w_dst.append((wk_hi[:, 2 * i:2 * i + 2], wk_lo[:, 2 * i:2 * i + 2]))
        for i in range(2):
            w_dst.append((wv_hi[:, i:i + 1, :], wv_lo[:, i:i + 1, :]))

        def flat(ap):
            return ap.rearrange("p a b c -> p (a b c)") if len(ap.shape) == 4 else ap.rearrange("p a b -> p (a b)")

        block = ctx.enter_context(nc.Block())

        @block.sync
        def _(sp):
            for i in range(4):
                sp.sem_inc(stored[i], 16 * 4)

            def load(c, width, pieces):
                for k in range(pieces):
                    sp.wait_ge(split_lo, HD_W + 4 * c - 4 + k + 1)
                    src = (g["qn_t"], g["c_t"])[k // 2]
                    sp.dma_start(raw[:, k, 0:width], src[(k % 2) * P:(k % 2 + 1) * P, ds(c * CW, width)])\
                      .then_inc(landed[k], 16)

            def load_trig(c):
                sp.dma_start(trig[64:128, :], g["trig_k"][:, ds(c * CW, CW)]).then_inc(trig_in, 16)

            def store(c, width, n):
                if n < 8:
                    sp.wait_ge(rotated, nth(c, 8, n))
                    take(sp, met)
                sp.wait_ge(copied, nth(c, 16, n))
                if n < 8:
                    dst, src = g["q_t"][n * 96:(n + 1) * 96, ds(c * CW, width)], out[0:96, n % 4, 0:width]
                elif n < 12:
                    dst, src = g["k_t"][(n - 8) * P:(n - 7) * P, ds(c * CW, width)], out[:, n % 4, 0:width]
                else:
                    dst, src = g["v"][ds(c * CW + (n - 12) * P, P), :], out[:, n % 4, :]
                sp.dma_start(dst, src).then_inc(stored[n % 4], 16)

            for m in range(HD_W):
                if m >= 4:
                    sp.wait_ge(split_lo, m - 3)
                sp.dma_start(raw[:, m % 4, :], g["w_hd_p"][m]).then_inc(landed[m % 4], 16)
            load(0, CW, 4)
            load_trig(0)
            with sp.Fori(0, CHUNKS - 1) as c:
                load(c + 1, CW, 4)
                for n in range(16):
                    store(c, CW, n)
                    if n == 7:
                        load_trig(c + 1)
            load(CHUNKS, SAMPLE, 2)
            for n in range(16):
                store(CHUNKS - 1, CW, n)
                if n == 7:
                    load_trig(CHUNKS)
            for n in range(8):
                store(CHUNKS, SAMPLE, n)
            for i in range(4):
                sp.wait_ge(stored[i], (nth(CHUNKS - 1, 4, 3) + 2) * 16)

        @block.gpsimd
        def _(pool):
            for m in range(HD_W):
                hi, lo = w_dst[m]
                pool.wait_ge(split_hi, m + 1)
                pool.tensor_tensor(flat(lo), raw[:, m % 4, :], f32(flat(hi)), ALU.subtract).then_inc(split_lo, 1)

            def split(c, par, width, pieces):
                for k in range(pieces):
                    pool.wait_ge(split_hi, HD_W + 4 * c + k + 1)
                    pool.tensor_tensor(x_lo[:, par, k, 0:width], raw[:, k, 0:width], f32(x_hi[:, par, k, 0:width]),
                                       ALU.subtract).then_inc(split_lo, 1)
            split(0, 0, CW, 4)
            with pool.Fori(0, CHUNKS // 2 - 1) as it:
                split(2 * it + 1, 1, CW, 4)
                split(2 * it + 2, 0, CW, 4)
            split(CHUNKS - 1, 1, CW, 4)
            split(CHUNKS, 0, SAMPLE, 2)

        @block.scalar
        def _(act):
            act.sem_inc(copied, 16)
            for m in range(HD_W):
                act.wait_ge(landed[m % 4], 16 * (m // 4 + 1))
                act.activation(flat(w_dst[m][0]), raw[:, m % 4, :], ACT.Copy).then_inc(split_hi, 1)

            def split(c, par, width, pieces):
                for k in range(pieces):
                    act.wait_ge(landed[k], 16 * (HD_W // 4 + c + 1))
                    if k == 0:
                        act.wait_ge(done, nth(c - 2, 16, 15))
                    act.activation(x_hi[:, par, k, 0:width], raw[:, k, 0:width], ACT.Copy).then_inc(split_hi, 1)

            def copy(c, n, width):
                act.wait_ge(done, nth(c, 16, n))
                act.wait_ge(stored[n % 4], nth(c, 4, n // 4 - 1) * 16)
                rows = NOPE if n < 8 else P
                act.activation(out[0:rows, n % 4, 0:width], ps[n % 8][0:rows, 0:width], ACT.Copy)\
                   .then_inc(copied, 1)

            def chunk(c, par, width, following):
                if following is not None:
                    split(c + 1, 1 - par, *following)
                for n in range(16 if width == CW else 8):
                    copy(c, n, width)

            for k in range(4):
                act.wait_ge(landed[k], 16 * (HD_W // 4 + 1))
                act.activation(x_hi[:, 0, k, :], raw[:, k, :], ACT.Copy).then_inc(split_hi, 1)
            with act.Fori(0, CHUNKS // 2 - 1) as it:
                chunk(2 * it, 0, CW, (CW, 4))
                chunk(2 * it + 1, 1, CW, (CW, 4))
            chunk(CHUNKS - 2, 0, CW, (CW, 4))
            chunk(CHUNKS - 1, 1, CW, (SAMPLE, 2))
            chunk(CHUNKS, 0, SAMPLE, None)

        @block.vector
        def _(dve):
            dve.sem_inc(turned, 16)
            dve.sem_inc(rotated, 8)

            def chunk(c, width):
                dve.wait_ge(trig_in, (c + 1) * 16)
                for n in range(8):
                    dve.wait_ge(done, nth(c, 16, n))
                    dve.wait_ge(rotated, nth(c, 8, n - 1))
                    dve.tensor_tensor(rot[64:96, 0, 0:width], ps[n][64:96, 0:width], trig[64:96, 0:width],
                                      ALU.mult).then_inc(turned, 1)
                    dve.tensor_tensor(rot[64:96, 1, 0:width], ps[n][96:128, 0:width], trig[96:128, 0:width],
                                      ALU.mult).then_inc(turned, 1)
                    dve.wait_ge(turned, nth(c, 16, 2 * n + 1))
                    dve.wait_ge(stored[n % 4], nth(c, 4, n // 4 - 1) * 16)
                    dve.tensor_tensor(out[64:96, n % 4, 0:width], rot[64:96, 0, 0:width], rot[64:96, 1, 0:width],
                                      ALU.add).then_inc(rotated, 1)

            with dve.Fori(0, CHUNKS) as c:
                chunk(c, CW)
            chunk(CHUNKS, SAMPLE)

        @block.tensor
        def _(pe):
            pe.sem_inc(done, 16)

            def chunk(c, par, width):
                def x(k, a=0, b=width):
                    return x_hi[:, par, k, a:b], x_lo[:, par, k, a:b]
                for n in range(16 if width == CW else 8):
                    if n == 0:
                        pe.wait_ge(split_lo, HD_W + 4 * c + 2)
                    if n == 8:
                        pe.wait_ge(split_lo, HD_W + 4 * c + 4)
                    if n < 8:
                        pe.wait_ge(copied, nth(c - 1, 16, n + 8))
                    else:
                        pe.wait_ge(copied, nth(c, 16, n - 8))
                        pe.wait_ge(turned, nth(c, 16, 2 * (n - 8) + 1))
                    for k in range(2):
                        if n < 8:
                            w, m = (wq_hi[:, n, k, :], wq_lo[:, n, k, :]), x(k)
                        elif n < 12:
                            w, m = (wk_hi[:, n - 8, k, :], wk_lo[:, n - 8, k, :]), x(2 + k)
                        else:
                            t = n - 12
                            w, m = x(2 + k, t * P, (t + 1) * P), (wv_hi[:, k, :], wv_lo[:, k, :])
                        o = ps[n % 8][:, 0:CW if n >= 12 else width]
                        mm = product(pe, o, w, m, k == 0, k == 1)
                    mm.then_inc(done, 1)

            with pe.Fori(0, CHUNKS // 2) as it:
                chunk(2 * it, 0, CW)
                chunk(2 * it + 1, 1, CW)
            chunk(CHUNKS, 0, SAMPLE)


QT = SEQ // P
TILES = 2 * QT
NCH = [t % QT // 4 + 1 for t in range(TILES)]
BASE = [sum(NCH[:t]) for t in range(TILES + 1)]
SBANKS = 4
STEPS = TILES + 5


def slots(k):
    return max([NCH[t] for t in (k, k - 2) if 0 <= t < TILES] + [1])


def value_parts(k, slot):
    j = k // 2 - 2
    if not 0 <= j < QT:
        return None, ()
    total = slots(2 * j + 4) + slots(2 * j + 5)
    n = 2 * (j % 8) + 2
    i = slot + (slots(2 * j + 4) if k % 2 else 0)
    return j, range(n * i // total, n * (i + 1) // total)
QB = 256
PIECES = (("k", 0), ("q", 0), ("v", 0), ("k", 1), ("q", 1), ("k", 2), ("q", 2), ("k", 3), ("q", 3))


def phase_attend(nc, g):
    with ExitStack() as ctx:
        ar = Arena(nc, ctx, "at")
        sb, bank, sem = ar.sb, ar.bank, ar.sem
        raw_k = sb("raw_k", [NOPE + ROPE, SEQ])
        raw_q = sb("raw_q", [NOPE + ROPE, SEQ])
        raw_v = sb("raw_v", [P, QT, VD])
        k_hi, k_lo = sb("k_hi", [96, 2, SEQ], F32R), sb("k_lo", [96, 2, SEQ], F32R)
        q_hi, q_lo = sb("q_hi", [96, 2, SEQ], F32R), sb("q_lo", [96, 2, SEQ], F32R)
        v_hi, v_lo = sb("v_hi", [P, 2, QT, VD], F32R), sb("v_lo", [P, 2, QT, VD], F32R)
        p = sb("p", [P, 2, SEQ])
        pt_hi, pt_lo = sb("pt_hi", [P, 2, QT, QB], F32R), sb("pt_lo", [P, 2, QT, QB], F32R)
        part = sb("part", [P, 2, 4])
        total = sb("total", [P, 2])
        rec = sb("rec", [P, 4])
        rec_row = sb("rec_row", [VD, QB])
        out = sb("out", [VD, 2, QB])
        ident = sb("ident", [P, P])
        neg_max = sb("neg_max", [P, 2, 4])
        neg_all = sb("neg_all", [P, 2])
        bias = sb("bias", [P, 2])
        ps_s = [bank(f"s{i}") for i in range(SBANKS)]
        ps_t = [bank("t0"), bank("t1")]
        ps_o = [bank("o0"), bank("o1")]

        k_in, q_in, v_in = sem("k_in"), sem("q_in"), sem("v_in")
        const_in, kr_in = sem("const_in"), sem("kr_in")
        kr_hi, kr_lo = sem("kr_hi"), sem("kr_lo")
        split_hi, split_lo = sem("split_hi"), sem("split_lo")
        scored = sem("scored")
        masked = sem("masked")
        reduced = sem("reduced")
        max_of = sem("max_of")
        biased = sem("biased")
        expd = sem("expd")
        turned = sem("turned")
        pthi, ptlo = sem("pthi"), sem("ptlo")
        summed = sem("summed")
        totalled, recd = sem("totalled"), sem("recd")
        rowed = sem("rowed")
        normed = sem("normed")
        stored = [sem("stored0"), sem("stored1")]

        def head_piece(h, s):
            return h * len(PIECES) + s + 1

        PAIRS = HEADS // 2
        block = ctx.enter_context(nc.Block())

        def width(t, c):
            return CW if c < NCH[t] - 1 else (t % 4 + 1) * P

        @block.sync
        def _(sp):
            for s in stored:
                sp.sem_inc(s, 16 * 8)

            def load(h):
                sp.dma_start(raw_k[0:NOPE, :], g["k_t"][ds(h * NOPE, NOPE), :]).then_inc(k_in, 16)
                sp.dma_start(raw_q[:, :], g["q_t"][ds(h * 96, 96), 0:SEQ]).then_inc(q_in, 16)
                sp.dma_start(raw_v[:, :, :], g["v"].rearrange("(t p) n -> p t n", p=P)[:, :, ds(h * VD, VD)])\
                  .then_inc(v_in, 16)

            sp.dma_start(raw_k[NOPE:96, :], g["kr_t"][:, 0:SEQ]).then_inc(kr_in, 16)
            load(0)
            sp.dma_start(ident[:, :], g["ident"]).then_inc(const_in, 16)
            sp.wait_ge(split_lo, head_piece(0, 8))
            load(1)

            def head(it, u, more):
                for jj in range(8):
                    j = 8 * u + jj
                    if jj == 6 and more:
                        sp.wait_ge(split_lo, head_piece(2 * it + u + 1, 8))
                        load(2 * it + u + 2)
                    sp.wait_ge(normed, nth(it, 16, j))
                    sp.dma_start(g["mix_t"][ds((2 * it + u) * VD, VD), jj * QB:(jj + 1) * QB],
                                 out[:, j % 2, :]).then_inc(stored[j % 2], 16)
            with sp.Fori(0, PAIRS - 1) as it:
                head(it, 0, True)
                head(it, 1, True)
            head(PAIRS - 1, 0, False)
            head(PAIRS - 1, 1, False)
            for s in stored:
                sp.wait_ge(s, nth(PAIRS - 1, 8, 7) * 16)

        def split_ops(eng, h, u, s, busy=None):
            kind, c = PIECES[s]
            cols = slice(c * CW, (c + 1) * CW)
            if kind == "k":
                return k_hi[0:NOPE, u, cols], k_lo[0:NOPE, u, cols], raw_k[0:NOPE, cols]
            if kind == "q":
                return q_hi[:, u, cols], q_lo[:, u, cols], raw_q[:, cols]
            return v_hi[:, u], v_lo[:, u], raw_v[:, :, :]

        @block.gpsimd
        def _(pool):
            def head(h, u):
                for s in range(len(PIECES)):
                    hi, lo, src = split_ops(pool, h, u, s)
                    pool.wait_ge(split_hi, head_piece(h, s))
                    pool.tensor_tensor(lo, src, f32(hi), ALU.subtract).then_inc(split_lo, 1)
            with pool.Fori(0, PAIRS) as it:
                head(2 * it, 0)
                head(2 * it + 1, 1)

        @block.scalar
        def _(act):
            act.sem_inc(expd, BASE[TILES])
            act.sem_inc(pthi, BASE[TILES])
            act.sem_inc(rowed, 16)
            act.wait_ge(kr_in, 16)
            for u in range(2):
                act.activation(k_hi[NOPE:96, u, :], raw_k[NOPE:96, :], ACT.Copy).then_inc(kr_hi, 1)

            def split(h, u, s):
                hi, _, src = split_ops(act, h, u, s)
                act.wait_ge({"k": k_in, "q": q_in, "v": v_in}[PIECES[s][0]], (h + 1) * 16)
                act.activation(hi, src, ACT.Copy).then_inc(split_hi, 1)

            for s in range(len(PIECES)):
                split(0, 0, s)

            def turn(it, more):
                for k in range(STEPS):
                    e, t = k - 1, k - 2
                    for c in range(4):
                        if 0 <= t < TILES and c < NCH[t]:
                            n, j = BASE[t] + c, t // 2
                            w = width(t, c)
                            act.wait_ge(turned, nth(it, BASE[TILES], n))
                            if c == 0 and t % 2 == 0:
                                act.wait_ge(summed, nth(it, 16, j - 2))
                            act.activation(pt_hi[:, j % 2, 4 * c:4 * c + w // P, t % 2 * P:t % 2 * P + P],
                                           ps_t[n % 2][:, 0:w].rearrange("p (a b) -> p a b", b=P),
                                           ACT.Copy).then_inc(pthi, 1)
                        if 0 <= e < TILES and c < NCH[e]:
                            n = BASE[e] + c
                            w = width(e, c)
                            if c == 0:
                                act.wait_ge(biased, nth(it, TILES, e))
                                act.wait_ge(totalled, nth(it, TILES, e - 2))
                                act.wait_ge(turned, nth(it, BASE[TILES], BASE[e - 1] - 1 if e >= 2 else
                                                        [-1 - NCH[TILES - 1], -1][e]))
                            act.activation(p[:, e % 2, c * CW:c * CW + w], ps_s[n % SBANKS][:, 0:w], ACT.Exp,
                                           bias=bias[:, e % 2:e % 2 + 1], scale=SCALE,
                                           accum_out=part[:, e % 2, c:c + 1]).then_inc(expd, 1)
                        if c == 0 and k % 2 == 0 and k >= 6:
                            j = (k - 6) // 2
                            act.wait_ge(summed, nth(it, 16, j))
                            act.wait_ge(normed, nth(it, 16, j - 1))
                            act.activation(rec_row[:, :], ps_o[j % 2][0:VD, QB:2 * QB], ACT.Copy).then_inc(rowed, 1)
                    i = k % QT
                    if k < TILES and 6 <= i < 6 + len(PIECES) and (k < QT or more):
                        u, s = k // QT, i - 6
                        if s == 0:
                            act.wait_ge(scored, nth(it, BASE[TILES], BASE[QT * u] - 1))
                            act.wait_ge(summed, nth(it, 16, 8 * u - 1))
                        split(2 * it + u + 1, 1 - u, s)

            with act.Fori(0, PAIRS - 1) as it:
                turn(it, True)
            turn(PAIRS - 1, False)

        @block.vector
        def _(dve):
            for s, n in ((masked, TILES), (reduced, BASE[TILES]), (max_of, TILES), (biased, TILES),
                         (ptlo, BASE[TILES]), (totalled, TILES), (recd, TILES), (normed, 16)):
                dve.sem_inc(s, n)
            dve.wait_ge(kr_hi, 2)
            for u in range(2):
                dve.tensor_tensor(k_lo[NOPE:96, u, :], raw_k[NOPE:96, :], f32(k_hi[NOPE:96, u, :]),
                                  ALU.subtract).then_inc(kr_lo, 1)

            def reciprocals(it, t):
                dve.wait_ge(expd, nth(it, BASE[TILES], BASE[t + 1] - 1))
                dve.wait_ge(recd, nth(it, TILES, t - 2))
                dve.tensor_reduce(total[:, t % 2:t % 2 + 1], part[:, t % 2, 0:NCH[t]], AX.X, ALU.add)\
                   .then_inc(totalled, 1)
                dve.wait_ge(totalled, nth(it, TILES, t))
                dve.wait_ge(summed, nth(it, 16, t // 2 - 2))
                dve.reciprocal(rec[:, t % 4:t % 4 + 1], total[:, t % 2:t % 2 + 1]).then_inc(recd, 1)

            def finish(it, j):
                dve.wait_ge(rowed, nth(it, 16, j))
                dve.wait_ge(stored[j % 2], nth(it, 8, j // 2 - 1) * 16)
                dve.tensor_tensor(out[:, j % 2, :], ps_o[j % 2][0:VD, 0:QB], rec_row[:, :], ALU.mult)\
                   .then_inc(normed, 1)

            def turn(it):
                for k in range(STEPS):
                    t = k - 2
                    for c in range(4):
                        if 0 <= t < TILES and c < NCH[t]:
                            n, j, w = BASE[t] + c, t // 2, width(t, c)
                            dve.wait_ge(pthi, nth(it, BASE[TILES], n))
                            at = (slice(None), j % 2, slice(4 * c, 4 * c + w // P), slice(t % 2 * P, t % 2 * P + P))
                            dve.tensor_tensor(pt_lo[at], ps_t[n % 2][:, 0:w].rearrange("p (a b) -> p a b", b=P),
                                              f32(pt_hi[at]), ALU.subtract).then_inc(ptlo, 1)
                        if 0 <= t < TILES and c == 0:
                            reciprocals(it, t)
                        if k < TILES and c < NCH[k]:
                            n, w = BASE[k] + c, width(k, c)
                            s = ps_s[n % SBANKS]
                            dve.wait_ge(scored, nth(it, BASE[TILES], n))
                            if c == NCH[k] - 1:
                                dve.memset(s[0:64, w - 64:w], NEG).then_inc(masked, 1)
                                dve.wait_ge(masked, nth(it, TILES, k))
                            if c == 0:
                                dve.wait_ge(max_of, nth(it, TILES, k - 2))
                            dve.tensor_reduce(neg_max[:, k % 2, c:c + 1], s[:, 0:w], AX.X, ALU.max, negate=True)\
                               .then_inc(reduced, 1)
                        if k < TILES and c == NCH[k] - 1:
                            dve.wait_ge(reduced, nth(it, BASE[TILES], BASE[k] + c))
                            dve.wait_ge(biased, nth(it, TILES, k - 1))
                            dve.tensor_reduce(neg_all[:, k % 2:k % 2 + 1], neg_max[:, k % 2, 0:NCH[k]], AX.X, ALU.min)\
                               .then_inc(max_of, 1)
                            dve.wait_ge(max_of, nth(it, TILES, k))
                            dve.wait_ge(expd, nth(it, BASE[TILES], BASE[k - 1] - 1 if k >= 2 else
                                                  [-1 - NCH[TILES - 1], -1][k]))
                            dve.tensor_scalar(bias[:, k % 2:k % 2 + 1], neg_all[:, k % 2:k % 2 + 1], SCALE, None,
                                              ALU.mult).then_inc(biased, 1)
                        if c == 0 and k % 2 == 0 and k >= 6:
                            finish(it, (k - 6) // 2)
            with dve.Fori(0, PAIRS) as it:
                turn(it)

        @block.tensor
        def _(pe):
            pe.sem_inc(scored, BASE[TILES])
            pe.sem_inc(turned, BASE[TILES])
            pe.sem_inc(summed, 16)
            pe.wait_ge(const_in, 16)
            pe.wait_ge(kr_lo, 2)

            def scores(it, t, c):
                u, i = t // QT, t % QT
                n, w = BASE[t] + c, width(t, c)
                if i % 4 == 0:
                    s = max(PIECES.index(("k", c)), PIECES.index(("q", i // 4)))
                    pe.wait_ge(split_lo, head_piece(2 * it + u, s))
                pe.wait_ge(expd, nth(it, BASE[TILES], n - SBANKS))
                rows, cols = slice(i * P, (i + 1) * P), slice(c * CW, c * CW + w)
                product(pe, ps_s[n % SBANKS][:, 0:w], (q_hi[:, u, rows], q_lo[:, u, rows]),
                        (k_hi[:, u, cols], k_lo[:, u, cols]), True, True).then_inc(scored, 1)

            def transposes(it, t, c):
                n, w = BASE[t] + c, width(t, c)
                pe.wait_ge(expd, nth(it, BASE[TILES], n))
                pe.wait_ge(ptlo, nth(it, BASE[TILES], n - 2))
                for b in range(w // P):
                    mm = pe.transpose(ps_t[n % 2][:, b * P:(b + 1) * P],
                                      p[:, t % 2, c * CW + b * P:c * CW + (b + 1) * P], ident[:, :])
                mm.then_inc(turned, 1)

            def values(it, j, key_tiles):
                u, last = j // 8, 2 * (j % 8) + 1
                if 0 in key_tiles:
                    pe.wait_ge(ptlo, nth(it, BASE[TILES], BASE[2 * j + 2] - 1))
                    pe.wait_ge(split_lo, head_piece(2 * it + u, 2))
                    pe.wait_ge(normed, nth(it, 16, j - 2))
                for kt in key_tiles:
                    cols = slice(P, QB) if kt == last else slice(0, QB)
                    mm = product(pe, ps_o[j % 2][0:VD, cols], (v_hi[:, u, kt, :], v_lo[:, u, kt, :]),
                                 (pt_hi[:, j % 2, kt, cols], pt_lo[:, j % 2, kt, cols]), kt == 0, kt == last,
                                 skip_group_check=True)
                if last in key_tiles:
                    for i in range(2):
                        pe.wait_ge(recd, nth(it, TILES, 2 * j + i))
                        t = (2 * j + i) % 4
                        mm = pe.matmul(ps_o[j % 2][0:VD, QB + i * P:QB + (i + 1) * P],
                                       rec[:, t:t + 1].to_broadcast([P, VD]), ident[:, :], start=False, stop=i == 1,
                                       skip_group_check=True)
                    mm.then_inc(summed, 1)

            with pe.Fori(0, PAIRS) as it:
                for k in range(STEPS):
                    for c in range(slots(k)):
                        if 2 <= k < TILES + 2 and c < NCH[k - 2]:
                            transposes(it, k - 2, c)
                        j, key_tiles = value_parts(k, c)
                        if key_tiles:
                            values(it, j, key_tiles)
                        if k < TILES and c < NCH[k]:
                            scores(it, k, c)



KEYS = PAST + NEW
KT = PAST // P


def phase_sample(nc, g):
    assert KEYS // 64 == PAST // 64
    with ExitStack() as ctx:
        ar = Arena(nc, ctx, "sa")
        sb, bank, sem = ar.sb, ar.bank, ar.sem
        uk_raw, uv_raw = sb("uk_raw", [NOPE, HEADS, LORA]), sb("uv_raw", [P, 2, HEADS, VD])
        uk_hi, uk_lo = sb("uk_hi", [NOPE, HEADS, LORA], F32R), sb("uk_lo", [NOPE, HEADS, LORA], F32R)
        uv_hi, uv_lo = sb("uv_hi", [P, 2, HEADS, VD], F32R), sb("uv_lo", [P, 2, HEADS, VD], F32R)
        qn_raw = sb("qn_raw", [NOPE, HEADS, SAMPLE])
        qn_hi, qn_lo = sb("qn_hi", [NOPE, HEADS, SAMPLE], F32R), sb("qn_lo", [NOPE, HEADS, SAMPLE], F32R)
        qr_raw = sb("qr_raw", [ROPE, HEADS, SAMPLE])
        q_lat = sb("q_lat", [P, 2, HEADS, SAMPLE])
        ident = sb("ident", [P, P])
        k_raw, v_raw, r_raw = sb("k_raw", [P, 2, 2, KEYS]), sb("v_raw", [P, 2, KT, LORA]), sb("r_raw", [ROPE, 2, KEYS])
        k_hi, k_lo = sb("k_hi", [P, 2, 2, KEYS], F32R), sb("k_lo", [P, 2, 2, KEYS], F32R)
        v_hi, v_lo = sb("v_hi", [P, 2, KT, LORA], F32R), sb("v_lo", [P, 2, KT, LORA], F32R)
        r_hi, r_lo = sb("r_hi", [ROPE, 2, KEYS], F32R), sb("r_lo", [ROPE, 2, KEYS], F32R)
        q_hi, q_lo = sb("q_hi", [P, 2, 2, HEADS, NEW], F32R), sb("q_lo", [P, 2, 2, HEADS, NEW], F32R)
        p_hi, p_lo = sb("p_hi", [ROPE, 2, HEADS, NEW], F32R), sb("p_lo", [ROPE, 2, HEADS, NEW], F32R)
        n_hi, n_lo = sb("n_hi", [NEW, 2, LORA], F32R), sb("n_lo", [NEW, 2, LORA], F32R)
        prob = sb("prob", [P, 2, KEYS])
        pt_hi, pt_lo = sb("pt_hi", [P, 2, KT, P], F32R), sb("pt_lo", [P, 2, KT, P], F32R)
        pn_hi, pn_lo = sb("pn_hi", [NEW, 2, P], F32R), sb("pn_lo", [NEW, 2, P], F32R)
        l_hi, l_lo = sb("l_hi", [P, 2, HEADS, SAMPLE], F32R), sb("l_lo", [P, 2, HEADS, SAMPLE], F32R)
        out = sb("out", [VD, HEADS, SAMPLE])
        stat = sb("stat", [P, 2, 8])
        ps_q, ps_new, ps_s, ps_sn, ps_t, ps_tn, ps_l, ps_o = (bank(n) for n in
                                                              ("q", "new", "s", "sn", "t", "tn", "l", "o"))

        const_in, met = sem("const_in"), sem("met")
        row_in = [sem("row_in0"), sem("row_in1")]
        w_hi, w_lo = sem("w_hi"), sem("w_lo")
        lat_q, lat_copied = sem("lat_q"), sem("lat_copied")
        split_hi, split_lo = sem("split_hi"), sem("split_lo")
        vhi, vlo = sem("vhi"), sem("vlo")
        new_turned, nhi, nlo = sem("new_turned"), sem("nhi"), sem("nlo")
        scored, maxed, least, biased = sem("scored"), sem("maxed"), sem("least"), sem("biased")
        expd, summed, recd, normed = sem("expd"), sem("summed"), sem("recd"), sem("normed")
        turned, thi, tlo = sem("turned"), sem("thi"), sem("tlo")
        mixed, lhi, llo = sem("mixed"), sem("lhi"), sem("llo")
        valued, copied, stored = sem("valued"), sem("copied"), sem("stored")
        LOADS = 6

        block = ctx.enter_context(nc.Block())

        @block.sync
        def _(sp):
            for dst, src in ((uk_raw[:, :, :], g["w_uk_p"]), (uv_raw[:, :, :, :], g["w_uv_p"]),
                             (ident[:, :], g["ident"])):
                sp.dma_start(dst, src).then_inc(const_in, 16)
            q = g["q_t"].rearrange("(h r) t -> r h t", r=NOPE + ROPE)
            sp.dma_start(qn_raw[:, :, :], q[0:NOPE, :, SEQ:TOK]).then_inc(const_in, 16)
            sp.dma_start(qr_raw[:, :, :], q[NOPE:NOPE + ROPE, :, SEQ:TOK]).then_inc(const_in, 16)

            def load(row, u):
                new = ds(SEQ + row * NEW, NEW)
                s = row_in[u]
                sp.dma_start(k_raw[:, u, :, 0:PAST], g["ckv_t"].rearrange("b p a t -> p b a t")[:, ds(row, 1)])\
                  .then_inc(s, 16)
                sp.dma_start(k_raw[:, u, :, PAST:KEYS], g["c_t"].rearrange("(a p) t -> p a t", p=P)[:, :, new])\
                  .then_inc(s, 16)
                sp.dma_start(r_raw[:, u, 0:PAST], g["krope_t"].rearrange("b p t -> p b t")[:, ds(row, 1)])\
                  .then_inc(s, 16)
                sp.dma_start(r_raw[:, u, PAST:KEYS], g["kr_t"][:, new]).then_inc(s, 16)
                for half in range(2):
                    sp.dma_start(v_raw[:, u, 2 * half:2 * half + 2, :],
                                 g["ckv"].rearrange("b p a l -> p b a l")[:, ds(row, 1), 2 * half:2 * half + 2])\
                      .then_inc(s, 16)

            def reload(row, u):
                sp.wait_ge(split_lo, at(row - 2, 4, 3))
                take(sp, met)
                sp.wait_ge(vlo, at(row - 2, 1, 0))
                sp.wait_ge(new_turned, at(row - 2, 1, 0))
                take(sp, met)
                load(row, u)

            load(0, 0)
            load(1, 1)
            reload(2, 0)
            with sp.Fori(0, ROWS // 2 - 2) as it:
                for u in range(2):
                    reload(2 * it + u + 3, 1 - u)
            reload(ROWS - 1, 1)
            sp.wait_ge(copied, 2)
            sp.dma_start(g["mix_t"][0:MLA, SEQ:TOK].rearrange("(h v) t -> v h t", v=VD), out[:, :, :])\
              .then_inc(stored, 16)
            sp.wait_ge(stored, 16)

        def splits(row, u):
            new = ds(row * NEW, NEW)
            return ((k_hi[:, u], k_lo[:, u], k_raw[:, u]), (r_hi[:, u], r_lo[:, u], r_raw[:, u]),
                    (q_hi[:, u], q_lo[:, u], q_lat[:, :, :, new]), (p_hi[:, u], p_lo[:, u], qr_raw[:, :, new]))

        @block.gpsimd
        def _(pool):
            pool.sem_inc(split_lo, 8)
            for i, (lo, raw, hi) in enumerate(((uk_lo, uk_raw, uk_hi), (qn_lo, qn_raw, qn_hi), (uv_lo, uv_raw, uv_hi))):
                pool.wait_ge(w_hi, i + 1)
                pool.tensor_tensor(lo[:], raw[:], f32(hi[:]), ALU.subtract).then_inc(w_lo, 1)
            with pool.Fori(0, ROWS // 2) as it:
                for u in range(2):
                    for k, (hi, lo, raw) in enumerate(splits(2 * it + u, u)):
                        pool.wait_ge(split_hi, at(2 * it + u, 4, k))
                        pool.tensor_tensor(lo, raw, f32(hi), ALU.subtract).then_inc(split_lo, 1)

        @block.scalar
        def _(act):
            for s, n in ((split_hi, 4), (vhi, 1), (nhi, 1), (expd, 2), (thi, 2), (lhi, 1)):
                act.sem_inc(s, 2 * n)
            act.wait_ge(const_in, 80)
            for hi, raw in ((uk_hi, uk_raw), (qn_hi, qn_raw), (uv_hi, uv_raw)):
                act.activation(hi[:], raw[:], ACT.Copy).then_inc(w_hi, 1)
            for n in range(4):
                act.wait_ge(lat_q, n + 1)
                act.activation(q_lat[:, n // 2, 4 * (n % 2):4 * (n % 2) + 4, :],
                               (ps_q, ps_s, ps_t, ps_l)[n][:, :].rearrange("p (h t) -> p h t", t=SAMPLE), ACT.Copy)\
                   .then_inc(lat_copied, 1)
            act.wait_ge(lat_copied, 4)

            def keys(row, u, fill):
                act.wait_ge(row_in[u], fill * 16 * LOADS)
                act.wait_ge(scored, at(row - 2, 1, 0))
                for hi, _, raw in splits(row, u):
                    act.activation(hi, raw, ACT.Copy).then_inc(split_hi, 1)

            def values(row, u):
                act.wait_ge(mixed, at(row - 2, 1, 0))
                act.activation(v_hi[:, u], v_raw[:, u], ACT.Copy).then_inc(vhi, 1)
                act.wait_ge(new_turned, at(row, 1, 0))
                act.activation(n_hi[:, u, :], ps_new[0:NEW, 0:LORA], ACT.Copy).then_inc(nhi, 1)

            def exps(row, u):
                act.wait_ge(biased, at(row, 1, 0))
                act.wait_ge(turned, at(row - 2, 1, 0))
                for i, (src, a, b) in enumerate(((ps_s, 0, PAST), (ps_sn, PAST, KEYS))):
                    act.activation(prob[:, u, a:b], src[:, 0:b - a], ACT.Exp, bias=stat[:, u, 3:4], scale=SCALE)\
                       .then_inc(expd, 1)

            def step(row, u, fill, ahead=2):
                if ahead:
                    values(row + 1, 1 - u)
                act.wait_ge(turned, at(row, 1, 0))
                act.activation(pt_hi[:, u], ps_t[:, :].rearrange("p (a b) -> p a b", b=P), ACT.Copy).then_inc(thi, 1)
                act.activation(pn_hi[:, u, :], ps_tn[0:NEW, 0:P], ACT.Copy).then_inc(thi, 1)
                if ahead:
                    exps(row + 1, 1 - u)
                if ahead == 2:
                    keys(row + 2, u, fill + 1)
                act.wait_ge(mixed, at(row, 1, 0))
                take(act, met)
                act.activation(l_hi[:, :, :, ds(row * NEW, NEW)],
                               ps_l[:, 0:2 * P].rearrange("p (a h t) -> p a h t", a=2, t=NEW), ACT.Copy).then_inc(lhi, 1)

            keys(0, 0, 1)
            values(0, 0)
            keys(1, 1, 1)
            exps(0, 0)
            with act.Fori(0, ROWS // 2 - 1) as it:
                step(2 * it, 0, it + 1)
                step(2 * it + 1, 1, it + 1)
            step(ROWS - 2, 0, ROWS // 2, ahead=1)
            step(ROWS - 1, 1, ROWS // 2, ahead=0)
            for i in range(2):
                act.wait_ge(valued, i + 1)
                act.activation(out[:, 4 * i:4 * i + 4, :], (ps_o, ps_new)[i][0:VD, :].rearrange("p (h t) -> p h t", t=SAMPLE),
                               ACT.Copy).then_inc(copied, 1)

        @block.vector
        def _(dve):
            for s, n in ((vlo, 1), (nlo, 1), (maxed, 2), (least, 1), (biased, 1), (summed, 1), (recd, 1),
                         (normed, 1), (tlo, 2), (llo, 1)):
                dve.sem_inc(s, 2 * n)

            def prepare(row, u):
                dve.wait_ge(vhi, at(row, 1, 0))
                dve.tensor_tensor(v_lo[:, u], v_raw[:, u], f32(v_hi[:, u]), ALU.subtract).then_inc(vlo, 1)
                dve.wait_ge(nhi, at(row, 1, 0))
                dve.tensor_tensor(n_lo[:, u, :], ps_new[0:NEW, 0:LORA], f32(n_hi[:, u, :]), ALU.subtract)\
                   .then_inc(nlo, 1)

            def maxima(row, u):
                dve.wait_ge(scored, at(row, 1, 0))
                dve.wait_ge(least, at(row - 2, 1, 0))
                for i, (src, w) in enumerate(((ps_s, PAST), (ps_sn, NEW))):
                    dve.tensor_reduce(stat[:, u, i:i + 1], src[:, 0:w], AX.X, ALU.max, negate=True).then_inc(maxed, 1)
                dve.wait_ge(maxed, at(row, 2, 1))
                dve.wait_ge(biased, at(row - 2, 1, 0))
                dve.tensor_reduce(stat[:, u, 2:3], stat[:, u, 0:2], AX.X, ALU.min).then_inc(least, 1)
                dve.wait_ge(least, at(row, 1, 0))
                dve.wait_ge(expd, at(row - 2, 2, 1))
                dve.tensor_scalar(stat[:, u, 3:4], stat[:, u, 2:3], SCALE, None, ALU.mult).then_inc(biased, 1)

            def normalise(row, u):
                dve.wait_ge(expd, at(row, 2, 1))
                dve.wait_ge(recd, at(row - 2, 1, 0))
                dve.tensor_reduce(stat[:, u, 4:5], prob[:, u, :], AX.X, ALU.add).then_inc(summed, 1)
                dve.wait_ge(summed, at(row, 1, 0))
                dve.wait_ge(normed, at(row - 2, 1, 0))
                dve.reciprocal(stat[:, u, 5:6], stat[:, u, 4:5]).then_inc(recd, 1)
                dve.wait_ge(recd, at(row, 1, 0))
                dve.tensor_scalar(prob[:, u, :], prob[:, u, :], stat[:, u, 5:6], None, ALU.mult).then_inc(normed, 1)

            def lows(row, u):
                dve.wait_ge(thi, at(row, 2, 1))
                dve.tensor_tensor(pt_lo[:, u], ps_t[:, :].rearrange("p (a b) -> p a b", b=P), f32(pt_hi[:, u]),
                                  ALU.subtract).then_inc(tlo, 1)
                dve.tensor_tensor(pn_lo[:, u, :], ps_tn[0:NEW, 0:P], f32(pn_hi[:, u, :]), ALU.subtract)\
                   .then_inc(tlo, 1)

            def latents(row, u):
                dve.wait_ge(lhi, at(row, 1, 0))
                new = ds(row * NEW, NEW)
                dve.tensor_tensor(l_lo[:, :, :, new], ps_l[:, 0:2 * P].rearrange("p (a h t) -> p a h t", a=2, t=NEW),
                                  f32(l_hi[:, :, :, new]), ALU.subtract).then_inc(llo, 1)

            def step(row, u, ahead=True):
                if ahead:
                    prepare(row + 1, 1 - u)
                lows(row, u)
                if ahead:
                    maxima(row + 1, 1 - u)
                latents(row, u)
                if ahead:
                    normalise(row + 1, 1 - u)

            prepare(0, 0)
            maxima(0, 0)
            normalise(0, 0)
            with dve.Fori(0, ROWS // 2 - 1) as it:
                step(2 * it, 0)
                step(2 * it + 1, 1)
            step(ROWS - 2, 0)
            step(ROWS - 1, 1, ahead=False)

        @block.tensor
        def _(pe):
            for s in (new_turned, scored, turned, mixed):
                pe.sem_inc(s, 2)
            pe.wait_ge(w_lo, 2)
            for n in range(4):
                for hh in range(4):
                    h, cols = 4 * (n % 2) + hh, slice(n // 2 * P, n // 2 * P + P)
                    mm = product(pe, (ps_q, ps_s, ps_t, ps_l)[n][:, hh * P:(hh + 1) * P],
                                 (uk_hi[:, h, cols], uk_lo[:, h, cols]), (qn_hi[:, h, :], qn_lo[:, h, :]),
                                 hh == 0, hh == 3, skip_group_check=True)
                mm.then_inc(lat_q, 1)
            pe.wait_ge(lat_copied, 4)
            pe.wait_ge(w_lo, 3)

            def new_tokens(row, u, fill):
                pe.wait_ge(row_in[u], fill * 16 * LOADS)
                pe.wait_ge(nlo, at(row - 1, 1, 0))
                for a in range(2):
                    mm = pe.transpose(ps_new[0:NEW, a * P:(a + 1) * P], k_raw[:, u, a, PAST:KEYS], ident[:, :])
                mm.then_inc(new_turned, 1)

            def scores(row, u):
                pe.wait_ge(split_lo, at(row, 4, 3))
                pe.wait_ge(expd, at(row - 1, 2, 1))
                for dst, a, b in ((ps_s, 0, PAST), (ps_sn, PAST, KEYS)):
                    for lt in range(2):
                        product(pe, dst[:, 0:b - a], (q_hi[:, u, lt], q_lo[:, u, lt]),
                                (k_hi[:, u, lt, a:b], k_lo[:, u, lt, a:b]), lt == 0, False)
                    mm = product(pe, dst[:, 0:b - a], (p_hi[:, u], p_lo[:, u]), (r_hi[:, u, a:b], r_lo[:, u, a:b]),
                                 False, True)
                mm.then_inc(scored, 1)

            def transposes(row, u):
                pe.wait_ge(normed, at(row, 1, 0))
                pe.wait_ge(tlo, at(row - 1, 2, 1))
                for kt in range(KT):
                    pe.transpose(ps_t[:, kt * P:(kt + 1) * P], prob[:, u, kt * P:(kt + 1) * P], ident[:, :])
                pe.transpose(ps_tn[0:NEW, 0:P], prob[:, u, PAST:KEYS], ident[:, :]).then_inc(turned, 1)

            def finish(row, u):
                pe.wait_ge(tlo, at(row, 2, 1))
                pe.wait_ge(vlo, at(row, 1, 0))
                pe.wait_ge(nlo, at(row, 1, 0))
                pe.wait_ge(llo, at(row - 1, 1, 0))
                for lt in range(2):
                    cols = slice(lt * P, (lt + 1) * P)
                    for kt in range(KT):
                        product(pe, ps_l[:, cols], (v_hi[:, u, kt, cols], v_lo[:, u, kt, cols]),
                                (pt_hi[:, u, kt, :], pt_lo[:, u, kt, :]), lt == 0 and kt == 0, False,
                                skip_group_check=True)
                    mm = product(pe, ps_l[:, cols], (n_hi[:, u, cols], n_lo[:, u, cols]),
                                 (pn_hi[:, u, :], pn_lo[:, u, :]), False, lt == 1, skip_group_check=True)
                mm.then_inc(mixed, 1)

            new_tokens(0, 0, 1)
            scores(0, 0)
            with pe.Fori(0, ROWS // 2 - 1) as it:
                for u in range(2):
                    row = 2 * it + u
                    new_tokens(row + 1, 1 - u, it + 1 + u)
                    transposes(row, u)
                    scores(row + 1, 1 - u)
                    finish(row, u)
            new_tokens(ROWS - 1, 1, ROWS // 2)
            transposes(ROWS - 2, 0)
            scores(ROWS - 1, 1)
            finish(ROWS - 2, 0)
            transposes(ROWS - 1, 1)
            finish(ROWS - 1, 1)
            pe.wait_ge(llo, at(ROWS - 1, 1, 0))
            pe.wait_ge(nlo, at(ROWS - 1, 1, 0))
            for i in range(2):
                for hh in range(4):
                    h = 4 * i + hh
                    for lt in range(2):
                        mm = product(pe, (ps_o, ps_new)[i][0:VD, hh * P:(hh + 1) * P],
                                     (uv_hi[:, lt, h, :], uv_lo[:, lt, h, :]), (l_hi[:, lt, h, :], l_lo[:, lt, h, :]),
                                     hh == 0 and lt == 0, hh == 3 and lt == 1, skip_group_check=True)
                mm.then_inc(valued, 1)


TT = TOK // P
LN_EPS = 1e-5


def phase_mix(nc, g):
    with ExitStack() as ctx:
        ar = Arena(nc, ctx, "mx")
        sb, bank, sem = ar.sb, ar.bank, ar.sem
        wo_hi, wo_lo = sb("wo_hi", [P, KD, D], F32R), sb("wo_lo", [P, KD, D], F32R)
        wg_hi, wg_lo = sb("wg_hi", [P, KD, D], F32R), sb("wg_lo", [P, KD, D], F32R)
        we_hi, we_lo = sb("we_hi", [P, 2, D], F32R), sb("we_lo", [P, 2, D], F32R)
        work = sb("work", [P, 4, D])
        m_raw, m_hi, m_lo = sb("m_raw", [P, 2, KD, P]), sb("m_hi", [P, KD, P], F32R), sb("m_lo", [P, KD, P], F32R)
        e_raw, e_hi, e_lo = sb("e_raw", [P, 2, 2, P]), sb("e_hi", [P, 2, 2, P], F32R), sb("e_lo", [P, 2, 2, P], F32R)
        x_raw = sb("x_raw", [P, 2, D])
        t_hi, t_lo = sb("t_hi", [P, KD, P], F32R), sb("t_lo", [P, KD, P], F32R)
        ln_g, ln_b = sb("ln_g", [P, D]), sb("ln_b", [P, D])
        ident = sb("ident", [P, P])
        stats, mv = sb("stats", [P, 2, 12]), sb("mv", [P, 2, 2])
        var_eps, rstd, power = sb("var_eps", [P, 2]), sb("rstd", [P, 2]), sb("power", [P, 1])
        x1_t, gate = work[:, 2, :], work[:, 3, :]
        ps_m = [bank("m0"), bank("m1")]
        ps_t = [bank("t0"), bank("t1")]
        ps_g = [bank("g0"), bank("g1")]
        ps_e = [bank("e0"), bank("e1")]

        const_in, met = sem("const_in"), sem("met")
        w_in = [sem(f"w_in{i}") for i in range(4)]
        whi, wlo_pool, wlo_dve = sem("whi"), sem("wlo_pool"), sem("wlo_dve")
        m_in, x_in = [sem("m_in0"), sem("m_in1")], [sem("x_in0"), sem("x_in1")]
        split_hi, split_lo = sem("split_hi"), sem("split_lo")
        mixed, emb, turned, gated = sem("mixed"), sem("emb"), sem("turned"), sem("gated")
        resid, stat, aggr, eps = sem("resid"), sem("stat"), sem("aggr"), sem("eps")
        rs, scaled = sem("rs"), sem("scaled")
        centred, shifted = sem("centred"), sem("shifted")
        thi, tlo, tcopy = sem("thi"), sem("tlo"), sem("tcopy")
        sig, prod, summed = sem("sig"), sem("prod"), sem("summed")
        powered = sem("powered")
        st_x, st_y = sem("st_x"), sem("st_y")
        W = [(wo_hi[:, k, :], wo_lo[:, k, :]) for k in range(KD)] + [(we_hi[:, k, :], we_lo[:, k, :]) for k in range(2)] \
            + [(wg_hi[:, k, :], wg_lo[:, k, :]) for k in range(KD)]
        H = (slice(0, 512), slice(512, 1024))

        def wait_piece(eng, n):
            eng.wait_ge(wlo_pool, n // 2 + 1)
            if n > 0:
                eng.wait_ge(wlo_dve, (n + 1) // 2)

        block = ctx.enter_context(nc.Block())

        @block.sync
        def _(sp):
            sp.sem_inc(st_x, 16)
            sp.sem_inc(st_y, 16)

            def load_w(n):
                if n >= 4:
                    sp.wait_ge(wlo_dve if n % 2 else wlo_pool, (n - 4) // 2 + 1)
                sp.dma_start(work[:, n % 4, :], g["w_mix_p"][n]).then_inc(w_in[n % 4], 16)

            def load_m(t, u):
                sp.dma_start(m_raw[:, u], g["mix_t"].rearrange("(k p) t -> p k t", p=P)[:, :, ds(t * P, P)])\
                  .then_inc(m_in[u], 16)
                sp.dma_start(e_raw[:, u], g["pe_t"].rearrange("(k p) t -> p k t", p=P)[:, :, ds(t * P, P)])\
                  .then_inc(m_in[u], 16)

            def load_x(t, u):
                sp.dma_start(x_raw[:, u, :], g["x"][ds(t * P, P), :]).then_inc(x_in[u], 16)

            def store(t):
                sp.wait_ge(tcopy, at(t, 2, 1))
                take(sp, met)
                sp.dma_start(g["x1_t"].rearrange("(k p) t -> p k t", p=P)[:, :, ds(t * P, P)],
                             x1_t.rearrange("p (k t) -> p k t", t=P)).then_inc(st_x, 16)
                sp.wait_ge(summed, at(t, 1, 0))
                sp.dma_start(g["y0"][ds(t * P, P), :], gate).then_inc(st_y, 16)

            for n in range(KD):
                load_w(n)
                if n == 3:
                    load_m(0, 0)
            sp.dma_start(ln_g[:, :], g["ln1_g"]).then_inc(const_in, 16)
            sp.dma_start(ln_b[:, :], g["ln1_b"]).then_inc(const_in, 16)
            sp.dma_start(ident[:, :], g["ident"]).then_inc(const_in, 16)
            load_x(0, 0)
            load_m(1, 1)
            for n in range(KD, len(W)):
                load_w(n)
            sp.wait_ge(split_lo, at(0, 2, 1))
            load_m(2, 0)

            def step(t, u, m, x=True):
                if x:
                    sp.wait_ge(resid, at(t - 1, 2, 1))
                    load_x(t + 1, 1 - u)
                if m:
                    sp.wait_ge(split_lo, at(t + 1, 2, 1))
                    load_m(t + 3, 1 - u)
                store(t)
            with sp.Fori(0, 7) as it:
                step(2 * it, 0, True)
                step(2 * it + 1, 1, True)
            step(TT - 3, 0, False)
            step(TT - 2, 1, False)
            step(TT - 1, 0, False, False)
            sp.wait_ge(st_x, (TT + 1) * 16)
            sp.wait_ge(st_y, (TT + 1) * 16)

        @block.gpsimd
        def _(pool):
            for s, n in ((split_lo, 2), (rs, 1), (scaled, 1)):
                pool.sem_inc(s, 2 * n)

            def weight(n):
                hi, lo = W[n]
                pool.wait_ge(whi, n + 1)
                pool.tensor_tensor(lo, work[:, n % 4, :], f32(hi), ALU.subtract).then_inc(wlo_pool, 1)

            def split(t, u):
                for i, (lo, raw, hi) in enumerate(((m_lo[:], m_raw, m_hi[:]), (e_lo[:, u], e_raw, e_hi[:, u]))):
                    pool.wait_ge(split_hi, at(t, 2, i))
                    pool.tensor_tensor(lo, raw[:, u], f32(hi), ALU.subtract).then_inc(split_lo, 1)

            def normalise(t, u, following=None):
                pool.wait_ge(eps, at(t, 1, 0))
                pool.wait_ge(centred, at(t - 2, 1, 0))
                pool.tensor_tensor(rstd[:, u:u + 1], var_eps[:, u:u + 1], power[:, :], ALU.pow).then_inc(rs, 1)
                if following is not None:
                    split(*following)
                pool.wait_ge(centred, at(t, 1, 0))
                pool.tensor_tensor(work[:, u, :], work[:, u, :], ln_g[:, :], ALU.mult).then_inc(scaled, 1)

            pool.memset(power[:, :], -0.5).then_inc(powered, 1)
            for n in range(0, KD, 2):
                weight(n)
            split(0, 0)
            for n in range(KD, len(W), 2):
                weight(n)
            pool.wait_ge(const_in, 48)
            pool.wait_ge(powered, 1)
            split(1, 1)
            normalise(0, 0)
            with pool.Fori(0, 7) as it:
                normalise(2 * it + 1, 1, (2 * it + 2, 0))
                normalise(2 * it + 2, 0, (2 * it + 3, 1))
            normalise(TT - 2, 1, (TT - 1, 0))
            normalise(TT - 1, 0)

        @block.scalar
        def _(act):
            for s, n in ((split_hi, 2), (thi, 2), (tcopy, 2), (sig, 2)):
                act.sem_inc(s, 2 * n)

            def weight(n):
                act.wait_ge(w_in[n % 4], 16 * (n // 4 + 1))
                act.activation(W[n][0], work[:, n % 4, :], ACT.Copy).then_inc(whi, 1)

            def split(t, u, fill):
                act.wait_ge(m_in[u], fill * 32)
                act.wait_ge(mixed, at(t - 1, 1, 0))
                act.activation(m_hi[:], m_raw[:, u], ACT.Copy).then_inc(split_hi, 1)
                act.wait_ge(emb, at(t - 2, 1, 0))
                act.activation(e_hi[:, u], e_raw[:, u], ACT.Copy).then_inc(split_hi, 1)

            def step(t, u, fill=None):
                act.wait_ge(gated, at(t - 1, 1, 0))
                act.wait_ge(tlo, at(t - 1, 2, 1))
                act.wait_ge(st_x, (t + 1) * 16)
                for i in range(2):
                    act.wait_ge(turned, at(t, 2, i))
                    act.activation(x1_t[:, H[i]], ps_t[i][:, :], ACT.Copy).then_inc(tcopy, 1)
                    act.activation(t_hi[:, 4 * i:4 * i + 4, :], ps_t[i][:, :].rearrange("p (k t) -> p k t", t=P),
                                   ACT.Copy).then_inc(thi, 1)
                if fill is not None:
                    split(t + 2, u, fill)
                act.wait_ge(gated, at(t, 1, 0))
                act.wait_ge(st_y, (t + 1) * 16)
                for i in range(2):
                    act.activation(gate[:, H[i]], ps_g[i][:, :], ACT.Sigmoid).then_inc(sig, 1)

            for n in range(KD):
                weight(n)
            split(0, 0, 1)
            for n in range(KD, len(W)):
                weight(n)
            act.wait_ge(wlo_pool, len(W) // 2)
            act.wait_ge(wlo_dve, len(W) // 2)
            split(1, 1, 1)
            with act.Fori(0, 7) as it:
                step(2 * it, 0, it + 2)
                step(2 * it + 1, 1, it + 2)
            step(TT - 3, 0, TT // 2 + 1)
            step(TT - 2, 1)
            step(TT - 1, 0)

        @block.vector
        def _(dve):
            for s, n in ((resid, 2), (stat, 2), (aggr, 1), (eps, 1), (centred, 1), (shifted, 1), (tlo, 2), (prod, 2),
                         (summed, 1)):
                dve.sem_inc(s, 2 * n)

            def weight(n):
                hi, lo = W[n]
                dve.wait_ge(whi, n + 1)
                dve.tensor_tensor(lo, work[:, n % 4, :], f32(hi), ALU.subtract).then_inc(wlo_dve, 1)

            def statistics(t, u, fill):
                dve.wait_ge(mixed, at(t, 1, 0))
                dve.wait_ge(x_in[u], fill * 16)
                dve.wait_ge(summed, at(t - 2, 1, 0))
                for i in range(2):
                    dve.scalar_tensor_tensor(work[:, u, H[i]], x_raw[:, u, H[i]], ALPHA, ps_m[i][:, :], ALU.mult,
                                             ALU.add).then_inc(resid, 1)
                for i in range(2):
                    dve.wait_ge(resid, at(t, 2, i))
                    dve.bn_stats(stats[:, u, 6 * i:6 * i + 6], work[:, u, H[i]]).then_inc(stat, 1)
                dve.wait_ge(stat, at(t, 2, 1))
                take(dve, met)
                dve.bn_aggr(mv[:, u, :], stats[:, u, :]).then_inc(aggr, 1)
                dve.wait_ge(aggr, at(t, 1, 0))
                dve.tensor_scalar(var_eps[:, u:u + 1], mv[:, u, 1:2], LN_EPS, None, ALU.add).then_inc(eps, 1)

            def centre(t, u):
                dve.wait_ge(rs, at(t, 1, 0))
                dve.tensor_scalar(work[:, u, :], work[:, u, :], mv[:, u, 0:1], rstd[:, u:u + 1], ALU.subtract,
                                  ALU.mult).then_inc(centred, 1)

            def shift(t, u):
                dve.wait_ge(scaled, at(t, 1, 0))
                dve.tensor_tensor(work[:, u, :], work[:, u, :], ln_b[:, :], ALU.add).then_inc(shifted, 1)

            def lows(t):
                for i in range(2):
                    dve.wait_ge(thi, at(t, 2, i))
                    dve.wait_ge(gated, at(t - 1, 1, 0))
                    dve.tensor_tensor(t_lo[:, 4 * i:4 * i + 4, :], x1_t[:, H[i]].rearrange("p (k t) -> p k t", t=P),
                                      f32(t_hi[:, 4 * i:4 * i + 4, :]), ALU.subtract).then_inc(tlo, 1)

            def output(t, u):
                for i in range(2):
                    dve.wait_ge(sig, at(t, 2, i))
                    if i == 0:
                        dve.wait_ge(emb, at(t, 1, 0))
                    dve.tensor_tensor(gate[:, H[i]], gate[:, H[i]], ps_e[i][:, :], ALU.mult).then_inc(prod, 1)
                dve.wait_ge(prod, at(t, 2, 1))
                dve.scalar_tensor_tensor(gate, work[:, u, :], ALPHA, gate, ALU.mult, ALU.add).then_inc(summed, 1)

            def step(t, u, fill):
                statistics(t + 1, 1 - u, fill)
                lows(t)
                centre(t + 1, 1 - u)
                output(t, u)
                shift(t + 1, 1 - u)

            for n in range(1, len(W), 2):
                weight(n)
            dve.wait_ge(const_in, 48)
            dve.wait_ge(wlo_pool, len(W) // 2)
            statistics(0, 0, 1)
            centre(0, 0)
            shift(0, 0)
            with dve.Fori(0, 8) as it:
                step(2 * it, 0, it + 1)
                step(2 * it + 1, 1, it + 2)
            lows(TT - 1)
            output(TT - 1, 0)

        @block.tensor
        def _(pe):
            for s, n in ((mixed, 1), (emb, 1), (turned, 2), (gated, 1)):
                pe.sem_inc(s, 2 * n)
            pe.wait_ge(const_in, 48)

            def mix(t, first=False):
                pe.wait_ge(split_lo, at(t, 2, 0))
                pe.wait_ge(resid, at(t - 1, 2, 1))
                for k in range(KD):
                    if first:
                        wait_piece(pe, k)
                    for i in range(2):
                        mm = product(pe, ps_m[i][:, :], (m_hi[:, k, :], m_lo[:, k, :]),
                                     (wo_hi[:, k, H[i]], wo_lo[:, k, H[i]]), k == 0, k == KD - 1)
                mm.then_inc(mixed, 1)

            def embed(t, u, first=False):
                if first:
                    wait_piece(pe, KD + 1)
                pe.wait_ge(split_lo, at(t, 2, 1))
                pe.wait_ge(prod, at(t - 1, 2, 1))
                for k in range(2):
                    for i in range(2):
                        mm = product(pe, ps_e[i][:, :], (e_hi[:, u, k, :], e_lo[:, u, k, :]),
                                     (we_hi[:, k, H[i]], we_lo[:, k, H[i]]), k == 0, k == 1)
                mm.then_inc(emb, 1)

            def turn(t, u):
                pe.wait_ge(shifted, at(t, 1, 0))
                for i in range(2):
                    pe.wait_ge(tlo, at(t - 1, 2, i))
                    for k in range(4):
                        mm = pe.transpose(ps_t[i][:, k * P:(k + 1) * P],
                                          work[:, u, (4 * i + k) * P:(4 * i + k + 1) * P], ident[:, :])
                    mm.then_inc(turned, 1)

            def gates(t, first=False):
                pe.wait_ge(sig, at(t - 1, 2, 1))
                for k in range(KD):
                    if first:
                        wait_piece(pe, KD + 2 + k)
                    if k % 4 == 0:
                        pe.wait_ge(tlo, at(t, 2, k // 4))
                    for i in range(2):
                        mm = product(pe, ps_g[i][:, :], (t_hi[:, k, :], t_lo[:, k, :]),
                                     (wg_hi[:, k, H[i]], wg_lo[:, k, H[i]]), k == 0, k == KD - 1)
                mm.then_inc(gated, 1)

            mix(0, True)
            wait_piece(pe, len(W) - 1)
            with pe.Fori(0, 8) as it:
                for u in range(2):
                    t = 2 * it + u
                    mix(t + 1)
                    embed(t, u)
                    turn(t, u)
                    gates(t)
            embed(TT - 1, 0)
            turn(TT - 1, 0)
            gates(TT - 1)


BLOCKS = (6, 6, 5)
FIRST = (0, 6, 12)
BW = BLOCKS[0] * P
CHW = BW // 2
PAIRS_F = FT // 2
UNITS_F = 3 * FT
RAWS = 3
EVEN, DOWN, ODD = (0, 1), (2, 3), (4, 5)
LAST = PAIRS_F - 1


def phase_ffn(nc, g):
    assert sum(BLOCKS) == TT and UNITS_F % RAWS == 0
    with ExitStack() as ctx:
        ar = Arena(nc, ctx, "ff")
        sb, bank, sem = ar.sb, ar.bank, ar.sem
        w_raw = sb("w_raw", [P, RAWS, D])
        w_hi, w_lo = sb("w_hi", [P, 6, KD, P], F32R), sb("w_lo", [P, 6, KD, P], F32R)
        x_raw = sb("x_raw", [P, 2, BW])
        x_hi, x_lo = sb("x_hi", [P, KD, BW], F32R), sb("x_lo", [P, KD, BW], F32R)
        h_hi, h_lo = sb("h_hi", [P, 2, BW], F32R), sb("h_lo", [P, 2, BW], F32R)
        y = sb("y", [P, BLOCKS[0], D])
        up = [sb("up_a", [P, 2 + BW]), sb("up_b", [P, 2 + BW])]
        cv = [sb("cv_a", [P, BW]), sb("cv_b", [P, BW])]
        h = sb("h", [P, 2, BW])
        carry = sb("carry", [P, 2, FT, 2])
        s_hist = sb("s_hist", [P, 2, FT, ROWS, 2])
        taps = sb("taps", [P, 2, FT, 4])
        ln_g, ln_b = sb("ln_g", [P, D]), sb("ln_b", [P, D])
        stats, mv = sb("stats", [P, BLOCKS[0], 12]), sb("mv", [P, BLOCKS[0], 2])
        var_eps, rstd, power = sb("var_eps", [P, BLOCKS[0]]), sb("rstd", [P, BLOCKS[0]]), sb("power", [P, 1])
        ps_u = [bank(f"u{i}") for i in range(4)]
        ps_d = [bank(f"d{i}") for i in range(4)]

        const_in, ln_in, met = sem("const_in"), sem("ln_in"), sem("met")
        w_in = [sem(f"w_in{i}") for i in range(RAWS)]
        x_in = [sem("x_in0"), sem("x_in1")]
        y_in, st_y, st_c = sem("y_in"), sem("st_y"), sem("st_c")
        whi, wlo = sem("whi"), sem("wlo")
        xhi, xlo = sem("xhi"), sem("xlo")
        upped = sem("upped")
        past = sem("past")
        evac = sem("evac")
        carried = sem("carried")
        conv = sem("conv")
        silu, mul = sem("silu"), sem("mul")
        hhi, hlo = sem("hhi"), sem("hlo")
        down = sem("down")
        added = sem("added")
        stat, aggr, eps = sem("stat"), sem("aggr"), sem("eps")
        rs, centred, scaled, shifted = sem("rs"), sem("centred"), sem("scaled"), sem("shifted")
        cleared, powered = sem("cleared"), sem("powered")
        H = (slice(0, 512), slice(512, 1024))

        def per_f(b, f, per, k):
            return (b * FT + f + 2) * per + k + 1

        def per_pair(b, p, per, k):
            return (FIRST[b] * PAIRS_F + BLOCKS[0] + p * BLOCKS[b]) * per + k + 1

        def unit(b, n):
            return b * UNITS_F + n + 1

        def chunks(b):
            w = BLOCKS[b] * P
            return (0, CHW), (CHW, w - CHW)

        def prompt_w(b):
            return BLOCKS[b] * P - (SAMPLE if b == 2 else 0)

        def sample_rows(buf):
            at0 = 2 + prompt_w(2)
            return buf[:, at0:at0 + ROWS * (NEW + 2)].rearrange("p (r t) -> p r t", t=NEW + 2)

        block = ctx.enter_context(nc.Block())

        @block.sync
        def _(sp):
            def load_w(b, n, q=0, register=None):
                i = n if register is None else n + 6 * register
                sp.wait_ge(wlo, b * UNITS_F + i + 1)
                sp.dma_start(w_raw[:, n % RAWS, :], g["w_ffn_p"][i] if register is None else
                             g["w_ffn_p"].rearrange("n p c -> p n c")[:, ds(i, 1), :]).then_inc(w_in[n % RAWS], 16)

            def load_x(b):
                w = BLOCKS[b] * P
                for k in range(KD):
                    sp.wait_ge(xlo, b * KD + k + 1)
                    sp.dma_start(x_raw[:, k % 2, 0:w], g["x1_t"][k * P:(k + 1) * P, FIRST[b] * P:FIRST[b] * P + w])\
                      .then_inc(x_in[k % 2], 16)

            def load_y(b):
                for t in range(BLOCKS[b]):
                    r = (FIRST[b] + t) * P
                    sp.dma_start(y[:, t, :], g["y0"][r:r + P, :]).then_inc(y_in, 16)

            def store_y(b):
                for t in range(BLOCKS[b]):
                    r = (FIRST[b] + t) * P
                    sp.wait_ge(shifted, FIRST[b] + t + 1)
                    sp.dma_start(g["y"][r:r + P, :], y[:, t, :]).then_inc(st_y, 16)

            sp.dma_start(taps[:, :, :, :], g["taps"]).then_inc(const_in, 16)
            sp.dma_start(s_hist[:, :, :, :, :], g["conv_hist"]).then_inc(const_in, 16)
            for b in range(3):
                for n in range(RAWS):
                    load_w(b, n)
                load_x(b)
                if b == 0:
                    sp.dma_start(ln_g[:, :], g["ln2_g"]).then_inc(ln_in, 16)
                    sp.dma_start(ln_b[:, :], g["ln2_b"]).then_inc(ln_in, 16)
                load_w(b, 3)
                if b > 0:
                    store_y(b - 1)
                    sp.wait_ge(st_y, 16 * FIRST[b])
                load_y(b)
                with sp.Fori(0, PAIRS_F - 1) as q:
                    for j in range(6):
                        load_w(b, 4 + j, register=q)
                for n in range(UNITS_F - 2, UNITS_F):
                    load_w(b, n)
            sp.wait_ge(carried, per_f(2, FT - 1, 2, 1) + 2 * FT)
            sp.dma_start(g["conv_p"].rearrange("p (s f) t -> p s f t", s=2), carry[:, :, :, :]).then_inc(st_c, 16)
            sp.dma_start(g["conv_s"].rearrange("p (s f) r t -> p s f r t", s=2), s_hist[:, :, :, :, :])\
              .then_inc(st_c, 16)
            store_y(2)
            sp.wait_ge(st_y, 16 * TT)
            sp.wait_ge(st_c, 32)

        def opening_units():
            return ((0, EVEN[0]), (1, EVEN[1])), ((2, ODD[0]), (3, ODD[1]))

        def even_units(first, last):
            own = () if first else ((4, ODD[0]), (5, ODD[1]))
            a = 4 if first else 6
            return own, tuple((a + i, (DOWN if last else EVEN)[i]) for i in range(2))

        def odd_units(first, last):
            a = 6 if first else 8
            return () if last else tuple((a + i, DOWN[i]) for i in range(2))

        @block.gpsimd
        def _(pool):
            pool.sem_inc(wlo, RAWS)
            pool.sem_inc(xlo, 2)
            pool.sem_inc(hlo, 2)
            pool.memset(power[:, :], -0.5).then_inc(powered, 1)
            pool.wait_ge(powered, 1)

            def weight(b, n, base, slot):
                pool.wait_ge(whi, unit(b, base + n))
                pool.tensor_tensor(w_lo[:, slot], w_raw[:, n % RAWS, :].rearrange("p (k c) -> p k c", c=P),
                                   f32(w_hi[:, slot]), ALU.subtract).then_inc(wlo, 1)

            def product_lo(b, f, i):
                w = BLOCKS[b] * P
                pool.wait_ge(hhi, per_f(b, f, 1, 0))
                pool.tensor_tensor(h_lo[:, i, 0:w], h[:, i, 0:w], f32(h_hi[:, i, 0:w]), ALU.subtract)\
                    .then_inc(hlo, 1)

            def opening(b):
                early, late = opening_units()
                for n, slot in early:
                    weight(b, n, 0, slot)
                w = BLOCKS[b] * P
                for k in range(KD):
                    pool.wait_ge(xhi, b * KD + k + 1)
                    pool.tensor_tensor(x_lo[:, k, 0:w], x_raw[:, k % 2, 0:w], f32(x_hi[:, k, 0:w]), ALU.subtract)\
                        .then_inc(xlo, 1)
                for n, slot in late:
                    weight(b, n, 0, slot)

            def pair(b, p, n0, base, first=False, last=False):
                for part in even_units(first, last):
                    for n, slot in part:
                        weight(b, n0 + n, base, slot)
                product_lo(b, 2 * p, 0)
                for n, slot in odd_units(first, last):
                    weight(b, n0 + n, base, slot)
                product_lo(b, 2 * p + 1, 1)

            def normalise(b):
                pool.wait_ge(ln_in, 32)
                for t in range(BLOCKS[b]):
                    n = FIRST[b] + t + 1
                    pool.wait_ge(eps, n)
                    pool.tensor_tensor(rstd[:, t:t + 1], var_eps[:, t:t + 1], power[:, :], ALU.pow).then_inc(rs, 1)
                    pool.wait_ge(centred, n)
                    pool.tensor_tensor(y[:, t, :], y[:, t, :], ln_g[:, :], ALU.mult).then_inc(scaled, 1)

            for b in range(3):
                opening(b)
                if b > 0:
                    normalise(b - 1)
                pair(b, 0, 0, 0, first=True)
                with pool.Fori(0, LAST - 1) as q:
                    pair(b, q + 1, 4, 6 * q)
                pair(b, LAST, 4, 6 * (LAST - 1), last=True)
            normalise(2)

        @block.scalar
        def _(act):
            for s, n in ((past, 2), (evac, 4), (carried, 2), (silu, 1), (hhi, 1)):
                act.sem_inc(s, 2 * n)
            act.sem_inc(carried, 2 * FT)

            def weight(b, n, base, slot, q2=0):
                act.wait_ge(w_in[n % RAWS], (b * (UNITS_F // RAWS) + n // RAWS + 1 + q2) * 16)
                act.activation(w_hi[:, slot], w_raw[:, n % RAWS, :].rearrange("p (k c) -> p k c", c=P), ACT.Copy)\
                   .then_inc(whi, 1)

            def opening(b):
                early, late = opening_units()
                act.wait_ge(upped, per_f(b, -2, 4, 3))
                for n, slot in early:
                    weight(b, n, 0, slot)
                act.wait_ge(upped, per_f(b, -1, 4, 3))
                w = BLOCKS[b] * P
                for k in range(KD):
                    act.wait_ge(x_in[k % 2], (b * KD // 2 + k // 2 + 1) * 16)
                    act.activation(x_hi[:, k, 0:w], x_raw[:, k % 2, 0:w], ACT.Copy).then_inc(xhi, 1)
                for n, slot in late:
                    weight(b, n, 0, slot)

            def rows(b, f):
                pw = prompt_w(b)
                for s in range(2):
                    buf, fs = up[s], f if isinstance(f, int) else None
                    at_f = slice(f, f + 1) if fs is not None else ds(f, 1)
                    act.wait_ge(conv, per_f(b, f - 1, 4, 3))
                    act.wait_ge(carried, per_f(b, f - 1, 2, 1) + 2 * FT)
                    act.activation(buf[:, 0:2], carry[:, s, at_f, :], ACT.Copy)
                    if b == 2:
                        act.activation(sample_rows(buf)[:, :, 0:2], s_hist[:, s, at_f], ACT.Copy)
                    for c, (a, w) in enumerate(chunks(b)):
                        ps = ps_u[2 * s + c]
                        act.wait_ge(upped, per_f(b, f, 4, 2 * s + c))
                        if a + w <= pw:
                            act.activation(buf[:, 2 + a:2 + a + w], ps[:, 0:w], ACT.Copy)
                        else:
                            act.activation(buf[:, 2 + a:2 + pw], ps[:, 0:pw - a], ACT.Copy)
                            act.activation(sample_rows(buf)[:, :, 2:2 + NEW],
                                           ps[:, pw - a:w].rearrange("p (r t) -> p r t", t=NEW), ACT.Copy)
                        if s == 0:
                            act.wait_ge(mul, per_f(b, f - 1, 1, 0))
                            act.wait_ge(silu, per_f(b, f - 1, 1, 0))
                            take(act, met)
                        act.activation(cv[s][:, a:a + w], ps[:, 0:w], ACT.Identity, scale=taps[:, s, at_f, 2:3],
                                       bias=taps[:, s, at_f, 3:4]).then_inc(evac, 1)
                    act.wait_ge(evac, per_f(b, f, 4, 2 * s + 1))
                    take(act, met)
                    if b == 2:
                        act.activation(s_hist[:, s, at_f], sample_rows(buf)[:, :, NEW:NEW + 2], ACT.Copy)
                    act.activation(carry[:, s, at_f, :], buf[:, pw:pw + 2], ACT.Copy).then_inc(carried, 1)

            def product_hi(b, f, i):
                w = BLOCKS[b] * P
                act.wait_ge(mul, per_f(b, f, 1, 0))
                act.activation(h_hi[:, i, 0:w], h[:, i, 0:w], ACT.Copy).then_inc(hhi, 1)

            def pair(b, p, n0, q2, first=False, last=False):
                w = BLOCKS[b] * P
                for i in range(2):
                    f = 2 * p + i
                    rows(b, f)
                    act.wait_ge(conv, per_f(b, f, 4, 1))
                    act.activation(cv[0][:, 0:w], cv[0][:, 0:w], ACT.Silu).then_inc(silu, 1)
                    if i == 0:
                        own, following = even_units(first, last)
                        for n, slot in own:
                            weight(b, n0 + n, 0, slot, q2)
                        if last:
                            act.wait_ge(down, per_pair(b, p - 1, 1, BLOCKS[b] - 1))
                        for n, slot in following:
                            weight(b, n0 + n, 0, slot, q2)
                        act.wait_ge(down, per_pair(b, p - 1, 1, BLOCKS[b] - 1))
                    else:
                        for n, slot in odd_units(first, last):
                            weight(b, n0 + n, 0, slot, q2)
                    product_hi(b, f, i)

            act.wait_ge(const_in, 32)
            act.wait_ge(cleared, 1)
            for b in range(3):
                opening(b)
                pair(b, 0, 0, 0, first=True)
                with act.Fori(0, LAST - 1) as q:
                    pair(b, q + 1, 4, 2 * q)
                pair(b, LAST, 4, 2 * (LAST - 1), last=True)

        @block.vector
        def _(dve):
            for s, n in ((conv, 4), (mul, 1)):
                dve.sem_inc(s, 2 * n)
            dve.sem_inc(added, 2 * BLOCKS[0])
            dve.memset(carry[:, :, :, :], 0.0).then_inc(cleared, 1)
            dve.wait_ge(const_in, 32)

            def convolve(b, f):
                pw = prompt_w(b)
                at_f = slice(f, f + 1) if isinstance(f, int) else ds(f, 1)
                for s in range(2):
                    dve.wait_ge(evac, per_f(b, f, 4, 2 * s + 1))
                    for k in (1, 0):
                        if k == 0:
                            dve.wait_ge(conv, per_f(b, f, 4, 2 * s))
                        tap = taps[:, s, at_f, k:k + 1]
                        op = dve.scalar_tensor_tensor(cv[s][:, 0:pw], up[s][:, k:k + pw], tap, cv[s][:, 0:pw],
                                                      ALU.mult, ALU.add)
                        if b == 2:
                            rows = cv[s][:, pw:pw + SAMPLE].rearrange("p (r t) -> p r t", t=NEW)
                            op = dve.scalar_tensor_tensor(rows, sample_rows(up[s])[:, :, k:k + NEW], tap, rows,
                                                          ALU.mult, ALU.add)
                        op.then_inc(conv, 1)

            def gate(b, f, i):
                w = BLOCKS[b] * P
                dve.wait_ge(silu, per_f(b, f, 1, 0))
                dve.wait_ge(conv, per_f(b, f, 4, 3))
                dve.wait_ge(hlo, per_f(b, f, 1, 0) - 2)
                dve.tensor_tensor(h[:, i, 0:w], cv[0][:, 0:w], cv[1][:, 0:w], ALU.mult).then_inc(mul, 1)

            def add(b, p, t, two):
                dve.wait_ge(down, per_pair(b, p, 1, t))
                if two is None or t == 0:
                    dve.wait_ge(added, per_pair(b, p - 1, 2, 2 * BLOCKS[b] - 1))
                for i in range(2):
                    dve.tensor_tensor(y[:, t, H[i]], y[:, t, H[i]], ps_d[2 * (t % 2) + i][:, :], ALU.add)\
                       .then_inc(added, 1)

            def adds(b, p, tiles):
                for t in tiles:
                    add(b, p, t, True)

            def pair(b, p, first=False):
                convolve(b, 2 * p)
                if first:
                    dve.wait_ge(y_in, 16 * (FIRST[b] + BLOCKS[b]))
                else:
                    adds(b, p - 1, (0,))
                gate(b, 2 * p, 0)
                if not first:
                    adds(b, p - 1, range(1, BLOCKS[b]))
                convolve(b, 2 * p + 1)
                gate(b, 2 * p + 1, 1)

            def statistics(b, t):
                n = FIRST[b] + t + 1
                dve.wait_ge(added, per_pair(b, LAST, 2, 2 * t + 1))
                for i in range(2):
                    dve.bn_stats(stats[:, t, 6 * i:6 * i + 6], y[:, t, H[i]]).then_inc(stat, 1)
                dve.wait_ge(stat, 2 * n)
                dve.bn_aggr(mv[:, t, :], stats[:, t, :]).then_inc(aggr, 1)
                dve.wait_ge(aggr, n)
                dve.tensor_scalar(var_eps[:, t:t + 1], mv[:, t, 1:2], LN_EPS, None, ALU.add).then_inc(eps, 1)

            def normalise(b):
                T = BLOCKS[b]
                dve.wait_ge(ln_in, 32)
                for t in range(T):
                    add(b, LAST, t, True)
                    statistics(b, t)
                for t in range(T + 1):
                    if t < T:
                        dve.wait_ge(rs, FIRST[b] + t + 1)
                        dve.tensor_scalar(y[:, t, :], y[:, t, :], mv[:, t, 0:1], rstd[:, t:t + 1], ALU.subtract,
                                          ALU.mult).then_inc(centred, 1)
                    if t > 0:
                        dve.wait_ge(scaled, FIRST[b] + t)
                        dve.tensor_tensor(y[:, t - 1, :], y[:, t - 1, :], ln_b[:, :], ALU.add).then_inc(shifted, 1)

            for b in range(3):
                pair(b, 0, first=True)
                with dve.Fori(0, LAST) as q:
                    pair(b, q + 1)
                normalise(b)

        @block.tensor
        def _(pe):
            pe.sem_inc(upped, 8)
            pe.sem_inc(down, BLOCKS[0])

            def rows(b, f, n, slots, opening=False):
                for s in range(2):
                    pe.wait_ge(wlo, RAWS + unit(b, n + s))
                    for c, (a, w) in enumerate(chunks(b)):
                        pe.wait_ge(evac, per_f(b, f - 1, 4, 2 * s + c))
                        for k in range(KD):
                            if opening and s == 0 and c == 0:
                                pe.wait_ge(xlo, 2 + b * KD + k + 1)
                            mm = product(pe, ps_u[2 * s + c][:, 0:w], (w_hi[:, slots[s], k, :], w_lo[:, slots[s], k, :]),
                                         (x_hi[:, k, a:a + w], x_lo[:, k, a:a + w]), k == 0, k == KD - 1)
                        mm.then_inc(upped, 1)

            def downs(b, p, n):
                pe.wait_ge(wlo, RAWS + unit(b, n + 1))
                pe.wait_ge(hlo, per_f(b, 2 * p + 1, 1, 0))
                for t in range(BLOCKS[b]):
                    if t < 2:
                        pe.wait_ge(added, per_pair(b, p - 1, 2, 2 * BLOCKS[b] - 1))
                    else:
                        pe.wait_ge(added, per_pair(b, p, 2, 2 * (t - 2) + 1))
                    for s in range(2):
                        for i in range(2):
                            wide = [x[:, DOWN[s], 4 * i:4 * i + 4, :].rearrange("p k c -> p (k c)") for x in (w_hi, w_lo)]
                            cols = slice(t * P, (t + 1) * P)
                            mm = product(pe, ps_d[2 * (t % 2) + i][:, :], (h_hi[:, s, cols], h_lo[:, s, cols]), wide,
                                         s == 0, s == 1)
                    mm.then_inc(down, 1)

            for b in range(3):
                rows(b, 0, 0, EVEN, opening=True)
                rows(b, 1, 2, ODD)
                with pe.Fori(0, LAST) as q:
                    n = 6 * q + 4
                    rows(b, 2 * q + 2, n, EVEN)
                    downs(b, q, n + 2)
                    rows(b, 2 * q + 3, n + 4, ODD)
                downs(b, LAST, UNITS_F - 2)


def kernel(**inputs):
    import numpy as np
    import concourse.bacc as bacc
    from concourse.bass_utils import run_bass_kernel_spmd

    a = {k: np.asarray(v) for k, v in inputs.items()}
    tile = lambda w, kt: w.reshape(kt, P, -1)
    w_in = a["w_in"][0]
    swap = np.r_[ROPE // 2:ROPE, 0:ROPE // 2]
    kr_cols = w_in[:, 2 * LORA:2 * LORA + ROPE]
    cols = {"q0": w_in[:, 0:128], "q1": w_in[:, 128:256], "c0": w_in[:, 256:384], "c1": w_in[:, 384:512],
            "kr": np.concatenate([kr_cols, kr_cols[:, swap]], 1)}
    for i in range(4):
        at = 2 * LORA + ROPE + i * P
        cols[f"u{i}"] = w_in[:, at:at + P]
    pieces = []
    for name in UNITS:
        t = tile(cols[name], KD).transpose(1, 0, 2)
        pieces += [t.reshape(P, CW)] if name == "kr" else [t[:, 0:4].reshape(P, CW), t[:, 4:8].reshape(P, CW)]
    pieces.append(a["w_pool"][0].transpose(1, 0, 2).reshape(P, CW))
    per_feature = lambda v: v.reshape(-1, P).T
    x_t = np.concatenate([a["x_prompt"][0].T, a["x_sample"].reshape(SAMPLE, D).T,
                          np.zeros((D, CW - SAMPLE), np.float32)], 1)
    inv = (1.0 / (np.float32(10000.0) ** (np.arange(0, ROPE, 2, dtype=np.float32) / ROPE))).astype(np.float32)
    pos = np.concatenate([np.arange(SEQ), np.tile(PAST + np.arange(NEW), ROWS),
                          np.zeros(CW - SAMPLE)]).astype(np.float32)
    ang = (pos[None, :] * inv[:, None]).astype(np.float32)
    cos, sin = np.cos(ang).astype(np.float32), np.sin(ang).astype(np.float32)
    trig_k = np.concatenate([cos, cos, -sin, sin], 0)
    inv_cnt = np.zeros((P, 2, 4, 16), np.float32)
    for i, w in enumerate(POOLS):
        inv_cnt[:, 0, i] = 1.0 / np.minimum(w, np.arange(16) + 1)
        inv_cnt[:, 1, i] = 1.0 / w
    w_q = tile(a["w_q_b"][0], 2).reshape(2, P, HEADS, NOPE + ROPE)
    w_q = np.concatenate([w_q, w_q[..., NOPE + swap]], 3).transpose(1, 2, 0, 3)
    w_kv = tile(a["w_kv_b"][0], 2).reshape(2, P, HEADS, NOPE + VD)
    w_k = w_kv[..., :NOPE].reshape(2, P, HEADS // 2, P).transpose(1, 2, 0, 3)
    w_v = w_kv[..., NOPE:].reshape(2, P, MLA).transpose(1, 0, 2)
    w_hd_p = np.concatenate([w.reshape(P, -1, CW).transpose(1, 0, 2) for w in (w_q, w_k, w_v)])
    w_up = tile(a["w_up"][0], KD).reshape(KD, P, 2, FT, P).transpose(2, 3, 1, 0, 4).reshape(2, FT, P, D)
    w_down = tile(a["w_down"][0], FT)
    order = [w_up[0, 0], w_up[1, 0], w_up[0, 1], w_up[1, 1]]
    for f in range(2, FT, 2):
        order += [w_up[0, f], w_up[1, f], w_down[f - 2], w_down[f - 1], w_up[0, f + 1], w_up[1, f + 1]]
    order += [w_down[FT - 2], w_down[FT - 1]]
    taps = np.concatenate([a["w_dw"][0], a["b_dw"]]).reshape(4, 2, FT, P).transpose(3, 1, 2, 0)
    ins = {
        "w_ffn_p": np.stack(order), "taps": taps,
        "conv_hist": a["state_ffn_conv"][0].reshape(ROWS, 2, 2, FT, P).transpose(4, 2, 3, 0, 1),
        "ln2_g": np.broadcast_to(a["ln2_g"][0], (P, D)), "ln2_b": np.broadcast_to(a["ln2_b"][0], (P, D)),
        "w_hd_p": w_hd_p,
        "ident": np.eye(P, dtype=np.float32),
        "x_t": x_t,
        "w_in_p": np.stack(pieces),
        "gains": np.concatenate([per_feature(a["g_kv"][0]), per_feature(a["g_q"][0]), per_feature(a["s_pool"][0])], 1),
        "inv_cnt": inv_cnt,
        "trig_k": trig_k,
        "w_mix_p": np.concatenate([tile(a["w_o"][0], KD), tile(a["w_pe"][0], 2), tile(a["w_pg"][0], KD)]),
        "x": np.concatenate([a["x_prompt"][0], a["x_sample"].reshape(SAMPLE, D)]),
        "pe_t": np.concatenate([a["p_prompt"][0, 0].T, a["p_sample"][0].reshape(SAMPLE, PLE).T], 1),
        "ln1_g": np.broadcast_to(a["ln1_g"][0], (P, D)), "ln1_b": np.broadcast_to(a["ln1_b"][0], (P, D)),
        "w_uk_p": w_kv[..., :NOPE].reshape(LORA, HEADS, NOPE).transpose(2, 1, 0),
        "w_uv_p": w_kv[..., NOPE:].transpose(1, 0, 2, 3),
        "ckv_t": a["cache_ckv"][0].reshape(ROWS, PAST, 2, P).transpose(0, 3, 2, 1),
        "ckv": a["cache_ckv"][0].reshape(ROWS, PAST // P, P, LORA).transpose(0, 2, 1, 3),
        "krope_t": a["cache_krope"][0].transpose(0, 2, 1),
        "pool_hist": a["state_pool"][0].reshape(ROWS, HIST, 4, P).transpose(3, 2, 0, 1),
    }
    ins = {k: np.ascontiguousarray(v) for k, v in ins.items()}
    outs = {"c_t": (LORA, TOK), "kr_t": (ROPE, TOK), "pool_p": (P, 4, HIST), "pool_s": (P, 4, ROWS, HIST),
            "y": (TOK, D), "conv_p": (P, 2 * FT, 2), "conv_s": (P, 2 * FT, ROWS, 2)}
    nc = bacc.Bacc("TRN2", target_bir_lowering=False, num_devices=1)
    g = {k: nc.dram_tensor(f"in_{k}", v.shape, F32, kind="ExternalInput").ap() for k, v in ins.items()}
    g |= {k: nc.dram_tensor(f"out_{k}", s, F32, kind="ExternalOutput").ap() for k, s in outs.items()}
    scratch = {"qn_t": (LORA, TOK), "mix_t": (D, TOK), "q_t": (HEADS * 96, TOK), "k_t": (HEADS * NOPE, SEQ),
               "v": (SEQ, MLA), "x1_t": (D, TOK), "y0": (TOK, D)}
    g |= {k: nc.dram_tensor(f"scratch_{k}", s, F32, kind="Internal").ap() for k, s in scratch.items()}
    build(nc, g)
    r = run_bass_kernel_spmd(nc, [{f"in_{k}": v for k, v in ins.items()}], core_ids=[0]).results[0]
    o = {k: r[f"out_{k}"] for k in outs}
    return finish(o)


def build(nc, g):
    for phase in (phase_project, phase_heads, phase_attend, phase_sample, phase_mix, phase_ffn):
        with nc.cleanup_on_exit():
            phase(nc, g)


def finish(o):
    ckv, kr = o["c_t"].T, o["kr_t"].T
    return (o["y"][:SEQ].reshape(1, SEQ, D), o["y"][SEQ:].reshape(ROWS, NEW, D),
            ckv[:SEQ].reshape(1, 1, SEQ, LORA), kr[:SEQ].reshape(1, 1, SEQ, ROPE),
            o["pool_p"].transpose(2, 1, 0).reshape(1, 1, HIST, MLA),
            o["conv_p"].transpose(2, 1, 0).reshape(1, 1, 2, 2 * FF),
            ckv[SEQ:].reshape(1, ROWS, NEW, LORA), kr[SEQ:].reshape(1, ROWS, NEW, ROPE),
            o["pool_s"].transpose(2, 3, 1, 0).reshape(1, ROWS, HIST, MLA),
            o["conv_s"].transpose(2, 3, 1, 0).reshape(1, ROWS, 2, 2 * FF))
```

```python
from contextlib import ExitStack

import concourse.bass as bass
from concourse import mybir

F32 = mybir.dt.float32
F32R = mybir.dt.float32r
ACT = mybir.ActivationFunctionType
ALU = mybir.AluOpType
AX = mybir.AxisListType

P = 128
D = 1024
KD = D // P
SEQ = 2048
ROWS, NEW, PAST = 8, 16, 512
SAMPLE = ROWS * NEW
TOK = SEQ + SAMPLE
LORA = 256
ROPE = 32
NOPE = 64
VD = 64
HEADS = 8
MLA = HEADS * VD
POOLS = (2, 4, 8, 16)
HIST = 15
FF = 2816
FT = FF // P
PLE = 256
CW = 512
CHUNKS = SEQ // CW
ALPHA = 2.0 ** 0.25
SCALE = (NOPE + ROPE) ** -0.5
NEG = -1e30
ds = bass.ds


class Arena:

    def __init__(self, nc, ctx, tag):
        self.nc, self.ctx, self.tag = nc, ctx, tag

    def sb(self, name, shape, dt=F32):
        return self.ctx.enter_context(self.nc.sbuf_tensor(f"{self.tag}_{name}", shape, dt))

    def bank(self, name):
        return self.ctx.enter_context(self.nc.psum_tensor(f"{self.tag}_{name}", [P, 512], F32))

    def sem(self, name):
        return self.nc.alloc_semaphore(name=f"{self.tag}_{name}")


def take(eng, met):
    eng.sem_inc(met, 1)


def f32(ap):
    return ap.bitcast(F32)


def product(pe, out, pairs, rhs_pairs, first, last, **kw):
    (lh, ll), (rh, rl) = pairs, rhs_pairs
    pe.matmul(out, lh, rh, start=first, stop=False, **kw)
    pe.matmul(out, ll, rh, start=False, stop=False, **kw)
    return pe.matmul(out, lh, rl, start=False, stop=last, **kw)

def at(c, per, k):
    return (c + 2) * per + k + 1


UNITS = ("u3", "u2", "u1", "u0", "c0", "c1", "q0", "q1", "kr")
UNIT_BANK = (0, 1, 2, 3, 0, 1, 2, 3, 0)
NU = len(UNITS)
RAW = 4
W_PIECES = 2 * 8 + 1 + 1


def nth(c, per, k):
    return (c + 1) * per + k + 1


def phase_project(nc, g):
    with ExitStack() as ctx:
        ar = Arena(nc, ctx, "pj")
        sb, bank, sem = ar.sb, ar.bank, ar.sem
        raw = sb("raw", [P, RAW, CW])
        w_hi = sb("w_hi", [P, 8, KD, P], F32R)
        w_lo = sb("w_lo", [P, 8, KD, P], F32R)
        wk_hi = sb("wk_hi", [P, KD, 64], F32R)
        wk_lo = sb("wk_lo", [P, KD, 64], F32R)
        wp_hi = sb("wp_hi", [P, 4, P], F32R)
        wp_lo = sb("wp_lo", [P, 4, P], F32R)
        x_hi = sb("x_hi", [P, 2, KD, CW], F32R)
        x_lo = sb("x_lo", [P, 2, KD, CW], F32R)
        u = sb("u", [P, 4, 16 + CW])
        win = sb("win", [P, 2, 16 + CW])
        dif = sb("dif", [P, 2, CW])
        t_hi = sb("t_hi", [P, 4, CW], F32R)
        t_lo = sb("t_lo", [P, 4, CW], F32R)
        lat = sb("lat", [P, 4, CW])
        sq = sb("sq", [P, CW])
        rstd = sb("rstd", [P, 2, CW])
        latn = sb("latn", [P, 2, CW])
        kr_t = sb("kr_t", [ROPE, 3, CW])
        trig = sb("trig", [64, CW])
        pool_o = sb("pool_o", [P, 2, CW])
        gains = sb("gains", [P, 8])
        inv_cnt = sb("inv_cnt", [P, 2, 4, 16])
        fix = sb("fix", [P, 16])
        ones = sb("ones", [P, P], F32R)
        ps = [bank(f"ps{i}") for i in range(4)]
        ps_stat = [bank("stat_c"), bank("stat_q")]
        ps_pool = [bank("pool0"), bank("pool1")]

        landed = [sem(f"landed{i}") for i in range(2 * RAW)]
        const_in, met = sem("const_in"), sem("met")
        trig_in = sem("trig_in")
        hist_in = sem("hist_in")
        cleared = sem("cleared")
        split_hi = sem("split_hi")
        split_lo = sem("split_lo")
        split_odd = sem("split_odd")
        unit_done = sem("unit_done")
        evac = sem("evac")
        squared = sem("squared")
        kr_mul = sem("kr_mul")
        kr_ready = sem("kr_ready")
        tmp_hi = sem("tmp_hi")
        tmp_lo = sem("tmp_lo")
        tmp_used = sem("tmp_used")
        var_eps = sem("var_eps")
        root = sem("root")
        rs = sem("rs")
        normed = sem("normed")
        step = sem("step")
        diff = sem("diff")
        fixed = sem("fixed")
        pool_ev = sem("pool_ev")
        st_lat = [sem("st_lat0"), sem("st_lat1")]
        st_kr = sem("st_kr")
        st_pool = [sem("st_pool0"), sem("st_pool1")]
        st_hist = sem("st_hist")
        SAMPLE_C = CHUNKS
        PJ_EPS = 1e-6

        w_dst = []
        for n, name in enumerate(UNITS):
            if name == "kr":
                w_dst.append((wk_hi[:, :, :], wk_lo[:, :, :]))
            else:
                m = n
                w_dst += [(w_hi[:, m, 4 * h:4 * h + 4, :], w_lo[:, m, 4 * h:4 * h + 4, :]) for h in range(2)]
        w_dst.append((wp_hi[:, :, :], wp_lo[:, :, :]))
        assert len(w_dst) == W_PIECES and W_PIECES % 2 == 0

        def unit_w(n, k):
            if UNITS[n] == "kr":
                return wk_hi[:, k, :], wk_lo[:, k, :]
            m = n
            return w_hi[:, m, k, :], w_lo[:, m, k, :]

        def x_slot(k):
            return (W_PIECES + k) % RAW

        def x_piece(c, k):
            return W_PIECES + c * KD + k

        def x_use(c, k):
            return len(range(x_slot(k), W_PIECES, 2 * RAW)) + k // RAW + 1 + c * (KD // RAW)

        def w_raw(m):
            s = m % (2 * RAW)
            return raw[:, s, :] if s < RAW else lat[:, s - RAW, :]

        def rows16(ap):
            return ap.rearrange("p (r t) -> p r t", t=NEW)

        def rows32(ap):
            return ap.rearrange("p (r t) -> p r t", t=32)

        block = ctx.enter_context(nc.Block())

        @block.sync
        def _(sp):
            sp.dma_start(gains[:, :], g["gains"]).then_inc(const_in, 16)
            sp.dma_start(inv_cnt[:, :, :, :], g["inv_cnt"]).then_inc(const_in, 16)
            for m in range(W_PIECES):
                if m >= 2 * RAW and m % 2:
                    sp.wait_ge(split_odd, (m - 2 * RAW) // 2 + 1)
                elif m >= 2 * RAW:
                    sp.wait_ge(split_lo, m - 2 * RAW + 1)
                sp.dma_start(w_raw(m), g["w_in_p"][m]).then_inc(landed[m % (2 * RAW)], 16)
            for s, n in ((st_lat[0], 2), (st_lat[1], 2), (st_kr, 1), (st_pool[0], 2), (st_pool[1], 2)):
                sp.sem_inc(s, 16 * n)

            def load_x(c, first=False):
                for k in range(KD):
                    if first and k in (1, 3):
                        sp.wait_ge(split_odd, (x_piece(0, k) - RAW) // 2 + 1)
                    sp.wait_ge(split_lo, x_piece(c, k) - RAW + 1)
                    sp.dma_start(raw[:, x_slot(k), :], g["x_t"][k * P:(k + 1) * P, ds(c * CW, CW)])\
                      .then_inc(landed[x_slot(k)], 16)

            def load_trig(c):
                sp.dma_start(trig[:, :], g["trig_k"][:, ds(c * CW, CW)]).then_inc(trig_in, 16)

            def store_pool(c, width):
                for i in range(4):
                    sp.wait_ge(pool_ev, nth(c, 4, i))
                    row = MLA + (3 - i) * P
                    sp.dma_start(g["mix_t"][row:row + P, ds(c * CW, width)], pool_o[:, i % 2, 0:width])\
                      .then_inc(st_pool[i % 2], 16)

            def store(c, width):
                for i in range(4):
                    dst = (g["c_t"], g["qn_t"])[i // 2]
                    sp.wait_ge(normed, nth(c, 4, i))
                    take(sp, met)
                    sp.dma_start(dst[(i % 2) * P:(i % 2 + 1) * P, ds(c * CW, width)], latn[:, i % 2, 0:width])\
                      .then_inc(st_lat[i % 2], 16)
                sp.wait_ge(kr_ready, nth(c, 1, 0))
                sp.dma_start(g["kr_t"][:, ds(c * CW, width)], kr_t[:, 2, 0:width]).then_inc(st_kr, 16)

            load_x(0, first=True)
            load_trig(0)
            with sp.Fori(0, CHUNKS - 1) as c:
                load_x(c + 1)
                store_pool(c, CW)
                sp.wait_ge(kr_mul, nth(c, 2, 1))
                load_trig(c + 1)
                store(c, CW)
            last = CHUNKS - 1
            load_x(SAMPLE_C)
            sp.wait_ge(diff, nth(last, 4, 3))
            sp.dma_start(g["pool_p"], u[:, :, CW + 1:CW + 16]).then_inc(st_hist, 16)
            sp.wait_ge(st_hist, 16)
            for grp in range(4):
                sp.dma_start(rows32(u[:, grp, 0:ROWS * 32])[:, :, 1:16], g["pool_hist"][:, grp]).then_inc(hist_in, 16)
            store_pool(last, CW)
            sp.wait_ge(kr_mul, nth(last, 2, 1))
            load_trig(SAMPLE_C)
            store(last, CW)
            sp.wait_ge(evac, nth(SAMPLE_C, 8, 3))
            for grp in range(4):
                sp.dma_start(g["pool_s"][:, grp], rows32(u[:, grp, 0:ROWS * 32])[:, :, 17:32]).then_inc(st_hist, 16)
            store_pool(SAMPLE_C, SAMPLE)
            store(SAMPLE_C, SAMPLE)
            sp.wait_ge(st_hist, 80)
            for s, n in ((st_lat[0], 2), (st_lat[1], 2), (st_kr, 1), (st_pool[0], 2), (st_pool[1], 2)):
                sp.wait_ge(s, nth(SAMPLE_C, n, n - 1) * 16)

        @block.gpsimd
        def _(pool):
            pool.sem_inc(tmp_lo, 8)

            def split_x(c, par):
                for k in range(KD):
                    pool.wait_ge(split_hi, x_piece(c, k) + 1)
                    pool.tensor_tensor(x_lo[:, par, k, :], raw[:, x_slot(k), :], f32(x_hi[:, par, k, :]),
                                       ALU.subtract).then_inc(split_lo, 1)

            def tmp(c, i, src, width):
                pool.wait_ge(tmp_hi, nth(c, 8, i))
                pool.tensor_tensor(t_lo[:, i % 4, 0:width], src[:, 0:width], f32(t_hi[:, i % 4, 0:width]),
                                   ALU.subtract).then_inc(tmp_lo, 1)

            def chunk(c, par, width, more=True):
                for i in range(4):
                    tmp(c, i, dif[:, i % 2, :], width)
                if more:
                    split_x(c + 1, 1 - par)
                for i in range(4):
                    tmp(c, 4 + i, sq[:, :], width)

            for m in range(0, W_PIECES, 2):
                hi, lo = w_dst[m]
                pool.wait_ge(split_hi, m + 1)
                pool.tensor_tensor(lo, w_raw(m).rearrange("p (a b) -> p a b", a=hi.shape[1]), f32(hi),
                                   ALU.subtract).then_inc(split_lo, 2)
            split_x(0, 0)
            with pool.Fori(0, CHUNKS // 2) as it:
                chunk(2 * it, 0, CW)
                chunk(2 * it + 1, 1, CW)
            chunk(SAMPLE_C, 0, SAMPLE, more=False)

        @block.scalar
        def _(act):
            for s, n in ((evac, 8), (squared, 4), (tmp_hi, 8), (root, 2), (pool_ev, 4)):
                act.sem_inc(s, n)

            def split_x(c, par):
                for k in range(KD):
                    act.wait_ge(landed[x_slot(k)], 16 * x_use(c, k))
                    if k == 0:
                        act.wait_ge(unit_done, nth(c - 2, NU, NU - 1))
                    act.activation(x_hi[:, par, k, :], raw[:, x_slot(k), :], ACT.Copy).then_inc(split_hi, 1)

            def keep_u(c, i, width, sample):
                act.wait_ge(unit_done, nth(c, NU, i))
                src = ps[i][:, 0:width]
                if sample:
                    act.wait_ge(hist_in, 64)
                    act.activation(rows32(u[:, 3 - i, 0:ROWS * 32])[:, :, 16:32], rows16(src),
                                   ACT.Copy).then_inc(evac, 1)
                else:
                    act.wait_ge(step, nth(c, 11, 0))
                    act.activation(u[:, 3 - i, 16:16 + width], src, ACT.Copy).then_inc(evac, 1)

            def difference(c, i, width):
                act.wait_ge(diff, nth(c, 4, i))
                act.wait_ge(tmp_used, nth(c, 8, i - 4))
                act.activation(t_hi[:, i, 0:width], dif[:, i % 2, 0:width], ACT.Copy).then_inc(tmp_hi, 1)

            def latent(c, i, width):
                act.wait_ge(unit_done, nth(c, NU, 4 + i))
                act.wait_ge(normed, nth(c - 1, 4, i))
                act.activation(lat[:, i, 0:width], ps[i][:, 0:width], ACT.Copy).then_inc(evac, 1)
                act.wait_ge(tmp_lo, nth(c, 8, 4 + i - 1))
                act.activation(sq[:, 0:width], ps[i][:, 0:width], ACT.Square).then_inc(squared, 1)
                act.wait_ge(squared, nth(c, 4, i))
                act.wait_ge(tmp_used, nth(c, 8, i))
                act.activation(t_hi[:, i, 0:width], sq[:, 0:width], ACT.Copy).then_inc(tmp_hi, 1)

            def pooled(c, i, width):
                act.wait_ge(tmp_used, nth(c, 8, i))
                act.wait_ge(st_pool[i % 2], nth(c, 2, i // 2 - 1) * 16)
                act.activation(pool_o[:, i % 2, 0:width], ps_pool[i % 2][:, 0:width], ACT.Copy,
                               scale=gains[:, 4 + 3 - i:5 + 3 - i]).then_inc(pool_ev, 1)

            def chunk(c, par, width, sample=False):
                for i in range(4):
                    keep_u(c, i, width, sample)
                    if i > 0:
                        difference(c, i - 1, width)
                difference(c, 3, width)
                if not sample:
                    split_x(c + 1, 1 - par)
                for i in range(4):
                    latent(c, i, width)
                    pooled(c, i, width)
                for i in range(2):
                    act.wait_ge(var_eps, nth(c, 2, i))
                    act.activation(rstd[:, i, 0:width], rstd[:, i, 0:width], ACT.Sqrt).then_inc(root, 1)

            act.wait_ge(const_in, 32)
            for m in range(W_PIECES):
                hi, _ = w_dst[m]
                act.wait_ge(landed[m % (2 * RAW)], 16 * (m // (2 * RAW) + 1))
                act.activation(hi, w_raw(m).rearrange("p (a b) -> p a b", a=hi.shape[1]),
                               ACT.Copy).then_inc(split_hi, 1)
            for k in range(KD):
                act.wait_ge(landed[x_slot(k)], 16 * x_use(0, k))
                act.activation(x_hi[:, 0, k, :], raw[:, x_slot(k), :], ACT.Copy).then_inc(split_hi, 1)
            with act.Fori(0, CHUNKS // 2) as it:
                chunk(2 * it, 0, CW)
                chunk(2 * it + 1, 1, CW)
            chunk(SAMPLE_C, 0, SAMPLE, sample=True)

        @block.vector
        def _(dve):
            dve.memset(u[:, :, :], 0.0).then_inc(cleared, 1)
            dve.memset(f32(ones[:, :]), 1.0).then_inc(cleared, 1)
            for s, n in ((kr_mul, 2), (kr_ready, 1), (var_eps, 2), (rs, 2), (normed, 4), (step, 11), (diff, 4),
                         (fixed, 9)):
                dve.sem_inc(s, n)
            dve.wait_ge(cleared, 2)
            for m in range(1, W_PIECES, 2):
                hi, lo = w_dst[m]
                dve.wait_ge(split_hi, m + 1)
                dve.tensor_tensor(lo, w_raw(m).rearrange("p (a b) -> p a b", a=hi.shape[1]), f32(hi),
                                  ALU.subtract).then_inc(split_odd, 1)
            dve.wait_ge(const_in, 32)

            def normalise(c, j, width):
                dve.wait_ge(tmp_used, nth(c, 8, 4 + 2 * j + 1))
                dve.wait_ge(normed, nth(c - 1, 4, 2 * j + 1))
                dve.tensor_scalar(rstd[:, j, 0:width], ps_stat[j][:, 0:width], 1.0 / LORA, PJ_EPS,
                                  ALU.mult, ALU.add).then_inc(var_eps, 1)
                dve.wait_ge(root, nth(c, 2, j))
                dve.reciprocal(rstd[:, j, 0:width], rstd[:, j, 0:width]).then_inc(rs, 1)
                dve.wait_ge(rs, nth(c, 2, j))
                for i in (2 * j, 2 * j + 1):
                    dve.wait_ge(evac, nth(c, 8, 4 + i))
                    dve.wait_ge(st_lat[i % 2], nth(c, 2, j - 1) * 16)
                    dve.scalar_tensor_tensor(out=latn[:, i % 2, 0:width], in0=lat[:, i, 0:width],
                                             scalar=gains[:, i:i + 1], in1=rstd[:, j, 0:width],
                                             op0=ALU.mult, op1=ALU.mult).then_inc(normed, 1)

            def pool_group(c, i, width, sample, done):
                grp = 3 - i
                dve.wait_ge(evac, nth(c, 8, i))
                if sample:
                    dve.wait_ge(diff, nth(c, 4, i - 1))

                def span(buf, a, b):
                    if sample:
                        return rows32(buf[:, 0:ROWS * 32])[:, :, a:b]
                    return buf[:, a:b]
                end = 32 if sample else 16 + width
                src = u[:, grp, :]
                for level in range(1, grp + 2):
                    dst = win[:, level % 2, :]
                    lo, back = 2 ** level, 2 ** (level - 1)
                    dve.wait_ge(step, nth(c, 11, done - 1))
                    dve.tensor_tensor(span(dst, lo, end), span(src, lo, end), span(src, lo - back, end - back),
                                      ALU.add).then_inc(step, 1)
                    done += 1
                    src = dst
                dve.wait_ge(step, nth(c, 11, done - 1))
                dve.wait_ge(tmp_lo, nth(c, 8, i - 2))
                out = dif[:, i % 2, 0:width]
                main = dve.scalar_tensor_tensor(
                    out=rows16(out) if sample else out, in0=span(src, 16, end), scalar=1.0 / POOLS[grp],
                    in1=span(u[:, grp, :], 16, end), op0=ALU.mult, op1=ALU.subtract)
                if sample:
                    main.then_inc(diff, 1)
                else:
                    main.then_inc(fixed, 1)
                    dve.tensor_tensor(fix[:, :], src[:, 16:32], inv_cnt[:, 0, grp, :], ALU.mult).then_inc(fixed, 1)
                    dve.wait_ge(fixed, nth(c, 9, 2 * i + 1))
                    dve.tensor_tensor(dif[:, i % 2, 0:16], fix[:, :], u[:, grp, 16:32], ALU.subtract)\
                       .then_inc(diff, 1)
                return done

            def chunk(c, width, sample=False):
                done = 1
                if not sample:
                    dve.wait_ge(evac, nth(c - 1, 8, 3))
                    dve.tensor_copy(u[:, :, 1:16], u[:, :, CW + 1:CW + 16]).then_inc(step, 1)
                for i in range(4):
                    done = pool_group(c, i, width, sample, done)
                if not sample:
                    dve.wait_ge(diff, nth(c, 4, 3))
                    dve.tensor_copy(inv_cnt[:, 0, :, :], inv_cnt[:, 1, :, :]).then_inc(fixed, 1)
                    dve.wait_ge(fixed, nth(c, 9, 8))
                dve.wait_ge(unit_done, nth(c, NU, 8))
                dve.wait_ge(trig_in, nth(c - 1, 1, 0) * 16)
                dve.wait_ge(kr_ready, nth(c - 1, 1, 0))
                src = ps[UNIT_BANK[8]]
                dve.tensor_tensor(kr_t[:, 0, 0:width], src[0:32, 0:width], trig[0:32, 0:width], ALU.mult)\
                   .then_inc(kr_mul, 1)
                dve.tensor_tensor(kr_t[:, 1, 0:width], src[32:64, 0:width], trig[32:64, 0:width], ALU.mult)\
                   .then_inc(kr_mul, 1)
                dve.wait_ge(kr_mul, nth(c, 2, 1))
                dve.wait_ge(st_kr, nth(c - 1, 1, 0) * 16)
                dve.tensor_tensor(kr_t[:, 2, 0:width], kr_t[:, 0, 0:width], kr_t[:, 1, 0:width], ALU.add)\
                   .then_inc(kr_ready, 1)
                normalise(c, 0, width)
                normalise(c, 1, width)

            with dve.Fori(0, CHUNKS) as c:
                chunk(c, CW)
            dve.sem_inc(step, 1)
            chunk(SAMPLE_C, SAMPLE, sample=True)

        @block.tensor
        def _(pe):
            pe.sem_inc(unit_done, NU)
            pe.sem_inc(tmp_used, 8)
            pe.wait_ge(cleared, 2)
            pe.wait_ge(split_odd, W_PIECES // 2)

            def squares(c, i, width):
                pe.wait_ge(tmp_lo, nth(c, 8, 4 + i))
                if i % 2 == 0:
                    pe.wait_ge(var_eps, nth(c - 1, 2, i // 2))
                out = ps_stat[i // 2][:, 0:width]
                pe.matmul(out, ones[:, :], t_hi[:, i, 0:width], start=i % 2 == 0, stop=False)
                pe.matmul(out, ones[:, :], t_lo[:, i, 0:width], start=False, stop=i % 2 == 1).then_inc(tmp_used, 1)

            def pooling(c, i, width):
                pe.wait_ge(tmp_lo, nth(c, 8, i))
                pe.wait_ge(pool_ev, nth(c, 4, i - 2))
                product(pe, ps_pool[i % 2][:, 0:width], (wp_hi[:, 3 - i, :], wp_lo[:, 3 - i, :]),
                        (t_hi[:, i, 0:width], t_lo[:, i, 0:width]), True, True).then_inc(tmp_used, 1)

            def chunk(c, par, width):
                for n in range(NU):
                    if n in (6, 7):
                        pooling(c, 2 * n - 12, width)
                        pooling(c, 2 * n - 11, width)
                    if n == 8:
                        squares(c, 0, width)
                        squares(c, 1, width)
                    m = 64 if UNITS[n] == "kr" else P
                    b = UNIT_BANK[n]
                    if n == 0:
                        pe.wait_ge(kr_mul, nth(c - 1, 2, 1))
                    elif n < 4:
                        pe.wait_ge(evac, nth(c - 1, 8, 4 + n))
                        pe.wait_ge(squared, nth(c - 1, 4, n))
                    else:
                        pe.wait_ge(evac, nth(c, 8, n - 4))
                    if n == 8:
                        pe.wait_ge(squared, nth(c, 4, 0))
                    for k in range(KD):
                        if n == 0:
                            pe.wait_ge(split_lo, x_piece(c, k) + 1)
                        mm = product(pe, ps[b][0:m, 0:width], unit_w(n, k),
                                     (x_hi[:, par, k, 0:width], x_lo[:, par, k, 0:width]), k == 0, k == KD - 1)
                    mm.then_inc(unit_done, 1)
                squares(c, 2, width)
                squares(c, 3, width)

            with pe.Fori(0, CHUNKS // 2) as it:
                chunk(2 * it, 0, CW)
                chunk(2 * it + 1, 1, CW)
            chunk(SAMPLE_C, 0, SAMPLE)



HD_W = 8


def phase_heads(nc, g):
    with ExitStack() as ctx:
        ar = Arena(nc, ctx, "hd")
        sb, bank, sem = ar.sb, ar.bank, ar.sem
        raw = sb("raw", [P, HD_W, CW])
        wq_hi, wq_lo = sb("wq_hi", [P, HEADS, 2, P], F32R), sb("wq_lo", [P, HEADS, 2, P], F32R)
        wk_hi, wk_lo = sb("wk_hi", [P, HEADS // 2, 2, P], F32R), sb("wk_lo", [P, HEADS // 2, 2, P], F32R)
        wv_hi, wv_lo = sb("wv_hi", [P, 2, MLA], F32R), sb("wv_lo", [P, 2, MLA], F32R)
        x_hi, x_lo = sb("x_hi", [P, 2, 4, CW], F32R), sb("x_lo", [P, 2, 4, CW], F32R)
        trig = sb("trig", [P, CW])
        rot = sb("rot", [P, 2, CW])
        out = sb("out", [P, 4, CW])
        ps = [bank(f"ps{i}") for i in range(8)]

        landed = [sem(f"landed{i}") for i in range(HD_W)]
        trig_in, met = sem("trig_in"), sem("met")
        split_hi, split_lo = sem("split_hi"), sem("split_lo")
        split_odd = sem("split_odd")
        done = sem("done")
        copied = sem("copied")
        turned = sem("turned")
        rotated = sem("rotated")
        stored = [sem(f"stored{i}") for i in range(4)]

        w_dst = []
        for i in range(4):
            w_dst.append((wq_hi[:, 2 * i:2 * i + 2], wq_lo[:, 2 * i:2 * i + 2]))
        for i in range(2):
            w_dst.append((wk_hi[:, 2 * i:2 * i + 2], wk_lo[:, 2 * i:2 * i + 2]))
        for i in range(2):
            w_dst.append((wv_hi[:, i:i + 1, :], wv_lo[:, i:i + 1, :]))

        def flat(ap):
            return ap.rearrange("p a b c -> p (a b c)") if len(ap.shape) == 4 else ap.rearrange("p a b -> p (a b)")

        block = ctx.enter_context(nc.Block())

        @block.sync
        def _(sp):
            for i in range(4):
                sp.sem_inc(stored[i], 16 * 4)

            def load(c, width, pieces, first=False):
                for k in range(pieces):
                    if not first:
                        sp.wait_ge(split_lo, HD_W + 4 * c - 4 + k + 1)
                    elif k % 2:
                        sp.wait_ge(split_odd, k // 2 + 1)
                    else:
                        sp.wait_ge(split_lo, k + 1)
                    src = (g["qn_t"], g["c_t"])[k // 2]
                    sp.dma_start(raw[:, k, 0:width], src[(k % 2) * P:(k % 2 + 1) * P, ds(c * CW, width)])\
                      .then_inc(landed[k], 16)

            def load_trig(c):
                sp.dma_start(trig[64:128, :], g["trig_k"][:, ds(c * CW, CW)]).then_inc(trig_in, 16)

            def store(c, width, n):
                if n < 8:
                    sp.wait_ge(rotated, nth(c, 8, n))
                    take(sp, met)
                sp.wait_ge(copied, nth(c, 16, n))
                if n < 8:
                    dst, src = g["q_t"][n * 96:(n + 1) * 96, ds(c * CW, width)], out[0:96, n % 4, 0:width]
                elif n < 12:
                    dst, src = g["k_t"][(n - 8) * P:(n - 7) * P, ds(c * CW, width)], out[:, n % 4, 0:width]
                else:
                    dst, src = g["v"][ds(c * CW + (n - 12) * P, P), :], out[:, n % 4, :]
                sp.dma_start(dst, src).then_inc(stored[n % 4], 16)

            for m in range(HD_W):
                sp.dma_start(raw[:, m, :], g["w_hd_p"][m]).then_inc(landed[m], 16)
            load(0, CW, 4, first=True)
            load_trig(0)
            with sp.Fori(0, CHUNKS - 1) as c:
                load(c + 1, CW, 4)
                for n in range(16):
                    store(c, CW, n)
                    if n == 7:
                        load_trig(c + 1)
            load(CHUNKS, SAMPLE, 2)
            for n in range(16):
                store(CHUNKS - 1, CW, n)
                if n == 7:
                    load_trig(CHUNKS)
            for n in range(8):
                store(CHUNKS, SAMPLE, n)
            for i in range(4):
                sp.wait_ge(stored[i], (nth(CHUNKS - 1, 4, 3) + 2) * 16)

        @block.gpsimd
        def _(pool):
            for m in range(0, HD_W, 2):
                hi, lo = w_dst[m]
                pool.wait_ge(split_hi, m + 1)
                pool.tensor_tensor(flat(lo), raw[:, m, :], f32(flat(hi)), ALU.subtract).then_inc(split_lo, 2)

            def split(c, par, width, pieces):
                for k in range(pieces):
                    pool.wait_ge(split_hi, HD_W + 4 * c + k + 1)
                    pool.tensor_tensor(x_lo[:, par, k, 0:width], raw[:, k, 0:width], f32(x_hi[:, par, k, 0:width]),
                                       ALU.subtract).then_inc(split_lo, 1)
            split(0, 0, CW, 4)
            with pool.Fori(0, CHUNKS // 2 - 1) as it:
                split(2 * it + 1, 1, CW, 4)
                split(2 * it + 2, 0, CW, 4)
            split(CHUNKS - 1, 1, CW, 4)
            split(CHUNKS, 0, SAMPLE, 2)

        @block.scalar
        def _(act):
            act.sem_inc(copied, 16)
            for m in range(HD_W):
                act.wait_ge(landed[m], 16)
                act.activation(flat(w_dst[m][0]), raw[:, m, :], ACT.Copy).then_inc(split_hi, 1)

            def split(c, par, width, pieces):
                for k in range(pieces):
                    act.wait_ge(landed[k], 16 * (c + 2))
                    if k == 0:
                        act.wait_ge(done, nth(c - 2, 16, 15))
                    act.activation(x_hi[:, par, k, 0:width], raw[:, k, 0:width], ACT.Copy).then_inc(split_hi, 1)

            def copy(c, n, width):
                act.wait_ge(done, nth(c, 16, n))
                act.wait_ge(stored[n % 4], nth(c, 4, n // 4 - 1) * 16)
                rows = NOPE if n < 8 else P
                act.activation(out[0:rows, n % 4, 0:width], ps[n % 8][0:rows, 0:width], ACT.Copy)\
                   .then_inc(copied, 1)

            def chunk(c, par, width, following):
                if following is not None:
                    split(c + 1, 1 - par, *following)
                for n in range(16 if width == CW else 8):
                    copy(c, n, width)

            for k in range(4):
                act.wait_ge(landed[k], 32)
                act.activation(x_hi[:, 0, k, :], raw[:, k, :], ACT.Copy).then_inc(split_hi, 1)
            with act.Fori(0, CHUNKS // 2 - 1) as it:
                chunk(2 * it, 0, CW, (CW, 4))
                chunk(2 * it + 1, 1, CW, (CW, 4))
            chunk(CHUNKS - 2, 0, CW, (CW, 4))
            chunk(CHUNKS - 1, 1, CW, (SAMPLE, 2))
            chunk(CHUNKS, 0, SAMPLE, None)

        @block.vector
        def _(dve):
            dve.sem_inc(turned, 16)
            dve.sem_inc(rotated, 8)
            for m in range(1, HD_W, 2):
                hi, lo = w_dst[m]
                dve.wait_ge(split_hi, m + 1)
                dve.tensor_tensor(flat(lo), raw[:, m, :], f32(flat(hi)), ALU.subtract).then_inc(split_odd, 1)

            def chunk(c, width):
                dve.wait_ge(trig_in, (c + 1) * 16)
                for n in range(8):
                    dve.wait_ge(done, nth(c, 16, n))
                    dve.wait_ge(rotated, nth(c, 8, n - 1))
                    dve.tensor_tensor(rot[64:96, 0, 0:width], ps[n][64:96, 0:width], trig[64:96, 0:width],
                                      ALU.mult).then_inc(turned, 1)
                    dve.tensor_tensor(rot[64:96, 1, 0:width], ps[n][96:128, 0:width], trig[96:128, 0:width],
                                      ALU.mult).then_inc(turned, 1)
                    dve.wait_ge(turned, nth(c, 16, 2 * n + 1))
                    dve.wait_ge(stored[n % 4], nth(c, 4, n // 4 - 1) * 16)
                    dve.tensor_tensor(out[64:96, n % 4, 0:width], rot[64:96, 0, 0:width], rot[64:96, 1, 0:width],
                                      ALU.add).then_inc(rotated, 1)

            with dve.Fori(0, CHUNKS) as c:
                chunk(c, CW)
            chunk(CHUNKS, SAMPLE)

        @block.tensor
        def _(pe):
            pe.sem_inc(done, 16)
            pe.wait_ge(split_odd, HD_W // 2)

            def chunk(c, par, width):
                def x(k, a=0, b=width):
                    return x_hi[:, par, k, a:b], x_lo[:, par, k, a:b]
                for n in range(16 if width == CW else 8):
                    if n == 0:
                        pe.wait_ge(split_lo, HD_W + 4 * c + 2)
                    if n == 8:
                        pe.wait_ge(split_lo, HD_W + 4 * c + 4)
                    if n < 8:
                        pe.wait_ge(copied, nth(c - 1, 16, n + 8))
                    else:
                        pe.wait_ge(copied, nth(c, 16, n - 8))
                        pe.wait_ge(turned, nth(c, 16, 2 * (n - 8) + 1))
                    for k in range(2):
                        if n < 8:
                            w, m = (wq_hi[:, n, k, :], wq_lo[:, n, k, :]), x(k)
                        elif n < 12:
                            w, m = (wk_hi[:, n - 8, k, :], wk_lo[:, n - 8, k, :]), x(2 + k)
                        else:
                            t = n - 12
                            w, m = x(2 + k, t * P, (t + 1) * P), (wv_hi[:, k, :], wv_lo[:, k, :])
                        o = ps[n % 8][:, 0:CW if n >= 12 else width]
                        mm = product(pe, o, w, m, k == 0, k == 1)
                    mm.then_inc(done, 1)

            with pe.Fori(0, CHUNKS // 2) as it:
                chunk(2 * it, 0, CW)
                chunk(2 * it + 1, 1, CW)
            chunk(CHUNKS, 0, SAMPLE)


QT = SEQ // P
TILES = 2 * QT
NCH = [t % QT // 4 + 1 for t in range(TILES)]
BASE = [sum(NCH[:t]) for t in range(TILES + 1)]
SBANKS = 4
STEPS = TILES + 5


def slots(k):
    return max([NCH[t] for t in (k, k - 2) if 0 <= t < TILES] + [1])


def value_parts(k, slot):
    j = k // 2 - 2
    if not 0 <= j < QT:
        return None, ()
    total = slots(2 * j + 4) + slots(2 * j + 5)
    n = 2 * (j % 8) + 2
    i = slot + (slots(2 * j + 4) if k % 2 else 0)
    return j, range(n * i // total, n * (i + 1) // total)
QB = 256
PIECES = (("k", 0), ("q", 0), ("v", 0), ("k", 1), ("q", 1), ("k", 2), ("q", 2), ("k", 3), ("q", 3))


def phase_attend(nc, g):
    with ExitStack() as ctx:
        ar = Arena(nc, ctx, "at")
        sb, bank, sem = ar.sb, ar.bank, ar.sem
        raw_k = sb("raw_k", [NOPE + ROPE, SEQ])
        raw_q = sb("raw_q", [NOPE + ROPE, SEQ])
        raw_v = sb("raw_v", [P, QT, VD])
        k_hi, k_lo = sb("k_hi", [96, 2, SEQ], F32R), sb("k_lo", [96, 2, SEQ], F32R)
        q_hi, q_lo = sb("q_hi", [96, 2, SEQ], F32R), sb("q_lo", [96, 2, SEQ], F32R)
        v_hi, v_lo = sb("v_hi", [P, 2, QT, VD], F32R), sb("v_lo", [P, 2, QT, VD], F32R)
        p = sb("p", [P, 2, SEQ])
        pt_hi, pt_lo = sb("pt_hi", [P, 2, QT, QB], F32R), sb("pt_lo", [P, 2, QT, QB], F32R)
        part = sb("part", [P, 2, 4])
        total = sb("total", [P, 2])
        rec = sb("rec", [P, 4])
        rec_row = sb("rec_row", [VD, QB])
        out = sb("out", [VD, 2, QB])
        ident = sb("ident", [P, P])
        neg_max = sb("neg_max", [P, 2, 4])
        neg_all = sb("neg_all", [P, 2])
        bias = sb("bias", [P, 2])
        ps_s = [bank(f"s{i}") for i in range(SBANKS)]
        ps_t = [bank("t0"), bank("t1")]
        ps_o = [bank("o0"), bank("o1")]

        k_in, q_in, v_in = sem("k_in"), sem("q_in"), sem("v_in")
        const_in, kr_in = sem("const_in"), sem("kr_in")
        kr_hi, kr_lo = sem("kr_hi"), sem("kr_lo")
        split_hi, split_lo = sem("split_hi"), sem("split_lo")
        scored = sem("scored")
        masked = sem("masked")
        reduced = sem("reduced")
        max_of = sem("max_of")
        biased = sem("biased")
        expd = sem("expd")
        turned = sem("turned")
        pthi, ptlo = sem("pthi"), sem("ptlo")
        summed = sem("summed")
        totalled, recd = sem("totalled"), sem("recd")
        rowed = sem("rowed")
        normed = sem("normed")
        stored = [sem("stored0"), sem("stored1")]

        def head_piece(h, s):
            return h * len(PIECES) + s + 1

        PAIRS = HEADS // 2
        block = ctx.enter_context(nc.Block())

        def width(t, c):
            return CW if c < NCH[t] - 1 else (t % 4 + 1) * P

        @block.sync
        def _(sp):
            for s in stored:
                sp.sem_inc(s, 16 * 8)

            def load(h):
                sp.dma_start(raw_k[0:NOPE, :], g["k_t"][ds(h * NOPE, NOPE), :]).then_inc(k_in, 16)
                sp.dma_start(raw_q[:, :], g["q_t"][ds(h * 96, 96), 0:SEQ]).then_inc(q_in, 16)
                sp.dma_start(raw_v[:, :, :], g["v"].rearrange("(t p) n -> p t n", p=P)[:, :, ds(h * VD, VD)])\
                  .then_inc(v_in, 16)

            sp.dma_start(raw_k[NOPE:96, :], g["kr_t"][:, 0:SEQ]).then_inc(kr_in, 16)
            load(0)
            sp.dma_start(ident[:, :], g["ident"]).then_inc(const_in, 16)
            sp.wait_ge(split_lo, head_piece(0, 8))
            load(1)

            def head(it, u, more):
                for jj in range(8):
                    j = 8 * u + jj
                    if jj == 6 and more:
                        sp.wait_ge(split_lo, head_piece(2 * it + u + 1, 8))
                        load(2 * it + u + 2)
                    sp.wait_ge(normed, nth(it, 16, j))
                    sp.dma_start(g["mix_t"][ds((2 * it + u) * VD, VD), jj * QB:(jj + 1) * QB],
                                 out[:, j % 2, :]).then_inc(stored[j % 2], 16)
            with sp.Fori(0, PAIRS - 1) as it:
                head(it, 0, True)
                head(it, 1, True)
            head(PAIRS - 1, 0, False)
            head(PAIRS - 1, 1, False)
            for s in stored:
                sp.wait_ge(s, nth(PAIRS - 1, 8, 7) * 16)

        def split_ops(u, s):
            kind, c = PIECES[s]
            cols = slice(c * CW, (c + 1) * CW)
            if kind == "k":
                return k_hi[0:NOPE, u, cols], k_lo[0:NOPE, u, cols], raw_k[0:NOPE, cols]
            if kind == "q":
                return q_hi[:, u, cols], q_lo[:, u, cols], raw_q[:, cols]
            return v_hi[:, u], v_lo[:, u], raw_v[:, :, :]

        @block.gpsimd
        def _(pool):
            def head(h, u):
                for s in range(len(PIECES)):
                    hi, lo, src = split_ops(u, s)
                    pool.wait_ge(split_hi, head_piece(h, s))
                    pool.tensor_tensor(lo, src, f32(hi), ALU.subtract).then_inc(split_lo, 1)
            with pool.Fori(0, PAIRS) as it:
                head(2 * it, 0)
                head(2 * it + 1, 1)

        @block.scalar
        def _(act):
            act.sem_inc(expd, BASE[TILES])
            act.sem_inc(pthi, BASE[TILES])
            act.sem_inc(rowed, 16)
            act.wait_ge(kr_in, 16)
            for u in range(2):
                act.activation(k_hi[NOPE:96, u, :], raw_k[NOPE:96, :], ACT.Copy).then_inc(kr_hi, 1)

            def split(h, u, s):
                hi, _, src = split_ops(u, s)
                act.wait_ge({"k": k_in, "q": q_in, "v": v_in}[PIECES[s][0]], (h + 1) * 16)
                act.activation(hi, src, ACT.Copy).then_inc(split_hi, 1)

            for s in range(len(PIECES)):
                split(0, 0, s)

            def turn(it, more):
                for k in range(STEPS):
                    e, t = k - 1, k - 2
                    for c in range(4):
                        if 0 <= t < TILES and c < NCH[t]:
                            n, j = BASE[t] + c, t // 2
                            w = width(t, c)
                            act.wait_ge(turned, nth(it, BASE[TILES], n))
                            if c == 0 and t % 2 == 0:
                                act.wait_ge(summed, nth(it, 16, j - 2))
                            act.activation(pt_hi[:, j % 2, 4 * c:4 * c + w // P, t % 2 * P:t % 2 * P + P],
                                           ps_t[n % 2][:, 0:w].rearrange("p (a b) -> p a b", b=P),
                                           ACT.Copy).then_inc(pthi, 1)
                        if 0 <= e < TILES and c < NCH[e]:
                            n = BASE[e] + c
                            w = width(e, c)
                            if c == 0:
                                act.wait_ge(biased, nth(it, TILES, e))
                                act.wait_ge(totalled, nth(it, TILES, e - 2))
                                act.wait_ge(turned, nth(it, BASE[TILES], BASE[e - 1] - 1 if e >= 2 else
                                                        [-1 - NCH[TILES - 1], -1][e]))
                            act.activation(p[:, e % 2, c * CW:c * CW + w], ps_s[n % SBANKS][:, 0:w], ACT.Exp,
                                           bias=bias[:, e % 2:e % 2 + 1], scale=SCALE,
                                           accum_out=part[:, e % 2, c:c + 1]).then_inc(expd, 1)
                        if c == 0 and k % 2 == 0 and k >= 6:
                            j = (k - 6) // 2
                            act.wait_ge(summed, nth(it, 16, j))
                            act.wait_ge(normed, nth(it, 16, j - 1))
                            act.activation(rec_row[:, :], ps_o[j % 2][0:VD, QB:2 * QB], ACT.Copy).then_inc(rowed, 1)
                    i = k % QT
                    if k < TILES and 6 <= i < 6 + len(PIECES) and (k < QT or more):
                        u, s = k // QT, i - 6
                        if s == 0:
                            act.wait_ge(scored, nth(it, BASE[TILES], BASE[QT * u] - 1))
                            act.wait_ge(summed, nth(it, 16, 8 * u - 1))
                        split(2 * it + u + 1, 1 - u, s)

            with act.Fori(0, PAIRS - 1) as it:
                turn(it, True)
            turn(PAIRS - 1, False)

        @block.vector
        def _(dve):
            for s, n in ((masked, TILES), (reduced, BASE[TILES]), (max_of, TILES), (biased, TILES),
                         (ptlo, BASE[TILES]), (totalled, TILES), (recd, TILES), (normed, 16)):
                dve.sem_inc(s, n)
            dve.wait_ge(kr_hi, 2)
            for u in range(2):
                dve.tensor_tensor(k_lo[NOPE:96, u, :], raw_k[NOPE:96, :], f32(k_hi[NOPE:96, u, :]),
                                  ALU.subtract).then_inc(kr_lo, 1)

            def reciprocals(it, t):
                dve.wait_ge(expd, nth(it, BASE[TILES], BASE[t + 1] - 1))
                dve.wait_ge(recd, nth(it, TILES, t - 2))
                dve.tensor_reduce(total[:, t % 2:t % 2 + 1], part[:, t % 2, 0:NCH[t]], AX.X, ALU.add)\
                   .then_inc(totalled, 1)
                dve.wait_ge(totalled, nth(it, TILES, t))
                dve.wait_ge(summed, nth(it, 16, t // 2 - 2))
                dve.reciprocal(rec[:, t % 4:t % 4 + 1], total[:, t % 2:t % 2 + 1]).then_inc(recd, 1)

            def finish(it, j):
                dve.wait_ge(rowed, nth(it, 16, j))
                dve.wait_ge(stored[j % 2], nth(it, 8, j // 2 - 1) * 16)
                dve.tensor_tensor(out[:, j % 2, :], ps_o[j % 2][0:VD, 0:QB], rec_row[:, :], ALU.mult)\
                   .then_inc(normed, 1)

            def turn(it):
                for k in range(STEPS):
                    t = k - 2
                    for slot in range(5):
                        c = slot
                        if 0 <= t < TILES and c < NCH[t]:
                            n, j, w = BASE[t] + c, t // 2, width(t, c)
                            dve.wait_ge(pthi, nth(it, BASE[TILES], n))
                            at = (slice(None), j % 2, slice(4 * c, 4 * c + w // P), slice(t % 2 * P, t % 2 * P + P))
                            dve.tensor_tensor(pt_lo[at], ps_t[n % 2][:, 0:w].rearrange("p (a b) -> p a b", b=P),
                                              f32(pt_hi[at]), ALU.subtract).then_inc(ptlo, 1)
                        c = slot - 1
                        if k < TILES and 0 <= c < NCH[k]:
                            n, w = BASE[k] + c, width(k, c)
                            s = ps_s[n % SBANKS]
                            dve.wait_ge(scored, nth(it, BASE[TILES], n))
                            if c == NCH[k] - 1:
                                dve.memset(s[0:64, w - 64:w], NEG).then_inc(masked, 1)
                                dve.wait_ge(masked, nth(it, TILES, k))
                            if c == 0:
                                dve.wait_ge(max_of, nth(it, TILES, k - 2))
                            dve.tensor_reduce(neg_max[:, k % 2, c:c + 1], s[:, 0:w], AX.X, ALU.max, negate=True)\
                               .then_inc(reduced, 1)
                        if k < TILES and c == NCH[k] - 1:
                            dve.wait_ge(reduced, nth(it, BASE[TILES], BASE[k] + c))
                            dve.wait_ge(biased, nth(it, TILES, k - 1))
                            dve.tensor_reduce(neg_all[:, k % 2:k % 2 + 1], neg_max[:, k % 2, 0:NCH[k]], AX.X, ALU.min)\
                               .then_inc(max_of, 1)
                            dve.wait_ge(max_of, nth(it, TILES, k))
                            dve.wait_ge(expd, nth(it, BASE[TILES], BASE[k - 1] - 1 if k >= 2 else
                                                  [-1 - NCH[TILES - 1], -1][k]))
                            dve.tensor_scalar(bias[:, k % 2:k % 2 + 1], neg_all[:, k % 2:k % 2 + 1], SCALE, None,
                                              ALU.mult).then_inc(biased, 1)
                        if 0 <= t < TILES and c == 0:
                            reciprocals(it, t)
                        if c == 0 and k % 2 == 0 and k >= 6:
                            finish(it, (k - 6) // 2)
            with dve.Fori(0, PAIRS) as it:
                turn(it)

        @block.tensor
        def _(pe):
            pe.sem_inc(scored, BASE[TILES])
            pe.sem_inc(turned, BASE[TILES])
            pe.sem_inc(summed, 16)
            pe.wait_ge(const_in, 16)
            pe.wait_ge(kr_lo, 2)

            def scores(it, t, c):
                u, i = t // QT, t % QT
                n, w = BASE[t] + c, width(t, c)
                if i % 4 == 0:
                    s = max(PIECES.index(("k", c)), PIECES.index(("q", i // 4)))
                    pe.wait_ge(split_lo, head_piece(2 * it + u, s))
                pe.wait_ge(expd, nth(it, BASE[TILES], n - SBANKS))
                rows, cols = slice(i * P, (i + 1) * P), slice(c * CW, c * CW + w)
                product(pe, ps_s[n % SBANKS][:, 0:w], (q_hi[:, u, rows], q_lo[:, u, rows]),
                        (k_hi[:, u, cols], k_lo[:, u, cols]), True, True).then_inc(scored, 1)

            def transposes(it, t, c):
                n, w = BASE[t] + c, width(t, c)
                pe.wait_ge(expd, nth(it, BASE[TILES], n))
                pe.wait_ge(ptlo, nth(it, BASE[TILES], n - 2))
                for b in range(w // P):
                    mm = pe.transpose(ps_t[n % 2][:, b * P:(b + 1) * P],
                                      p[:, t % 2, c * CW + b * P:c * CW + (b + 1) * P], ident[:, :])
                mm.then_inc(turned, 1)

            def values(it, j, key_tiles):
                u, last = j // 8, 2 * (j % 8) + 1
                if 0 in key_tiles:
                    pe.wait_ge(ptlo, nth(it, BASE[TILES], BASE[2 * j + 2] - 1))
                    pe.wait_ge(split_lo, head_piece(2 * it + u, 2))
                    pe.wait_ge(normed, nth(it, 16, j - 2))
                for kt in key_tiles:
                    cols = slice(P, QB) if kt == last else slice(0, QB)
                    mm = product(pe, ps_o[j % 2][0:VD, cols], (v_hi[:, u, kt, :], v_lo[:, u, kt, :]),
                                 (pt_hi[:, j % 2, kt, cols], pt_lo[:, j % 2, kt, cols]), kt == 0, kt == last,
                                 skip_group_check=True)
                if last in key_tiles:
                    for i in range(2):
                        pe.wait_ge(recd, nth(it, TILES, 2 * j + i))
                        t = (2 * j + i) % 4
                        mm = pe.matmul(ps_o[j % 2][0:VD, QB + i * P:QB + (i + 1) * P],
                                       rec[:, t:t + 1].to_broadcast([P, VD]), ident[:, :], start=False, stop=i == 1,
                                       skip_group_check=True)
                    mm.then_inc(summed, 1)

            with pe.Fori(0, PAIRS) as it:
                for k in range(STEPS):
                    for c in range(slots(k) + 1):
                        if 2 <= k < TILES + 2 and c < NCH[k - 2]:
                            transposes(it, k - 2, c)
                        j, key_tiles = value_parts(k, c) if c < slots(k) else (None, ())
                        if key_tiles:
                            values(it, j, key_tiles)
                        if k < TILES and 0 < c <= NCH[k]:
                            scores(it, k, c - 1)



KEYS = PAST + NEW
KT = PAST // P


def phase_sample(nc, g):
    assert KEYS // 64 == PAST // 64
    with ExitStack() as ctx:
        ar = Arena(nc, ctx, "sa")
        sb, bank, sem = ar.sb, ar.bank, ar.sem
        uk_raw, uv_raw = sb("uk_raw", [NOPE, HEADS, LORA]), sb("uv_raw", [P, 2, HEADS, VD])
        uk_hi, uk_lo = sb("uk_hi", [NOPE, HEADS, LORA], F32R), sb("uk_lo", [NOPE, HEADS, LORA], F32R)
        uv_hi, uv_lo = sb("uv_hi", [P, 2, HEADS, VD], F32R), sb("uv_lo", [P, 2, HEADS, VD], F32R)
        qn_raw = sb("qn_raw", [NOPE, HEADS, SAMPLE])
        qn_hi, qn_lo = sb("qn_hi", [NOPE, HEADS, SAMPLE], F32R), sb("qn_lo", [NOPE, HEADS, SAMPLE], F32R)
        qr_raw = sb("qr_raw", [ROPE, HEADS, SAMPLE])
        q_lat = sb("q_lat", [P, 2, HEADS, SAMPLE])
        ident = sb("ident", [P, P])
        k_raw, v_raw, r_raw = sb("k_raw", [P, 2, 2, KEYS]), sb("v_raw", [P, 2, KT, LORA]), sb("r_raw", [ROPE, 2, KEYS])
        k_hi, k_lo = sb("k_hi", [P, 2, 2, KEYS], F32R), sb("k_lo", [P, 2, 2, KEYS], F32R)
        v_hi, v_lo = sb("v_hi", [P, 2, KT, LORA], F32R), sb("v_lo", [P, 2, KT, LORA], F32R)
        r_hi, r_lo = sb("r_hi", [ROPE, 2, KEYS], F32R), sb("r_lo", [ROPE, 2, KEYS], F32R)
        q_hi, q_lo = sb("q_hi", [P, 2, 2, HEADS, NEW], F32R), sb("q_lo", [P, 2, 2, HEADS, NEW], F32R)
        p_hi, p_lo = sb("p_hi", [ROPE, 2, HEADS, NEW], F32R), sb("p_lo", [ROPE, 2, HEADS, NEW], F32R)
        n_hi, n_lo = sb("n_hi", [NEW, 2, LORA], F32R), sb("n_lo", [NEW, 2, LORA], F32R)
        prob = sb("prob", [P, 2, KEYS])
        pt_hi, pt_lo = sb("pt_hi", [P, 2, KT, P], F32R), sb("pt_lo", [P, 2, KT, P], F32R)
        pn_hi, pn_lo = sb("pn_hi", [NEW, 2, P], F32R), sb("pn_lo", [NEW, 2, P], F32R)
        l_hi, l_lo = sb("l_hi", [P, 2, HEADS, SAMPLE], F32R), sb("l_lo", [P, 2, HEADS, SAMPLE], F32R)
        out = sb("out", [VD, HEADS, SAMPLE])
        stat = sb("stat", [P, 2, 8])
        ps_q, ps_new, ps_s, ps_sn, ps_t, ps_tn, ps_l, ps_o = (bank(n) for n in
                                                              ("q", "new", "s", "sn", "t", "tn", "l", "o"))

        const_in, met = sem("const_in"), sem("met")
        row_in = [sem("row_in0"), sem("row_in1")]
        w_hi, w_lo = sem("w_hi"), sem("w_lo")
        lat_q, lat_copied = sem("lat_q"), sem("lat_copied")
        split_hi, split_lo = sem("split_hi"), sem("split_lo")
        vhi, vlo = sem("vhi"), sem("vlo")
        new_turned, nhi, nlo = sem("new_turned"), sem("nhi"), sem("nlo")
        scored, maxed, least, biased = sem("scored"), sem("maxed"), sem("least"), sem("biased")
        expd, summed, recd, normed = sem("expd"), sem("summed"), sem("recd"), sem("normed")
        turned, thi, tlo = sem("turned"), sem("thi"), sem("tlo")
        mixed, lhi, llo = sem("mixed"), sem("lhi"), sem("llo")
        valued, copied, stored = sem("valued"), sem("copied"), sem("stored")
        LOADS = 6

        block = ctx.enter_context(nc.Block())

        @block.sync
        def _(sp):
            for dst, src in ((uk_raw[:, :, :], g["w_uk_p"]), (uv_raw[:, :, :, :], g["w_uv_p"]),
                             (ident[:, :], g["ident"])):
                sp.dma_start(dst, src).then_inc(const_in, 16)
            q = g["q_t"].rearrange("(h r) t -> r h t", r=NOPE + ROPE)
            sp.dma_start(qn_raw[:, :, :], q[0:NOPE, :, SEQ:TOK]).then_inc(const_in, 16)
            sp.dma_start(qr_raw[:, :, :], q[NOPE:NOPE + ROPE, :, SEQ:TOK]).then_inc(const_in, 16)

            def load(row, u):
                new = ds(SEQ + row * NEW, NEW)
                s = row_in[u]
                sp.dma_start(k_raw[:, u, :, 0:PAST], g["ckv_t"].rearrange("b p a t -> p b a t")[:, ds(row, 1)])\
                  .then_inc(s, 16)
                sp.dma_start(k_raw[:, u, :, PAST:KEYS], g["c_t"].rearrange("(a p) t -> p a t", p=P)[:, :, new])\
                  .then_inc(s, 16)
                sp.dma_start(r_raw[:, u, 0:PAST], g["krope_t"].rearrange("b p t -> p b t")[:, ds(row, 1)])\
                  .then_inc(s, 16)
                sp.dma_start(r_raw[:, u, PAST:KEYS], g["kr_t"][:, new]).then_inc(s, 16)
                for half in range(2):
                    sp.dma_start(v_raw[:, u, 2 * half:2 * half + 2, :],
                                 g["ckv"].rearrange("b p a l -> p b a l")[:, ds(row, 1), 2 * half:2 * half + 2])\
                      .then_inc(s, 16)

            def reload(row, u):
                sp.wait_ge(split_lo, at(row - 2, 4, 3))
                take(sp, met)
                sp.wait_ge(vlo, at(row - 2, 1, 0))
                sp.wait_ge(new_turned, at(row - 2, 1, 0))
                take(sp, met)
                load(row, u)

            load(0, 0)
            load(1, 1)
            reload(2, 0)
            with sp.Fori(0, ROWS // 2 - 2) as it:
                for u in range(2):
                    reload(2 * it + u + 3, 1 - u)
            reload(ROWS - 1, 1)
            sp.wait_ge(copied, 2)
            sp.dma_start(g["mix_t"][0:MLA, SEQ:TOK].rearrange("(h v) t -> v h t", v=VD), out[:, :, :])\
              .then_inc(stored, 16)
            sp.wait_ge(stored, 16)

        def splits(row, u):
            new = ds(row * NEW, NEW)
            return ((k_hi[:, u], k_lo[:, u], k_raw[:, u]), (r_hi[:, u], r_lo[:, u], r_raw[:, u]),
                    (q_hi[:, u], q_lo[:, u], q_lat[:, :, :, new]), (p_hi[:, u], p_lo[:, u], qr_raw[:, :, new]))

        @block.gpsimd
        def _(pool):
            pool.sem_inc(split_lo, 8)
            for i, (lo, raw, hi) in enumerate(((uk_lo, uk_raw, uk_hi), (qn_lo, qn_raw, qn_hi), (uv_lo, uv_raw, uv_hi))):
                pool.wait_ge(w_hi, i + 1)
                pool.tensor_tensor(lo[:], raw[:], f32(hi[:]), ALU.subtract).then_inc(w_lo, 1)
            with pool.Fori(0, ROWS // 2) as it:
                for u in range(2):
                    for k, (hi, lo, raw) in enumerate(splits(2 * it + u, u)):
                        pool.wait_ge(split_hi, at(2 * it + u, 4, k))
                        pool.tensor_tensor(lo, raw, f32(hi), ALU.subtract).then_inc(split_lo, 1)

        @block.scalar
        def _(act):
            for s, n in ((split_hi, 4), (vhi, 1), (nhi, 1), (expd, 2), (thi, 2), (lhi, 1)):
                act.sem_inc(s, 2 * n)
            act.wait_ge(const_in, 80)
            for hi, raw in ((uk_hi, uk_raw), (qn_hi, qn_raw), (uv_hi, uv_raw)):
                act.activation(hi[:], raw[:], ACT.Copy).then_inc(w_hi, 1)
            def keys(row, u, fill, parts=slice(0, 4)):
                act.wait_ge(row_in[u], fill * 16 * LOADS)
                act.wait_ge(scored, at(row - 2, 1, 0))
                for hi, _, raw in splits(row, u)[parts]:
                    act.activation(hi, raw, ACT.Copy).then_inc(split_hi, 1)

            def values(row, u):
                act.wait_ge(mixed, at(row - 2, 1, 0))
                act.activation(v_hi[:, u], v_raw[:, u], ACT.Copy).then_inc(vhi, 1)
                act.wait_ge(new_turned, at(row, 1, 0))
                act.activation(n_hi[:, u, :], ps_new[0:NEW, 0:LORA], ACT.Copy).then_inc(nhi, 1)

            def exps(row, u):
                act.wait_ge(biased, at(row, 1, 0))
                act.wait_ge(turned, at(row - 2, 1, 0))
                for i, (src, a, b) in enumerate(((ps_s, 0, PAST), (ps_sn, PAST, KEYS))):
                    act.activation(prob[:, u, a:b], src[:, 0:b - a], ACT.Exp, bias=stat[:, u, 3:4], scale=SCALE)\
                       .then_inc(expd, 1)

            def step(row, u, fill, ahead=2):
                if ahead:
                    values(row + 1, 1 - u)
                act.wait_ge(turned, at(row, 1, 0))
                act.activation(pt_hi[:, u], ps_t[:, :].rearrange("p (a b) -> p a b", b=P), ACT.Copy).then_inc(thi, 1)
                act.activation(pn_hi[:, u, :], ps_tn[0:NEW, 0:P], ACT.Copy).then_inc(thi, 1)
                if ahead:
                    exps(row + 1, 1 - u)
                if ahead == 2:
                    keys(row + 2, u, fill + 1)
                act.wait_ge(mixed, at(row, 1, 0))
                take(act, met)
                act.activation(l_hi[:, :, :, ds(row * NEW, NEW)],
                               ps_l[:, 0:2 * P].rearrange("p (a h t) -> p a h t", a=2, t=NEW), ACT.Copy).then_inc(lhi, 1)

            keys(0, 0, 1, slice(0, 2))
            for n in range(4):
                act.wait_ge(lat_q, n + 1)
                act.activation(q_lat[:, n // 2, 4 * (n % 2):4 * (n % 2) + 4, :],
                               (ps_q, ps_s, ps_t, ps_l)[n][:, :].rearrange("p (h t) -> p h t", t=SAMPLE), ACT.Copy)\
                   .then_inc(lat_copied, 1)
            act.wait_ge(lat_copied, 4)
            keys(0, 0, 1, slice(2, 4))
            values(0, 0)
            keys(1, 1, 1)
            exps(0, 0)
            with act.Fori(0, ROWS // 2 - 1) as it:
                step(2 * it, 0, it + 1)
                step(2 * it + 1, 1, it + 1)
            step(ROWS - 2, 0, ROWS // 2, ahead=1)
            step(ROWS - 1, 1, ROWS // 2, ahead=0)
            for i in range(2):
                act.wait_ge(valued, i + 1)
                act.activation(out[:, 4 * i:4 * i + 4, :], (ps_o, ps_new)[i][0:VD, :].rearrange("p (h t) -> p h t", t=SAMPLE),
                               ACT.Copy).then_inc(copied, 1)

        @block.vector
        def _(dve):
            for s, n in ((vlo, 1), (nlo, 1), (maxed, 2), (least, 1), (biased, 1), (summed, 1), (recd, 1),
                         (normed, 1), (tlo, 2), (llo, 1)):
                dve.sem_inc(s, 2 * n)

            def prepare(row, u):
                dve.wait_ge(vhi, at(row, 1, 0))
                dve.tensor_tensor(v_lo[:, u], v_raw[:, u], f32(v_hi[:, u]), ALU.subtract).then_inc(vlo, 1)
                dve.wait_ge(nhi, at(row, 1, 0))
                dve.tensor_tensor(n_lo[:, u, :], ps_new[0:NEW, 0:LORA], f32(n_hi[:, u, :]), ALU.subtract)\
                   .then_inc(nlo, 1)

            def maxima(row, u):
                dve.wait_ge(scored, at(row, 1, 0))
                dve.wait_ge(least, at(row - 2, 1, 0))
                for i, (src, w) in enumerate(((ps_s, PAST), (ps_sn, NEW))):
                    dve.tensor_reduce(stat[:, u, i:i + 1], src[:, 0:w], AX.X, ALU.max, negate=True).then_inc(maxed, 1)
                dve.wait_ge(maxed, at(row, 2, 1))
                dve.wait_ge(biased, at(row - 2, 1, 0))
                dve.tensor_reduce(stat[:, u, 2:3], stat[:, u, 0:2], AX.X, ALU.min).then_inc(least, 1)
                dve.wait_ge(least, at(row, 1, 0))
                dve.wait_ge(expd, at(row - 2, 2, 1))
                dve.tensor_scalar(stat[:, u, 3:4], stat[:, u, 2:3], SCALE, None, ALU.mult).then_inc(biased, 1)

            def normalise(row, u):
                dve.wait_ge(expd, at(row, 2, 1))
                dve.wait_ge(recd, at(row - 2, 1, 0))
                dve.tensor_reduce(stat[:, u, 4:5], prob[:, u, :], AX.X, ALU.add).then_inc(summed, 1)
                dve.wait_ge(summed, at(row, 1, 0))
                dve.wait_ge(normed, at(row - 2, 1, 0))
                dve.reciprocal(stat[:, u, 5:6], stat[:, u, 4:5]).then_inc(recd, 1)
                dve.wait_ge(recd, at(row, 1, 0))
                dve.tensor_scalar(prob[:, u, :], prob[:, u, :], stat[:, u, 5:6], None, ALU.mult).then_inc(normed, 1)

            def lows(row, u):
                dve.wait_ge(thi, at(row, 2, 1))
                dve.tensor_tensor(pt_lo[:, u], ps_t[:, :].rearrange("p (a b) -> p a b", b=P), f32(pt_hi[:, u]),
                                  ALU.subtract).then_inc(tlo, 1)
                dve.tensor_tensor(pn_lo[:, u, :], ps_tn[0:NEW, 0:P], f32(pn_hi[:, u, :]), ALU.subtract)\
                   .then_inc(tlo, 1)

            def latents(row, u):
                dve.wait_ge(lhi, at(row, 1, 0))
                new = ds(row * NEW, NEW)
                dve.tensor_tensor(l_lo[:, :, :, new], ps_l[:, 0:2 * P].rearrange("p (a h t) -> p a h t", a=2, t=NEW),
                                  f32(l_hi[:, :, :, new]), ALU.subtract).then_inc(llo, 1)

            def step(row, u, ahead=True):
                if ahead:
                    prepare(row + 1, 1 - u)
                lows(row, u)
                if ahead:
                    maxima(row + 1, 1 - u)
                latents(row, u)
                if ahead:
                    normalise(row + 1, 1 - u)

            prepare(0, 0)
            maxima(0, 0)
            normalise(0, 0)
            with dve.Fori(0, ROWS // 2 - 1) as it:
                step(2 * it, 0)
                step(2 * it + 1, 1)
            step(ROWS - 2, 0)
            step(ROWS - 1, 1, ahead=False)

        @block.tensor
        def _(pe):
            for s in (new_turned, scored, turned, mixed):
                pe.sem_inc(s, 2)
            pe.wait_ge(w_lo, 2)
            for n in range(4):
                for hh in range(4):
                    h, cols = 4 * (n % 2) + hh, slice(n // 2 * P, n // 2 * P + P)
                    mm = product(pe, (ps_q, ps_s, ps_t, ps_l)[n][:, hh * P:(hh + 1) * P],
                                 (uk_hi[:, h, cols], uk_lo[:, h, cols]), (qn_hi[:, h, :], qn_lo[:, h, :]),
                                 hh == 0, hh == 3, skip_group_check=True)
                mm.then_inc(lat_q, 1)
            pe.wait_ge(lat_copied, 4)
            pe.wait_ge(w_lo, 3)

            def new_tokens(row, u, fill):
                pe.wait_ge(row_in[u], fill * 16 * LOADS)
                pe.wait_ge(nlo, at(row - 1, 1, 0))
                for a in range(2):
                    mm = pe.transpose(ps_new[0:NEW, a * P:(a + 1) * P], k_raw[:, u, a, PAST:KEYS], ident[:, :])
                mm.then_inc(new_turned, 1)

            def scores(row, u):
                pe.wait_ge(split_lo, at(row, 4, 3))
                pe.wait_ge(expd, at(row - 1, 2, 1))
                for dst, a, b in ((ps_s, 0, PAST), (ps_sn, PAST, KEYS)):
                    for lt in range(2):
                        product(pe, dst[:, 0:b - a], (q_hi[:, u, lt], q_lo[:, u, lt]),
                                (k_hi[:, u, lt, a:b], k_lo[:, u, lt, a:b]), lt == 0, False)
                    mm = product(pe, dst[:, 0:b - a], (p_hi[:, u], p_lo[:, u]), (r_hi[:, u, a:b], r_lo[:, u, a:b]),
                                 False, True)
                mm.then_inc(scored, 1)

            def transposes(row, u):
                pe.wait_ge(normed, at(row, 1, 0))
                pe.wait_ge(tlo, at(row - 1, 2, 1))
                for kt in range(KT):
                    pe.transpose(ps_t[:, kt * P:(kt + 1) * P], prob[:, u, kt * P:(kt + 1) * P], ident[:, :])
                pe.transpose(ps_tn[0:NEW, 0:P], prob[:, u, PAST:KEYS], ident[:, :]).then_inc(turned, 1)

            def finish(row, u):
                pe.wait_ge(tlo, at(row, 2, 1))
                pe.wait_ge(vlo, at(row, 1, 0))
                pe.wait_ge(nlo, at(row, 1, 0))
                pe.wait_ge(llo, at(row - 1, 1, 0))
                for lt in range(2):
                    cols = slice(lt * P, (lt + 1) * P)
                    for kt in range(KT):
                        product(pe, ps_l[:, cols], (v_hi[:, u, kt, cols], v_lo[:, u, kt, cols]),
                                (pt_hi[:, u, kt, :], pt_lo[:, u, kt, :]), lt == 0 and kt == 0, False,
                                skip_group_check=True)
                    mm = product(pe, ps_l[:, cols], (n_hi[:, u, cols], n_lo[:, u, cols]),
                                 (pn_hi[:, u, :], pn_lo[:, u, :]), False, lt == 1, skip_group_check=True)
                mm.then_inc(mixed, 1)

            new_tokens(0, 0, 1)
            scores(0, 0)
            with pe.Fori(0, ROWS // 2 - 1) as it:
                for u in range(2):
                    row = 2 * it + u
                    new_tokens(row + 1, 1 - u, it + 1 + u)
                    transposes(row, u)
                    scores(row + 1, 1 - u)
                    finish(row, u)
            new_tokens(ROWS - 1, 1, ROWS // 2)
            transposes(ROWS - 2, 0)
            scores(ROWS - 1, 1)
            finish(ROWS - 2, 0)
            transposes(ROWS - 1, 1)
            finish(ROWS - 1, 1)
            pe.wait_ge(llo, at(ROWS - 1, 1, 0))
            pe.wait_ge(nlo, at(ROWS - 1, 1, 0))
            for i in range(2):
                for hh in range(4):
                    h = 4 * i + hh
                    for lt in range(2):
                        mm = product(pe, (ps_o, ps_new)[i][0:VD, hh * P:(hh + 1) * P],
                                     (uv_hi[:, lt, h, :], uv_lo[:, lt, h, :]), (l_hi[:, lt, h, :], l_lo[:, lt, h, :]),
                                     hh == 0 and lt == 0, hh == 3 and lt == 1, skip_group_check=True)
                mm.then_inc(valued, 1)


TT = TOK // P
LN_EPS = 1e-5


def phase_mix(nc, g):
    with ExitStack() as ctx:
        ar = Arena(nc, ctx, "mx")
        sb, bank, sem = ar.sb, ar.bank, ar.sem
        wo_hi, wo_lo = sb("wo_hi", [P, KD, D], F32R), sb("wo_lo", [P, KD, D], F32R)
        wg_hi, wg_lo = sb("wg_hi", [P, KD, D], F32R), sb("wg_lo", [P, KD, D], F32R)
        we_hi, we_lo = sb("we_hi", [P, 2, D], F32R), sb("we_lo", [P, 2, D], F32R)
        work = sb("work", [P, 4, D])
        m_raw, m_hi, m_lo = sb("m_raw", [P, 2, KD, P]), sb("m_hi", [P, KD, P], F32R), sb("m_lo", [P, KD, P], F32R)
        e_raw, e_hi, e_lo = sb("e_raw", [P, 2, 2, P]), sb("e_hi", [P, 2, 2, P], F32R), sb("e_lo", [P, 2, 2, P], F32R)
        x_raw = sb("x_raw", [P, 2, D])
        t_hi, t_lo = sb("t_hi", [P, KD, P], F32R), sb("t_lo", [P, KD, P], F32R)
        ln_g, ln_b = sb("ln_g", [P, D]), sb("ln_b", [P, D])
        ident = sb("ident", [P, P])
        stats, mv = sb("stats", [P, 2, 12]), sb("mv", [P, 2, 2])
        var_eps, rstd, power = sb("var_eps", [P, 2]), sb("rstd", [P, 2]), sb("power", [P, 1])
        x1_t, gate = work[:, 2, :], work[:, 3, :]
        ps_m = [bank("m0"), bank("m1")]
        ps_t = [bank("t0"), bank("t1")]
        ps_g = [bank("g0"), bank("g1")]
        ps_e = [bank("e0"), bank("e1")]

        const_in, met = sem("const_in"), sem("met")
        w_in = [sem(f"w_in{i}") for i in range(4)]
        whi, wlo_pool, wlo_dve = sem("whi"), sem("wlo_pool"), sem("wlo_dve")
        m_in, x_in = [sem("m_in0"), sem("m_in1")], [sem("x_in0"), sem("x_in1")]
        split_hi, split_lo = sem("split_hi"), sem("split_lo")
        mixed, emb, turned, gated = sem("mixed"), sem("emb"), sem("turned"), sem("gated")
        resid, stat, aggr, eps = sem("resid"), sem("stat"), sem("aggr"), sem("eps")
        rs, scaled = sem("rs"), sem("scaled")
        centred, shifted = sem("centred"), sem("shifted")
        thi, tlo, tcopy = sem("thi"), sem("tlo"), sem("tcopy")
        sig, prod, summed = sem("sig"), sem("prod"), sem("summed")
        powered = sem("powered")
        st_x, st_y = sem("st_x"), sem("st_y")
        W = [(wo_hi[:, k, :], wo_lo[:, k, :]) for k in range(KD)] + [(we_hi[:, k, :], we_lo[:, k, :]) for k in range(2)] \
            + [(wg_hi[:, k, :], wg_lo[:, k, :]) for k in range(KD)]
        H = (slice(0, 512), slice(512, 1024))

        slot = [n % 4 if n < 10 else 1 + (n - 10) % 3 for n in range(len(W))]

        def wait_piece(eng, n):
            eng.wait_ge(wlo_pool, n // 2 + 1)
            if n > 0:
                eng.wait_ge(wlo_dve, (n + 1) // 2)

        block = ctx.enter_context(nc.Block())

        @block.sync
        def _(sp):
            sp.sem_inc(st_x, 16)
            sp.sem_inc(st_y, 16)

            def load_w(n):
                before = [m for m in range(n) if slot[m] == slot[n]]
                if before:
                    m = before[-1]
                    sp.wait_ge(wlo_dve if m % 2 else wlo_pool, m // 2 + 1)
                sp.dma_start(work[:, slot[n], :], g["w_mix_p"][n]).then_inc(w_in[slot[n]], 16)

            def load_m(t, u):
                sp.dma_start(m_raw[:, u], g["mix_t"].rearrange("(k p) t -> p k t", p=P)[:, :, ds(t * P, P)])\
                  .then_inc(m_in[u], 16)
                sp.dma_start(e_raw[:, u], g["pe_t"].rearrange("(k p) t -> p k t", p=P)[:, :, ds(t * P, P)])\
                  .then_inc(m_in[u], 16)

            def load_x(t, u):
                sp.dma_start(x_raw[:, u, :], g["x"][ds(t * P, P), :]).then_inc(x_in[u], 16)

            def store(t):
                sp.wait_ge(tcopy, at(t, 2, 1))
                take(sp, met)
                sp.dma_start(g["x1_t"].rearrange("(k p) t -> p k t", p=P)[:, :, ds(t * P, P)],
                             x1_t.rearrange("p (k t) -> p k t", t=P)).then_inc(st_x, 16)
                sp.wait_ge(summed, at(t, 1, 0))
                sp.dma_start(g["y0"][ds(t * P, P), :], gate).then_inc(st_y, 16)

            for n in range(KD):
                load_w(n)
                if n == 1:
                    load_m(0, 0)
            sp.dma_start(ln_g[:, :], g["ln1_g"]).then_inc(const_in, 16)
            sp.dma_start(ln_b[:, :], g["ln1_b"]).then_inc(const_in, 16)
            sp.dma_start(ident[:, :], g["ident"]).then_inc(const_in, 16)
            load_x(0, 0)
            load_m(1, 1)
            for n in range(KD, len(W)):
                load_w(n)
            sp.wait_ge(split_lo, at(0, 2, 1))
            load_m(2, 0)

            def step(t, u, m, x=True):
                if x:
                    sp.wait_ge(resid, at(t - 1, 2, 1))
                    load_x(t + 1, 1 - u)
                if m:
                    sp.wait_ge(split_lo, at(t + 1, 2, 1))
                    load_m(t + 3, 1 - u)
                store(t)
            with sp.Fori(0, 7) as it:
                step(2 * it, 0, True)
                step(2 * it + 1, 1, True)
            step(TT - 3, 0, False)
            step(TT - 2, 1, False)
            step(TT - 1, 0, False, False)
            sp.wait_ge(st_x, (TT + 1) * 16)
            sp.wait_ge(st_y, (TT + 1) * 16)

        @block.gpsimd
        def _(pool):
            for s, n in ((split_lo, 2), (rs, 1), (scaled, 1)):
                pool.sem_inc(s, 2 * n)

            def weight(n):
                hi, lo = W[n]
                pool.wait_ge(whi, n + 1)
                pool.tensor_tensor(lo, work[:, slot[n], :], f32(hi), ALU.subtract).then_inc(wlo_pool, 1)

            def split(t, u):
                for i, (lo, raw, hi) in enumerate(((m_lo[:], m_raw, m_hi[:]), (e_lo[:, u], e_raw, e_hi[:, u]))):
                    pool.wait_ge(split_hi, at(t, 2, i))
                    pool.tensor_tensor(lo, raw[:, u], f32(hi), ALU.subtract).then_inc(split_lo, 1)

            def normalise(t, u, following=None):
                pool.wait_ge(eps, at(t, 1, 0))
                pool.wait_ge(centred, at(t - 2, 1, 0))
                pool.tensor_tensor(rstd[:, u:u + 1], var_eps[:, u:u + 1], power[:, :], ALU.pow).then_inc(rs, 1)
                if following is not None:
                    split(*following)
                pool.wait_ge(centred, at(t, 1, 0))
                pool.tensor_tensor(work[:, u, :], work[:, u, :], ln_g[:, :], ALU.mult).then_inc(scaled, 1)

            pool.memset(power[:, :], -0.5).then_inc(powered, 1)
            for n in range(0, len(W), 2):
                weight(n)
                if n == 2:
                    split(0, 0)
                if n == 12:
                    split(1, 1)
            pool.wait_ge(const_in, 48)
            pool.wait_ge(powered, 1)
            normalise(0, 0)
            with pool.Fori(0, 7) as it:
                normalise(2 * it + 1, 1, (2 * it + 2, 0))
                normalise(2 * it + 2, 0, (2 * it + 3, 1))
            normalise(TT - 2, 1, (TT - 1, 0))
            normalise(TT - 1, 0)

        @block.scalar
        def _(act):
            for s, n in ((split_hi, 2), (thi, 2), (tcopy, 2), (sig, 2)):
                act.sem_inc(s, 2 * n)

            def weight(n):
                act.wait_ge(w_in[slot[n]], 16 * slot[:n + 1].count(slot[n]))
                act.activation(W[n][0], work[:, slot[n], :], ACT.Copy).then_inc(whi, 1)

            def split(t, u, fill):
                act.wait_ge(m_in[u], fill * 32)
                act.wait_ge(mixed, at(t - 1, 1, 0))
                act.activation(m_hi[:], m_raw[:, u], ACT.Copy).then_inc(split_hi, 1)
                act.wait_ge(emb, at(t - 2, 1, 0))
                act.activation(e_hi[:, u], e_raw[:, u], ACT.Copy).then_inc(split_hi, 1)

            def step(t, u, fill=None):
                act.wait_ge(gated, at(t - 1, 1, 0))
                act.wait_ge(tlo, at(t - 1, 2, 1))
                act.wait_ge(st_x, (t + 1) * 16)
                for i in range(2):
                    act.wait_ge(turned, at(t, 2, i))
                    act.activation(x1_t[:, H[i]], ps_t[i][:, :], ACT.Copy).then_inc(tcopy, 1)
                    act.activation(t_hi[:, 4 * i:4 * i + 4, :], ps_t[i][:, :].rearrange("p (k t) -> p k t", t=P),
                                   ACT.Copy).then_inc(thi, 1)
                if fill is not None:
                    split(t + 2, u, fill)
                act.wait_ge(gated, at(t, 1, 0))
                act.wait_ge(st_y, (t + 1) * 16)
                for i in range(2):
                    act.activation(gate[:, H[i]], ps_g[i][:, :], ACT.Sigmoid).then_inc(sig, 1)

            for n in range(len(W)):
                weight(n)
                if n == 3:
                    split(0, 0, 1)
                if n == 13:
                    split(1, 1, 1)
            act.wait_ge(wlo_pool, len(W) // 2)
            act.wait_ge(wlo_dve, len(W) // 2)
            with act.Fori(0, 7) as it:
                step(2 * it, 0, it + 2)
                step(2 * it + 1, 1, it + 2)
            step(TT - 3, 0, TT // 2 + 1)
            step(TT - 2, 1)
            step(TT - 1, 0)

        @block.vector
        def _(dve):
            for s, n in ((resid, 2), (stat, 2), (aggr, 1), (eps, 1), (centred, 1), (shifted, 1), (tlo, 2), (prod, 2),
                         (summed, 1)):
                dve.sem_inc(s, 2 * n)

            def weight(n):
                hi, lo = W[n]
                dve.wait_ge(whi, n + 1)
                dve.tensor_tensor(lo, work[:, slot[n], :], f32(hi), ALU.subtract).then_inc(wlo_dve, 1)

            def statistics(t, u, fill):
                dve.wait_ge(mixed, at(t, 1, 0))
                dve.wait_ge(x_in[u], fill * 16)
                dve.wait_ge(summed, at(t - 2, 1, 0))
                for i in range(2):
                    dve.scalar_tensor_tensor(work[:, u, H[i]], x_raw[:, u, H[i]], ALPHA, ps_m[i][:, :], ALU.mult,
                                             ALU.add).then_inc(resid, 1)
                for i in range(2):
                    dve.wait_ge(resid, at(t, 2, i))
                    dve.bn_stats(stats[:, u, 6 * i:6 * i + 6], work[:, u, H[i]]).then_inc(stat, 1)
                dve.wait_ge(stat, at(t, 2, 1))
                take(dve, met)
                dve.bn_aggr(mv[:, u, :], stats[:, u, :]).then_inc(aggr, 1)
                dve.wait_ge(aggr, at(t, 1, 0))
                dve.tensor_scalar(var_eps[:, u:u + 1], mv[:, u, 1:2], LN_EPS, None, ALU.add).then_inc(eps, 1)

            def centre(t, u):
                dve.wait_ge(rs, at(t, 1, 0))
                dve.tensor_scalar(work[:, u, :], work[:, u, :], mv[:, u, 0:1], rstd[:, u:u + 1], ALU.subtract,
                                  ALU.mult).then_inc(centred, 1)

            def shift(t, u):
                dve.wait_ge(scaled, at(t, 1, 0))
                dve.tensor_tensor(work[:, u, :], work[:, u, :], ln_b[:, :], ALU.add).then_inc(shifted, 1)

            def lows(t):
                for i in range(2):
                    dve.wait_ge(thi, at(t, 2, i))
                    dve.wait_ge(gated, at(t - 1, 1, 0))
                    dve.tensor_tensor(t_lo[:, 4 * i:4 * i + 4, :], x1_t[:, H[i]].rearrange("p (k t) -> p k t", t=P),
                                      f32(t_hi[:, 4 * i:4 * i + 4, :]), ALU.subtract).then_inc(tlo, 1)

            def output(t, u):
                for i in range(2):
                    dve.wait_ge(sig, at(t, 2, i))
                    if i == 0:
                        dve.wait_ge(emb, at(t, 1, 0))
                    dve.tensor_tensor(gate[:, H[i]], gate[:, H[i]], ps_e[i][:, :], ALU.mult).then_inc(prod, 1)
                dve.wait_ge(prod, at(t, 2, 1))
                dve.scalar_tensor_tensor(gate, work[:, u, :], ALPHA, gate, ALU.mult, ALU.add).then_inc(summed, 1)

            def step(t, u, fill):
                statistics(t + 1, 1 - u, fill)
                lows(t)
                centre(t + 1, 1 - u)
                output(t, u)
                shift(t + 1, 1 - u)

            for n in range(1, len(W), 2):
                weight(n)
                if n == 13:
                    dve.wait_ge(wlo_pool, 5)
                    statistics(0, 0, 1)
            dve.wait_ge(const_in, 48)
            dve.wait_ge(wlo_pool, len(W) // 2)
            centre(0, 0)
            shift(0, 0)
            with dve.Fori(0, 8) as it:
                step(2 * it, 0, it + 1)
                step(2 * it + 1, 1, it + 2)
            lows(TT - 1)
            output(TT - 1, 0)

        @block.tensor
        def _(pe):
            for s, n in ((mixed, 1), (emb, 1), (turned, 2), (gated, 1)):
                pe.sem_inc(s, 2 * n)

            def mix(t, first=False):
                pe.wait_ge(split_lo, at(t, 2, 0))
                pe.wait_ge(resid, at(t - 1, 2, 1))
                for k in range(KD):
                    if first:
                        wait_piece(pe, k)
                    for i in range(2):
                        mm = product(pe, ps_m[i][:, :], (m_hi[:, k, :], m_lo[:, k, :]),
                                     (wo_hi[:, k, H[i]], wo_lo[:, k, H[i]]), k == 0, k == KD - 1)
                mm.then_inc(mixed, 1)

            def embed(t, u, first=False):
                if first:
                    wait_piece(pe, KD + 1)
                pe.wait_ge(split_lo, at(t, 2, 1))
                pe.wait_ge(prod, at(t - 1, 2, 1))
                for k in range(2):
                    for i in range(2):
                        mm = product(pe, ps_e[i][:, :], (e_hi[:, u, k, :], e_lo[:, u, k, :]),
                                     (we_hi[:, k, H[i]], we_lo[:, k, H[i]]), k == 0, k == 1)
                mm.then_inc(emb, 1)

            def turn(t, u):
                pe.wait_ge(shifted, at(t, 1, 0))
                for i in range(2):
                    pe.wait_ge(tlo, at(t - 1, 2, i))
                    for k in range(4):
                        mm = pe.transpose(ps_t[i][:, k * P:(k + 1) * P],
                                          work[:, u, (4 * i + k) * P:(4 * i + k + 1) * P], ident[:, :])
                    mm.then_inc(turned, 1)

            def gates(t, first=False):
                pe.wait_ge(sig, at(t - 1, 2, 1))
                for k in range(KD):
                    if first:
                        wait_piece(pe, KD + 2 + k)
                    if k % 4 == 0:
                        pe.wait_ge(tlo, at(t, 2, k // 4))
                    for i in range(2):
                        mm = product(pe, ps_g[i][:, :], (t_hi[:, k, :], t_lo[:, k, :]),
                                     (wg_hi[:, k, H[i]], wg_lo[:, k, H[i]]), k == 0, k == KD - 1)
                mm.then_inc(gated, 1)

            def step(t, u):
                mix(t + 1)
                turn(t, u)
                embed(t, u)
                gates(t)

            mix(0, True)
            mix(1)
            pe.wait_ge(const_in, 48)
            turn(0, 0)
            embed(0, 0, True)
            gates(0, True)
            with pe.Fori(0, 7) as it:
                step(2 * it + 1, 1)
                step(2 * it + 2, 0)
            step(TT - 2, 1)
            turn(TT - 1, 0)
            embed(TT - 1, 0)
            gates(TT - 1)


BLOCKS = (6, 6, 5)
FIRST = (0, 6, 12)
BW = BLOCKS[0] * P
CHW = BW // 2
PAIRS_F = FT // 2
UNITS_F = 3 * FT
RAWS = 3
XRAWS = 4
EVEN, DOWN, ODD = (0, 1), (2, 3), (4, 5)
LAST = PAIRS_F - 1


def phase_ffn(nc, g):
    assert sum(BLOCKS) == TT and UNITS_F % RAWS == 0
    with ExitStack() as ctx:
        ar = Arena(nc, ctx, "ff")
        sb, bank, sem = ar.sb, ar.bank, ar.sem
        w_raw = sb("w_raw", [P, RAWS, D])
        w_hi, w_lo = sb("w_hi", [P, 6, KD, P], F32R), sb("w_lo", [P, 6, KD, P], F32R)
        x_raw = sb("x_raw", [P, XRAWS, BW])
        x_hi, x_lo = sb("x_hi", [P, KD, BW], F32R), sb("x_lo", [P, KD, BW], F32R)
        h_hi, h_lo = sb("h_hi", [P, 4, BW], F32R), sb("h_lo", [P, 4, BW], F32R)
        y = sb("y", [P, BLOCKS[0], D])
        up = [sb("up_a", [P, 2 + BW]), sb("up_b", [P, 2 + BW])]
        cv = [sb("cv_a", [P, BW]), sb("cv_b", [P, BW])]
        h = sb("h", [P, 2, BW])
        carry = sb("carry", [P, 2, FT, 2])
        s_hist = sb("s_hist", [P, 2, FT, ROWS, 2])
        taps = sb("taps", [P, 2, FT, 4])
        ln_g, ln_b = sb("ln_g", [P, D]), sb("ln_b", [P, D])
        stats, mv = sb("stats", [P, BLOCKS[0], 12]), sb("mv", [P, BLOCKS[0], 2])
        var_eps, rstd, power = sb("var_eps", [P, BLOCKS[0]]), sb("rstd", [P, BLOCKS[0]]), sb("power", [P, 1])
        neg_mean, offset = sb("neg_mean", [P, BLOCKS[0]]), sb("offset", [P, BLOCKS[0]])
        ps_u = [bank(f"u{i}") for i in range(4)]
        ps_d = [bank(f"d{i}") for i in range(4)]

        const_in, ln_in, met = sem("const_in"), sem("ln_in"), sem("met")
        w_in = [sem(f"w_in{i}") for i in range(RAWS)]
        x_in = [sem(f"x_in{i}") for i in range(XRAWS)]
        y_in, st_y, st_c = sem("y_in"), sem("st_y"), sem("st_c")
        whi, wlo = sem("whi"), sem("wlo")
        xhi, xlo = sem("xhi"), sem("xlo")
        upped = sem("upped")
        past = sem("past")
        evac = sem("evac")
        carried = sem("carried")
        conv = sem("conv")
        silu, mul = sem("silu"), sem("mul")
        hhi, hlo = sem("hhi"), sem("hlo")
        down = sem("down")
        added = sem("added")
        stat, aggr, eps = sem("stat"), sem("aggr"), sem("eps")
        rs, offs = sem("rs"), sem("offs")
        centred, scaled, shifted = sem("centred"), sem("scaled"), sem("shifted")
        cleared, powered = sem("cleared"), sem("powered")
        H = (slice(0, 512), slice(512, 1024))

        def per_f(b, f, per, k):
            return (b * FT + f + 2) * per + k + 1

        def per_pair(b, p, per, k):
            return (FIRST[b] * PAIRS_F + BLOCKS[0] + p * BLOCKS[b]) * per + k + 1

        def unit(b, n):
            return b * UNITS_F + n + 1

        def chunks(b):
            w = BLOCKS[b] * P
            return (0, CHW), (CHW, w - CHW)

        def prompt_w(b):
            return BLOCKS[b] * P - (SAMPLE if b == 2 else 0)

        def sample_rows(buf):
            at0 = 2 + prompt_w(2)
            return buf[:, at0:at0 + ROWS * (NEW + 2)].rearrange("p (r t) -> p r t", t=NEW + 2)

        block = ctx.enter_context(nc.Block())

        @block.sync
        def _(sp):
            def load_w(b, n, register=None):
                i = n if register is None else n + 6 * register
                sp.wait_ge(wlo, b * UNITS_F + i + 1)
                sp.dma_start(w_raw[:, n % RAWS, :], g["w_ffn_p"][i] if register is None else
                             g["w_ffn_p"].rearrange("n p c -> p n c")[:, ds(i, 1), :]).then_inc(w_in[n % RAWS], 16)

            def load_x(b):
                w = BLOCKS[b] * P
                for k in range(KD):
                    sp.wait_ge(xlo, b * KD + k + 1)
                    sp.dma_start(x_raw[:, k % XRAWS, 0:w], g["x1_t"][k * P:(k + 1) * P, FIRST[b] * P:FIRST[b] * P + w])\
                      .then_inc(x_in[k % XRAWS], 16)

            def load_y(b):
                for t in range(BLOCKS[b]):
                    r = (FIRST[b] + t) * P
                    sp.dma_start(y[:, t, :], g["y0"][r:r + P, :]).then_inc(y_in, 16)

            def store_y(b):
                for t in range(BLOCKS[b]):
                    r = (FIRST[b] + t) * P
                    sp.wait_ge(shifted, FIRST[b] + t + 1)
                    sp.dma_start(g["y"][r:r + P, :], y[:, t, :]).then_inc(st_y, 16)

            sp.dma_start(taps[:, :, :, :], g["taps"]).then_inc(const_in, 16)
            sp.dma_start(s_hist[:, :, :, :, :], g["conv_hist"]).then_inc(const_in, 16)
            for b in range(3):
                for n in range(RAWS):
                    load_w(b, n)
                load_x(b)
                if b == 0:
                    sp.dma_start(ln_g[:, :], g["ln2_g"]).then_inc(ln_in, 16)
                    sp.dma_start(ln_b[:, :], g["ln2_b"]).then_inc(ln_in, 16)
                load_w(b, 3)
                if b > 0:
                    store_y(b - 1)
                    sp.wait_ge(st_y, 16 * FIRST[b])
                load_y(b)
                with sp.Fori(0, PAIRS_F - 1) as q:
                    for j in range(6):
                        load_w(b, 4 + j, register=q)
                for n in range(UNITS_F - 2, UNITS_F):
                    load_w(b, n)
            sp.wait_ge(carried, per_f(2, FT - 1, 2, 1) + 2 * FT)
            sp.dma_start(g["conv_p"].rearrange("p (s f) t -> p s f t", s=2), carry[:, :, :, :]).then_inc(st_c, 16)
            sp.dma_start(g["conv_s"].rearrange("p (s f) r t -> p s f r t", s=2), s_hist[:, :, :, :, :])\
              .then_inc(st_c, 16)
            store_y(2)
            sp.wait_ge(st_y, 16 * TT)
            sp.wait_ge(st_c, 32)

        def opening_units():
            return (0, ODD[0]), (1, ODD[1]), (2, DOWN[0]), (3, DOWN[1])

        def even_units(first, last):
            own = () if first else ((4, ODD[0]), (5, ODD[1]))
            a = 4 if first else 6
            return own, tuple((a + i, EVEN[i]) for i in range(2))

        def odd_units(first, last):
            a = 6 if first else 8
            return () if last else tuple((a + i, DOWN[i]) for i in range(2))

        @block.gpsimd
        def _(pool):
            pool.sem_inc(wlo, RAWS)
            pool.sem_inc(xlo, XRAWS)
            pool.sem_inc(hlo, 2)
            pool.memset(power[:, :], -0.5).then_inc(powered, 1)
            pool.wait_ge(powered, 1)

            def weight(b, n, base, slot):
                pool.wait_ge(whi, unit(b, base + n))
                pool.tensor_tensor(w_lo[:, slot], w_raw[:, n % RAWS, :].rearrange("p (k c) -> p k c", c=P),
                                   f32(w_hi[:, slot]), ALU.subtract).then_inc(wlo, 1)

            def product_lo(b, f, i, extra):
                w = BLOCKS[b] * P
                pool.wait_ge(hhi, per_f(b, f, 1, 0))
                pool.tensor_tensor(h_lo[:, i + extra, 0:w], h[:, i, 0:w], f32(h_hi[:, i + extra, 0:w]), ALU.subtract)\
                    .then_inc(hlo, 1)

            def opening(b, pieces, units):
                w = BLOCKS[b] * P
                for k in pieces:
                    pool.wait_ge(xhi, b * KD + k + 1)
                    pool.tensor_tensor(x_lo[:, k, 0:w], x_raw[:, k % XRAWS, 0:w], f32(x_hi[:, k, 0:w]), ALU.subtract)\
                        .then_inc(xlo, 1)
                    if k in units:
                        weight(b, k, 0, opening_units()[k][1])
                for n in units:
                    if n not in pieces:
                        weight(b, n, 0, opening_units()[n][1])

            def pair(b, p, n0, base, first=False, last=False):
                for part in even_units(first, last):
                    for n, slot in part:
                        weight(b, n0 + n, base, slot)
                product_lo(b, 2 * p, 0, 2 * last)
                for n, slot in odd_units(first, last):
                    weight(b, n0 + n, base, slot)
                if last and b < 2:
                    opening(b + 1, (0, 1), (0, 1))
                product_lo(b, 2 * p + 1, 1, 2 * last)

            def normalise(b):
                pool.wait_ge(ln_in, 32)
                for t in range(BLOCKS[b]):
                    n = FIRST[b] + t + 1
                    pool.wait_ge(eps, n)
                    pool.tensor_tensor(rstd[:, t:t + 1], var_eps[:, t:t + 1], power[:, :], ALU.pow).then_inc(rs, 1)
                    pool.wait_ge(rs, n)
                    pool.tensor_tensor(offset[:, t:t + 1], neg_mean[:, t:t + 1], rstd[:, t:t + 1], ALU.mult)\
                        .then_inc(offs, 1)
                    if t > 0:
                        scale(b, t - 1)
                scale(b, BLOCKS[b] - 1)

            def scale(b, t):
                pool.wait_ge(centred, FIRST[b] + t + 1)
                pool.tensor_tensor(y[:, t, :], y[:, t, :], ln_g[:, :], ALU.mult).then_inc(scaled, 1)

            opening(0, (0, 1), (0, 1))
            for b in range(3):
                opening(b, range(2, KD), ())
                opening(b, (), (2, 3))
                if b > 0:
                    normalise(b - 1)
                pair(b, 0, 0, 0, first=True)
                with pool.Fori(0, LAST - 1) as q:
                    pair(b, q + 1, 4, 6 * q)
                pair(b, LAST, 4, 6 * (LAST - 1), last=True)
            normalise(2)

        @block.scalar
        def _(act):
            for s, n in ((past, 2), (evac, 4), (carried, 2), (silu, 1), (hhi, 1)):
                act.sem_inc(s, 2 * n)
            act.sem_inc(carried, 2 * FT)

            def weight(b, n, base, slot, q2=0):
                act.wait_ge(w_in[n % RAWS], (b * (UNITS_F // RAWS) + n // RAWS + 1 + q2) * 16)
                act.activation(w_hi[:, slot], w_raw[:, n % RAWS, :].rearrange("p (k c) -> p k c", c=P), ACT.Copy)\
                   .then_inc(whi, 1)

            def opening(b, pieces, units):
                act.wait_ge(upped, per_f(b, -1, 4, 3))
                w = BLOCKS[b] * P
                for k in pieces:
                    act.wait_ge(x_in[k % XRAWS], (b * KD // XRAWS + k // XRAWS + 1) * 16)
                    act.activation(x_hi[:, k, 0:w], x_raw[:, k % XRAWS, 0:w], ACT.Copy).then_inc(xhi, 1)
                    if k in units:
                        weight(b, k, 0, opening_units()[k][1])
                if 2 in units:
                    act.wait_ge(down, per_pair(b - 1, LAST - 1, 1, BLOCKS[b - 1] - 1) if b else BLOCKS[0])
                for n in units:
                    if n not in pieces:
                        weight(b, n, 0, opening_units()[n][1])

            def centre(b):
                for t in range(BLOCKS[b]):
                    act.wait_ge(offs, FIRST[b] + t + 1)
                    act.activation(y[:, t, :], y[:, t, :], ACT.Identity, scale=rstd[:, t:t + 1],
                                   bias=offset[:, t:t + 1]).then_inc(centred, 1)

            def rows(b, f):
                pw = prompt_w(b)
                for s in range(2):
                    buf, fs = up[s], f if isinstance(f, int) else None
                    at_f = slice(f, f + 1) if fs is not None else ds(f, 1)
                    act.wait_ge(conv, per_f(b, f - 1, 4, 3))
                    act.wait_ge(carried, per_f(b, f - 1, 2, 1) + 2 * FT)
                    act.activation(buf[:, 0:2], carry[:, s, at_f, :], ACT.Copy)
                    if b == 2:
                        act.activation(sample_rows(buf)[:, :, 0:2], s_hist[:, s, at_f], ACT.Copy)
                    for c, (a, w) in enumerate(chunks(b)):
                        ps = ps_u[2 * s + c]
                        act.wait_ge(upped, per_f(b, f, 4, 2 * s + c))
                        if a + w <= pw:
                            act.activation(buf[:, 2 + a:2 + a + w], ps[:, 0:w], ACT.Copy)
                        else:
                            act.activation(buf[:, 2 + a:2 + pw], ps[:, 0:pw - a], ACT.Copy)
                            act.activation(sample_rows(buf)[:, :, 2:2 + NEW],
                                           ps[:, pw - a:w].rearrange("p (r t) -> p r t", t=NEW), ACT.Copy)
                        if s == 0:
                            act.wait_ge(mul, per_f(b, f - 1, 1, 0))
                            act.wait_ge(silu, per_f(b, f - 1, 1, 0))
                            take(act, met)
                        act.activation(cv[s][:, a:a + w], ps[:, 0:w], ACT.Identity, scale=taps[:, s, at_f, 2:3],
                                       bias=taps[:, s, at_f, 3:4]).then_inc(evac, 1)
                    act.wait_ge(evac, per_f(b, f, 4, 2 * s + 1))
                    take(act, met)
                    if b == 2:
                        act.activation(s_hist[:, s, at_f], sample_rows(buf)[:, :, NEW:NEW + 2], ACT.Copy)
                    act.activation(carry[:, s, at_f, :], buf[:, pw:pw + 2], ACT.Copy).then_inc(carried, 1)

            def product_hi(b, f, i, extra):
                w = BLOCKS[b] * P
                act.wait_ge(mul, per_f(b, f, 1, 0))
                act.activation(h_hi[:, i + extra, 0:w], h[:, i, 0:w], ACT.Copy).then_inc(hhi, 1)

            def pair(b, p, n0, q2, first=False, last=False):
                w = BLOCKS[b] * P
                for i in range(2):
                    f = 2 * p + i
                    rows(b, f)
                    act.wait_ge(conv, per_f(b, f, 4, 1))
                    act.activation(cv[0][:, 0:w], cv[0][:, 0:w], ACT.Silu).then_inc(silu, 1)
                    if i == 0:
                        own, following = even_units(first, last)
                        for n, slot in own:
                            weight(b, n0 + n, 0, slot, q2)
                        for n, slot in following:
                            weight(b, n0 + n, 0, slot, q2)
                        if not last:
                            act.wait_ge(down, per_pair(b, p - 1, 1, BLOCKS[b] - 1))
                    else:
                        for n, slot in odd_units(first, last):
                            weight(b, n0 + n, 0, slot, q2)
                    if last and i == 1 and b < 2:
                        opening(b + 1, (0, 1), (0, 1))
                    product_hi(b, f, i, 2 * last)

            act.wait_ge(const_in, 32)
            act.wait_ge(cleared, 1)
            opening(0, (0, 1), (0, 1))
            for b in range(3):
                opening(b, range(2, KD), ())
                opening(b, (), (2, 3))
                if b > 0:
                    centre(b - 1)
                pair(b, 0, 0, 0, first=True)
                with act.Fori(0, LAST - 1) as q:
                    pair(b, q + 1, 4, 2 * q)
                pair(b, LAST, 4, 2 * (LAST - 1), last=True)
            centre(2)

        @block.vector
        def _(dve):
            for s, n in ((conv, 4), (mul, 1)):
                dve.sem_inc(s, 2 * n)
            dve.sem_inc(added, 2 * BLOCKS[0])
            dve.memset(carry[:, :, :, :], 0.0).then_inc(cleared, 1)
            dve.wait_ge(const_in, 32)

            def convolve(b, f):
                pw = prompt_w(b)
                at_f = slice(f, f + 1) if isinstance(f, int) else ds(f, 1)
                for s in range(2):
                    dve.wait_ge(evac, per_f(b, f, 4, 2 * s + 1))
                    for k in (1, 0):
                        if k == 0:
                            dve.wait_ge(conv, per_f(b, f, 4, 2 * s))
                        tap = taps[:, s, at_f, k:k + 1]
                        op = dve.scalar_tensor_tensor(cv[s][:, 0:pw], up[s][:, k:k + pw], tap, cv[s][:, 0:pw],
                                                      ALU.mult, ALU.add)
                        if b == 2:
                            rows = cv[s][:, pw:pw + SAMPLE].rearrange("p (r t) -> p r t", t=NEW)
                            op = dve.scalar_tensor_tensor(rows, sample_rows(up[s])[:, :, k:k + NEW], tap, rows,
                                                          ALU.mult, ALU.add)
                        op.then_inc(conv, 1)

            def gate(b, f, i):
                w = BLOCKS[b] * P
                dve.wait_ge(silu, per_f(b, f, 1, 0))
                dve.wait_ge(conv, per_f(b, f, 4, 3))
                dve.wait_ge(hlo, per_f(b, f, 1, 0) - 2)
                dve.tensor_tensor(h[:, i, 0:w], cv[0][:, 0:w], cv[1][:, 0:w], ALU.mult).then_inc(mul, 1)

            def add(b, p, t):
                dve.wait_ge(down, per_pair(b, p, 1, t))
                if t == 0:
                    dve.wait_ge(added, per_pair(b, p - 1, 2, 2 * BLOCKS[b] - 1))
                for i in range(2):
                    dve.tensor_tensor(y[:, t, H[i]], y[:, t, H[i]], ps_d[2 * (t % 2) + i][:, :], ALU.add)\
                       .then_inc(added, 1)

            def adds(b, p, tiles):
                for t in tiles:
                    add(b, p, t)

            def pair(b, p, first=False):
                convolve(b, 2 * p)
                if not first:
                    adds(b, p - 1, (0,))
                gate(b, 2 * p, 0)
                if not first:
                    adds(b, p - 1, range(1, BLOCKS[b]))
                convolve(b, 2 * p + 1)
                gate(b, 2 * p + 1, 1)
                if first:
                    dve.wait_ge(y_in, 16 * (FIRST[b] + BLOCKS[b]))

            def last_pair(b, p):
                convolve(b, 2 * p)
                gate(b, 2 * p, 0)
                convolve(b, 2 * p + 1)
                adds(b, p - 1, (0,))
                gate(b, 2 * p + 1, 1)
                adds(b, p - 1, range(1, BLOCKS[b]))

            def statistics(b, t):
                n = FIRST[b] + t + 1
                dve.wait_ge(added, per_pair(b, LAST, 2, 2 * t + 1))
                for i in range(2):
                    dve.bn_stats(stats[:, t, 6 * i:6 * i + 6], y[:, t, H[i]]).then_inc(stat, 1)
                dve.wait_ge(stat, 2 * n)
                dve.bn_aggr(mv[:, t, :], stats[:, t, :]).then_inc(aggr, 1)
                dve.wait_ge(aggr, n)
                dve.tensor_scalar(neg_mean[:, t:t + 1], mv[:, t, 0:1], -1.0, None, ALU.mult)
                dve.tensor_scalar(var_eps[:, t:t + 1], mv[:, t, 1:2], LN_EPS, None, ALU.add).then_inc(eps, 1)

            def normalise(b):
                T = BLOCKS[b]
                dve.wait_ge(ln_in, 32)
                for t in range(T + 2):
                    if t < T:
                        add(b, LAST, t)
                        statistics(b, t)
                    if t >= 2:
                        dve.wait_ge(scaled, FIRST[b] + t - 1)
                        dve.tensor_tensor(y[:, t - 2, :], y[:, t - 2, :], ln_b[:, :], ALU.add).then_inc(shifted, 1)

            for b in range(3):
                pair(b, 0, first=True)
                with dve.Fori(0, LAST - 1) as q:
                    pair(b, q + 1)
                last_pair(b, LAST)
                normalise(b)

        @block.tensor
        def _(pe):
            pe.sem_inc(upped, 8)
            pe.sem_inc(down, BLOCKS[0])

            def rows(b, f, n, slots, opening=False):
                if opening:
                    pe.wait_ge(wlo, RAWS + unit(b, n + 1))
                    pe.wait_ge(evac, per_f(b, f - 1, 4, 3))
                for s in range(2) if not opening else ():
                    pe.wait_ge(wlo, RAWS + unit(b, n + s))
                    for c, (a, w) in enumerate(chunks(b)):
                        pe.wait_ge(evac, per_f(b, f - 1, 4, 2 * s + c))
                        for k in range(KD):
                            mm = part(b, s, c, a, w, k, slots)
                        mm.then_inc(upped, 1)
                for k in range(KD) if opening else ():
                    pe.wait_ge(xlo, XRAWS + b * KD + k + 1)
                    for s in range(2):
                        for c, (a, w) in enumerate(chunks(b)):
                            mm = part(b, s, c, a, w, k, slots)
                            if k == KD - 1:
                                mm.then_inc(upped, 1)

            def part(b, s, c, a, w, k, slots):
                return product(pe, ps_u[2 * s + c][:, 0:w], (w_hi[:, slots[s], k, :], w_lo[:, slots[s], k, :]),
                               (x_hi[:, k, a:a + w], x_lo[:, k, a:a + w]), k == 0, k == KD - 1)

            def downs(b, p, n, slots=DOWN, extra=0):
                pe.wait_ge(wlo, RAWS + unit(b, n + 1))
                pe.wait_ge(hlo, per_f(b, 2 * p + 1, 1, 0))
                for t in range(BLOCKS[b]):
                    if t < 2:
                        pe.wait_ge(added, per_pair(b, p - 1, 2, 2 * BLOCKS[b] - 1))
                    else:
                        pe.wait_ge(added, per_pair(b, p, 2, 2 * (t - 2) + 1))
                    for s in range(2):
                        for i in range(2):
                            wide = [x[:, slots[s], 4 * i:4 * i + 4, :].rearrange("p k c -> p (k c)") for x in (w_hi, w_lo)]
                            cols = slice(t * P, (t + 1) * P)
                            mm = product(pe, ps_d[2 * (t % 2) + i][:, :], (h_hi[:, s + extra, cols], h_lo[:, s + extra, cols]), wide,
                                         s == 0, s == 1)
                    mm.then_inc(down, 1)

            for b in range(3):
                rows(b, 0, 0, ODD, opening=True)
                rows(b, 1, 2, DOWN)
                with pe.Fori(0, LAST - 1) as q:
                    n = 6 * q + 4
                    rows(b, 2 * q + 2, n, EVEN)
                    downs(b, q, n + 2)
                    rows(b, 2 * q + 3, n + 4, ODD)
                n = 6 * (LAST - 1) + 4
                rows(b, 2 * LAST, n, EVEN)
                rows(b, 2 * LAST + 1, n + 4, ODD)
                downs(b, LAST - 1, n + 2)
                downs(b, LAST, UNITS_F - 2, EVEN, 2)


def kernel(**inputs):
    import numpy as np
    import concourse.bacc as bacc
    from concourse.bass_utils import run_bass_kernel_spmd

    a = {k: np.asarray(v) for k, v in inputs.items()}
    tile = lambda w, kt: w.reshape(kt, P, -1)
    w_in = a["w_in"][0]
    swap = np.r_[ROPE // 2:ROPE, 0:ROPE // 2]
    kr_cols = w_in[:, 2 * LORA:2 * LORA + ROPE]
    cols = {"q0": w_in[:, 0:128], "q1": w_in[:, 128:256], "c0": w_in[:, 256:384], "c1": w_in[:, 384:512],
            "kr": np.concatenate([kr_cols, kr_cols[:, swap]], 1)}
    for i in range(4):
        at = 2 * LORA + ROPE + i * P
        cols[f"u{i}"] = w_in[:, at:at + P]
    pieces = []
    for name in UNITS:
        t = tile(cols[name], KD).transpose(1, 0, 2)
        pieces += [t.reshape(P, CW)] if name == "kr" else [t[:, 0:4].reshape(P, CW), t[:, 4:8].reshape(P, CW)]
    pieces.append(a["w_pool"][0].transpose(1, 0, 2).reshape(P, CW))
    per_feature = lambda v: v.reshape(-1, P).T
    x_t = np.concatenate([a["x_prompt"][0].T, a["x_sample"].reshape(SAMPLE, D).T,
                          np.zeros((D, CW - SAMPLE), np.float32)], 1)
    inv = (1.0 / (np.float32(10000.0) ** (np.arange(0, ROPE, 2, dtype=np.float32) / ROPE))).astype(np.float32)
    pos = np.concatenate([np.arange(SEQ), np.tile(PAST + np.arange(NEW), ROWS),
                          np.zeros(CW - SAMPLE)]).astype(np.float32)
    ang = (pos[None, :] * inv[:, None]).astype(np.float32)
    cos, sin = np.cos(ang).astype(np.float32), np.sin(ang).astype(np.float32)
    trig_k = np.concatenate([cos, cos, -sin, sin], 0)
    inv_cnt = np.zeros((P, 2, 4, 16), np.float32)
    for i, w in enumerate(POOLS):
        inv_cnt[:, 0, i] = 1.0 / np.minimum(w, np.arange(16) + 1)
        inv_cnt[:, 1, i] = 1.0 / w
    w_q = tile(a["w_q_b"][0], 2).reshape(2, P, HEADS, NOPE + ROPE)
    w_q = np.concatenate([w_q, w_q[..., NOPE + swap]], 3).transpose(1, 2, 0, 3)
    w_kv = tile(a["w_kv_b"][0], 2).reshape(2, P, HEADS, NOPE + VD)
    w_k = w_kv[..., :NOPE].reshape(2, P, HEADS // 2, P).transpose(1, 2, 0, 3)
    w_v = w_kv[..., NOPE:].reshape(2, P, MLA).transpose(1, 0, 2)
    w_hd_p = np.concatenate([w.reshape(P, -1, CW).transpose(1, 0, 2) for w in (w_q, w_k, w_v)])
    w_up = tile(a["w_up"][0], KD).reshape(KD, P, 2, FT, P).transpose(2, 3, 1, 0, 4).reshape(2, FT, P, D)
    w_down = tile(a["w_down"][0], FT)
    order = [w_up[0, 0], w_up[1, 0], w_up[0, 1], w_up[1, 1]]
    for f in range(2, FT, 2):
        order += [w_up[0, f], w_up[1, f], w_down[f - 2], w_down[f - 1], w_up[0, f + 1], w_up[1, f + 1]]
    order += [w_down[FT - 2], w_down[FT - 1]]
    taps = np.concatenate([a["w_dw"][0], a["b_dw"]]).reshape(4, 2, FT, P).transpose(3, 1, 2, 0)
    ins = {
        "w_ffn_p": np.stack(order), "taps": taps,
        "conv_hist": a["state_ffn_conv"][0].reshape(ROWS, 2, 2, FT, P).transpose(4, 2, 3, 0, 1),
        "ln2_g": np.broadcast_to(a["ln2_g"][0], (P, D)), "ln2_b": np.broadcast_to(a["ln2_b"][0], (P, D)),
        "w_hd_p": w_hd_p,
        "ident": np.eye(P, dtype=np.float32),
        "x_t": x_t,
        "w_in_p": np.stack(pieces),
        "gains": np.concatenate([per_feature(a["g_kv"][0]), per_feature(a["g_q"][0]), per_feature(a["s_pool"][0])], 1),
        "inv_cnt": inv_cnt,
        "trig_k": trig_k,
        "w_mix_p": np.concatenate([tile(a["w_o"][0], KD), tile(a["w_pe"][0], 2), tile(a["w_pg"][0], KD)]),
        "x": np.concatenate([a["x_prompt"][0], a["x_sample"].reshape(SAMPLE, D)]),
        "pe_t": np.concatenate([a["p_prompt"][0, 0].T, a["p_sample"][0].reshape(SAMPLE, PLE).T], 1),
        "ln1_g": np.broadcast_to(a["ln1_g"][0], (P, D)), "ln1_b": np.broadcast_to(a["ln1_b"][0], (P, D)),
        "w_uk_p": w_kv[..., :NOPE].reshape(LORA, HEADS, NOPE).transpose(2, 1, 0),
        "w_uv_p": w_kv[..., NOPE:].transpose(1, 0, 2, 3),
        "ckv_t": a["cache_ckv"][0].reshape(ROWS, PAST, 2, P).transpose(0, 3, 2, 1),
        "ckv": a["cache_ckv"][0].reshape(ROWS, PAST // P, P, LORA).transpose(0, 2, 1, 3),
        "krope_t": a["cache_krope"][0].transpose(0, 2, 1),
        "pool_hist": a["state_pool"][0].reshape(ROWS, HIST, 4, P).transpose(3, 2, 0, 1),
    }
    ins = {k: np.ascontiguousarray(v) for k, v in ins.items()}
    outs = {"c_t": (LORA, TOK), "kr_t": (ROPE, TOK), "pool_p": (P, 4, HIST), "pool_s": (P, 4, ROWS, HIST),
            "y": (TOK, D), "conv_p": (P, 2 * FT, 2), "conv_s": (P, 2 * FT, ROWS, 2)}
    nc = bacc.Bacc("TRN2", target_bir_lowering=False, num_devices=1)
    g = {k: nc.dram_tensor(f"in_{k}", v.shape, F32, kind="ExternalInput").ap() for k, v in ins.items()}
    g |= {k: nc.dram_tensor(f"out_{k}", s, F32, kind="ExternalOutput").ap() for k, s in outs.items()}
    scratch = {"qn_t": (LORA, TOK), "mix_t": (D, TOK), "q_t": (HEADS * 96, TOK), "k_t": (HEADS * NOPE, SEQ),
               "v": (SEQ, MLA), "x1_t": (D, TOK), "y0": (TOK, D)}
    g |= {k: nc.dram_tensor(f"scratch_{k}", s, F32, kind="Internal").ap() for k, s in scratch.items()}
    build(nc, g)
    r = run_bass_kernel_spmd(nc, [{f"in_{k}": v for k, v in ins.items()}], core_ids=[0]).results[0]
    o = {k: r[f"out_{k}"] for k in outs}
    return finish(o)


def build(nc, g):
    for phase in (phase_project, phase_heads, phase_attend, phase_sample, phase_mix, phase_ffn):
        with nc.cleanup_on_exit():
            phase(nc, g)


def finish(o):
    ckv, kr = o["c_t"].T, o["kr_t"].T
    return (o["y"][:SEQ].reshape(1, SEQ, D), o["y"][SEQ:].reshape(ROWS, NEW, D),
            ckv[:SEQ].reshape(1, 1, SEQ, LORA), kr[:SEQ].reshape(1, 1, SEQ, ROPE),
            o["pool_p"].transpose(2, 1, 0).reshape(1, 1, HIST, MLA),
            o["conv_p"].transpose(2, 1, 0).reshape(1, 1, 2, 2 * FF),
            ckv[SEQ:].reshape(1, ROWS, NEW, LORA), kr[SEQ:].reshape(1, ROWS, NEW, ROPE),
            o["pool_s"].transpose(2, 3, 1, 0).reshape(1, ROWS, HIST, MLA),
            o["conv_s"].transpose(2, 3, 1, 0).reshape(1, ROWS, 2, 2 * FF))
```
